# Optimizing a Trainium2 kernel written in Bass

```python
import math
import jax
import jax.numpy as jnp
from jax import lax
import numpy as np

D_MODEL = 1024
BATCH = 1
SEQ = 1024
DEPTH = 1

D_SSM = 512
SSM_GROUP = 16
N_SSM_GROUPS = D_SSM // SSM_GROUP
SSM_STATE = 64
D_ATTN = D_MODEL - D_SSM
HEAD_DIM = 64
N_Q_HEADS = D_ATTN // HEAD_DIM
N_KV_HEADS = 2
Q_PER_KV = N_Q_HEADS // N_KV_HEADS
KV_DIM = N_KV_HEADS * HEAD_DIM
D_IN = D_SSM + D_ATTN + 2 * KV_DIM
WINDOW = 128
BLOCK = 128
N_BUCKETS = 32
MAX_DISTANCE = 128
D_FF = 2816
CONV_WIDTH = 3
N_MOD = 6
EPS = 1e-6
NEG_INF = -1e30


def _rms(x, w):
    xf = x.astype(jnp.float32)
    y = xf * lax.rsqrt(jnp.mean(xf * xf, axis=-1, keepdims=True) + EPS)
    return (y * w.astype(jnp.float32)).astype(x.dtype)

def _t5_bucket(n):
    n = np.maximum(n, 0)
    max_exact = N_BUCKETS // 2
    log_part = np.log(np.maximum(n, 1) / max_exact) / math.log(MAX_DISTANCE / max_exact)
    large = max_exact + (log_part * (N_BUCKETS - max_exact)).astype(np.int32)
    large = np.minimum(large, N_BUCKETS - 1)
    return np.where(n < max_exact, n, large).astype(np.int32)

def _s5(u, lam_re, lam_im, log_dt, b_re, b_im, c_re, c_im, d_skip, w_glu, b_glu):
    bsz, seq = u.shape[0], u.shape[1]
    f32 = jnp.float32
    ug = u.astype(f32).reshape(bsz, seq, N_SSM_GROUPS, SSM_GROUP)
    lr = jnp.minimum(lam_re.astype(f32), -1e-4)
    li = lam_im.astype(f32)
    dt = jnp.exp(log_dt.astype(f32))[:, None]
    mag = jnp.exp(dt * lr)
    a_re = mag * jnp.cos(dt * li)
    a_im = mag * jnp.sin(dt * li)
    den = lr * lr + li * li
    f_re = ((a_re - 1.0) * lr + a_im * li) / den
    f_im = (a_im * lr - (a_re - 1.0) * li) / den
    br = b_re.astype(f32)
    bi = b_im.astype(f32)
    bb_re = f_re[..., None] * br - f_im[..., None] * bi
    bb_im = f_re[..., None] * bi + f_im[..., None] * br
    bu_re = jnp.einsum("blgh,gph->blgp", ug, bb_re)
    bu_im = jnp.einsum("blgh,gph->blgp", ug, bb_im)
    shape_a = (1, seq, N_SSM_GROUPS, SSM_STATE)
    a_re_t = jnp.broadcast_to(a_re, shape_a)
    a_im_t = jnp.broadcast_to(a_im, shape_a)

    def combine(e1, e2):
        a1r, a1i, b1r, b1i = e1
        a2r, a2i, b2r, b2i = e2
        return (a2r * a1r - a2i * a1i,
                a2r * a1i + a2i * a1r,
                a2r * b1r - a2i * b1i + b2r,
                a2r * b1i + a2i * b1r + b2i)

    _, _, s_re, s_im = lax.associative_scan(combine, (a_re_t, a_im_t, bu_re, bu_im), axis=1)
    y = (jnp.einsum("blgp,ghp->blgh", s_re, c_re.astype(f32))
         - jnp.einsum("blgp,ghp->blgh", s_im, c_im.astype(f32))
         + d_skip.astype(f32).reshape(N_SSM_GROUPS, SSM_GROUP) * ug)
    z = jax.nn.gelu(y.reshape(bsz, seq, D_SSM))
    out = z * jax.nn.sigmoid(z @ w_glu.astype(f32) + b_glu.astype(f32))
    return out.astype(u.dtype)

def _swa_sink(q, k, v, rel_bias, sinks):
    bsz, seq = q.shape[0], q.shape[1]
    nb = seq // BLOCK
    f32 = jnp.float32
    qb = q.astype(f32).reshape(bsz, nb, BLOCK, N_KV_HEADS, Q_PER_KV, HEAD_DIM)
    pad = ((0, 0), (BLOCK, 0), (0, 0), (0, 0))
    kb = jnp.pad(k.astype(f32), pad).reshape(bsz, nb + 1, BLOCK, N_KV_HEADS, HEAD_DIM)
    vb = jnp.pad(v.astype(f32), pad).reshape(bsz, nb + 1, BLOCK, N_KV_HEADS, HEAD_DIM)
    k_band = jnp.concatenate([kb[:, :-1], kb[:, 1:]], axis=2)
    v_band = jnp.concatenate([vb[:, :-1], vb[:, 1:]], axis=2)
    logits = jnp.einsum("bnqhgd,bnkhd->bnhgqk", qb, k_band) * (HEAD_DIM ** -0.5)
    q_off = np.arange(BLOCK)[:, None] + BLOCK
    k_off = np.arange(2 * BLOCK)[None, :]
    dist = q_off - k_off
    bias = jnp.take(rel_bias.astype(f32), _t5_bucket(dist), axis=0)
    bias = bias.transpose(2, 0, 1).reshape(N_KV_HEADS, Q_PER_KV, BLOCK, 2 * BLOCK)
    key_pos = np.arange(nb)[:, None, None] * BLOCK + k_off[None] - BLOCK
    mask = (dist[None] >= 0) & (dist[None] < WINDOW) & (key_pos >= 0)
    logits = jnp.where(mask[None, :, None, None], logits + bias, NEG_INF)
    sink = sinks.astype(f32).reshape(N_KV_HEADS, Q_PER_KV)[None, None, :, :, None, None]
    m = jnp.maximum(jnp.max(logits, axis=-1, keepdims=True), sink)
    p = jnp.exp(logits - m)
    probs = p / (jnp.sum(p, axis=-1, keepdims=True) + jnp.exp(sink - m))
    out = jnp.einsum("bnhgqk,bnkhd->bnqhgd", probs, v_band)
    return out.reshape(bsz, seq, D_ATTN).astype(q.dtype)

def _conv_ffn(h, w_up, conv_w, conv_b, w_down):
    up = h @ w_up
    rhs = conv_w.reshape(CONV_WIDTH, 1, 2 * D_FF).astype(up.dtype)
    up = lax.conv_general_dilated(up, rhs, window_strides=(1,),
                                  padding=[(CONV_WIDTH - 1, 0)],
                                  dimension_numbers=("NWC", "WIO", "NWC"),
                                  feature_group_count=2 * D_FF) + conv_b
    val, gate = jnp.split(up, 2, axis=-1)
    return (jax.nn.silu(gate) * val) @ w_down

def first_inputs(seed: int = 0) -> dict:
    key = jax.random.key(seed)
    ks = jax.random.split(key, 28)
    f32 = jnp.float32

    def nrm(k, shape, scale):
        return jax.random.normal(k, shape, f32) * scale

    def gain(k, shape):
        return 1.0 + 0.05 * jax.random.normal(k, shape, f32)

    G, P, H = N_SSM_GROUPS, SSM_STATE, SSM_GROUP
    lam_im0 = math.pi * jnp.arange(P, dtype=f32)
    return {
        "x": nrm(ks[0], (BATCH, SEQ, D_MODEL), 1.0),
        "c": nrm(ks[1], (BATCH, D_MODEL), 1.0),
        "w_mod": nrm(ks[2], (DEPTH, D_MODEL, N_MOD * D_MODEL), 0.5 * D_MODEL ** -0.5),
        "b_mod": nrm(ks[3], (DEPTH, N_MOD * D_MODEL), 0.02),
        "norm1_w": gain(ks[4], (DEPTH, D_MODEL)),
        "w_in": nrm(ks[5], (DEPTH, D_MODEL, D_IN), D_MODEL ** -0.5),
        "lam_re": -0.5 * jnp.exp(0.1 * jax.random.normal(ks[6], (DEPTH, G, P), f32)),
        "lam_im": lam_im0 + 0.05 * jax.random.normal(ks[7], (DEPTH, G, P), f32),
        "log_dt": jax.random.uniform(ks[8], (DEPTH, G), f32, math.log(1e-3), math.log(1e-1)),
        "ssm_b_re": nrm(ks[9], (DEPTH, G, P, H), (2 * H) ** -0.5),
        "ssm_b_im": nrm(ks[10], (DEPTH, G, P, H), (2 * H) ** -0.5),
        "ssm_c_re": nrm(ks[11], (DEPTH, G, H, P), (2 * P) ** -0.5),
        "ssm_c_im": nrm(ks[12], (DEPTH, G, H, P), (2 * P) ** -0.5),
        "ssm_d": nrm(ks[13], (DEPTH, D_SSM), 1.0),
        "w_glu": nrm(ks[14], (DEPTH, D_SSM, D_SSM), D_SSM ** -0.5),
        "b_glu": nrm(ks[15], (DEPTH, D_SSM), 0.02),
        "q_norm_w": gain(ks[16], (DEPTH, HEAD_DIM)),
        "k_norm_w": gain(ks[17], (DEPTH, HEAD_DIM)),
        "rel_bias": nrm(ks[18], (N_BUCKETS, N_Q_HEADS), 0.5),
        "sinks": nrm(ks[19], (DEPTH, N_Q_HEADS), 0.5),
        "out_norm_ssm": gain(ks[20], (DEPTH, D_SSM)),
        "out_norm_attn": gain(ks[21], (DEPTH, D_ATTN)),
        "w_out": nrm(ks[22], (DEPTH, D_MODEL, D_MODEL), D_MODEL ** -0.5),
        "norm2_w": gain(ks[23], (DEPTH, D_MODEL)),
        "w_up": nrm(ks[24], (DEPTH, D_MODEL, 2 * D_FF), D_MODEL ** -0.5),
        "conv_w": nrm(ks[25], (DEPTH, CONV_WIDTH, 2 * D_FF), CONV_WIDTH ** -0.5),
        "conv_b": nrm(ks[26], (DEPTH, 2 * D_FF), 0.02),
        "w_down": nrm(ks[27], (DEPTH, D_FF, D_MODEL), D_FF ** -0.5),
    }

def first_block(x, c, w_mod, b_mod, norm1_w, w_in, lam_re, lam_im, log_dt,
              ssm_b_re, ssm_b_im, ssm_c_re, ssm_c_im, ssm_d, w_glu, b_glu,
              q_norm_w, k_norm_w, rel_bias, sinks, out_norm_ssm, out_norm_attn,
              w_out, norm2_w, w_up, conv_w, conv_b, w_down):
    bsz, seq = x.shape[0], x.shape[1]
    c_act = jax.nn.silu(c)
    for l in range(DEPTH):
        mod = (c_act @ w_mod[l] + b_mod[l])[:, None, :]
        sh1, sc1, g1, sh2, sc2, g2 = jnp.split(mod, N_MOD, axis=-1)

        h = _rms(x, norm1_w[l]) * (1 + sc1) + sh1
        proj = h @ w_in[l]
        u, q, k, v = jnp.split(proj, [D_SSM, D_SSM + D_ATTN, D_SSM + D_ATTN + KV_DIM], axis=-1)
        y_ssm = _s5(u, lam_re[l], lam_im[l], log_dt[l], ssm_b_re[l], ssm_b_im[l],
                    ssm_c_re[l], ssm_c_im[l], ssm_d[l], w_glu[l], b_glu[l])
        q = _rms(q.reshape(bsz, seq, N_Q_HEADS, HEAD_DIM), q_norm_w[l])
        k = _rms(k.reshape(bsz, seq, N_KV_HEADS, HEAD_DIM), k_norm_w[l])
        v = v.reshape(bsz, seq, N_KV_HEADS, HEAD_DIM)
        y_attn = _swa_sink(q, k, v, rel_bias, sinks[l])
        mixed = jnp.concatenate([_rms(y_ssm, out_norm_ssm[l]),
                                 _rms(y_attn, out_norm_attn[l])], axis=-1)
        x = x + g1 * (mixed @ w_out[l])

        h2 = _rms(x, norm2_w[l]) * (1 + sc2) + sh2
        x = x + g2 * _conv_ffn(h2, w_up[l], conv_w[l], conv_b[l], w_down[l])
    return x


GRID_W = 64
CTX_LEN = 256
HG_DK = 128
HG_WIDTH = D_MODEL // 2
HG_HEADS = HG_WIDTH // HG_DK
HG_CHUNK = 64
SC_WIDTH = D_MODEL // 4
SC_TAPS = 3
SG_WIDTH = D_MODEL // 4
SG_HEADS = 4
SG_HEAD_DIM = SG_WIDTH // SG_HEADS
SG_CHUNK = 128
MIX_WIDTH = HG_WIDTH + SC_WIDTH + SG_WIDTH
HG_STATE_COLS = 3 * HG_WIDTH
IN_COLS = 5 * HG_WIDTH + 3 * SC_WIDTH + 2 * SG_WIDTH
ALPHA = (2 * DEPTH) ** 0.25
BETA = (8 * DEPTH) ** -0.25
TINY = 1e-30

O_Q = 3 * HG_WIDTH
O_G = 4 * HG_WIDTH
O_SC = 5 * HG_WIDTH
O_SG = O_SC + 3 * SC_WIDTH


F32 = jnp.float32

def layer_norm(x, g=None, b=None):
    xf = x.astype(F32)
    xc = xf - jnp.mean(xf, axis=-1, keepdims=True)
    y = xc * lax.rsqrt(jnp.mean(xc * xc, axis=-1, keepdims=True) + EPS)
    if g is not None:
        y = y * g.astype(F32) + b.astype(F32)
    return y.astype(x.dtype)

def modulate(x, shift, scale):
    return layer_norm(x) * (1.0 + scale) + shift

def hg_lower_bounds(lb_logits):
    p = jax.nn.softmax(lb_logits.astype(F32), axis=0)
    return jnp.cumsum(p, axis=0) - p[:1]

def hg_forget(z, lb):
    z = z.astype(F32)
    k = (1.0 - lb) * jax.nn.sigmoid(-z)
    logf = jnp.log(jnp.maximum(lb + (1.0 - lb) * jax.nn.sigmoid(z), TINY))
    return k, logf

def split_heads(a):
    return a.reshape(a.shape[0], a.shape[1], HG_HEADS, HG_DK)

def flip(a):
    return a[:, ::-1]

def hg_state_inputs(p_state, lb_f, lb_b):
    i, z_f, z_b = jnp.split(p_state.astype(F32), 3, axis=-1)
    k_f, lf_f = hg_forget(z_f, lb_f)
    k_b, lf_b = hg_forget(z_b, lb_b)
    return (split_heads(i), split_heads(k_f), split_heads(k_b), split_heads(lf_f), split_heads(lf_b))

def gla_chunk_scan(q, k, v, logf, s0):
    bsz, t, h, dk = q.shape
    dv = v.shape[-1]
    n = t // HG_CHUNK

    def to_chunks(a):
        return a.astype(F32).reshape(bsz, n, HG_CHUNK, h, a.shape[-1]).transpose(1, 0, 3, 2, 4)

    causal = jnp.tril(jnp.ones((HG_CHUNK, HG_CHUNK), bool))[:, :, None]

    def step(s, inp):
        qc, kc, vc, gc = inp
        b = jnp.cumsum(gc, axis=2)
        inter = jnp.einsum('bhtk,bhkv->bhtv', qc * jnp.exp(b), s)
        diff = b[:, :, :, None, :] - b[:, :, None, :, :]
        decay = jnp.where(causal, jnp.exp(jnp.minimum(diff, 0.0)), 0.0)
        scores = jnp.einsum('bhtk,bhtsk,bhsk->bhts', qc, decay, kc)
        intra = jnp.einsum('bhts,bhsv->bhtv', scores, vc)
        b_last = b[:, :, -1:, :]
        s_new = jnp.exp(b_last[:, :, 0, :, None]) * s + jnp.einsum('bhsk,bhsv->bhkv', kc * jnp.exp(jnp.minimum(b_last - b, 0.0)), vc)
        return s_new, inter + intra

    _, o = lax.scan(step, s0.astype(F32), (to_chunks(q), to_chunks(k), to_chunks(v), to_chunks(logf)))
    return o.transpose(1, 0, 3, 2, 4).reshape(bsz, t, h, dv)

def gla_final_state(k, v, logf):
    suffix = jnp.minimum(lax.cumsum(logf, axis=1, reverse=True) - logf, 0.0)
    return jnp.einsum('bthk,bthv->bhkv', k * jnp.exp(suffix), v)

def hgrn2_bidir(q, v, k_f, k_b, lf_f, lf_b, s0_f, s0_b):
    o_f = gla_chunk_scan(q, k_f, v, lf_f, s0_f)
    o_b = flip(gla_chunk_scan(flip(q), flip(k_b), flip(v), flip(lf_b), s0_b))
    return o_f + o_b

def conv1d_centred(x, w):
    xp = jnp.pad(x, ((0, 0), (1, 1), (0, 0)))
    return xp[:, :-2] * w[0] + xp[:, 1:-1] * w[1] + xp[:, 2:] * w[2]

def chunk_spatial_gate(u, v, ln_g, ln_b, w_s, b_s):
    bsz, t, _ = v.shape
    n = t // SG_CHUNK
    vh = layer_norm(v.reshape(bsz, t, SG_HEADS, SG_HEAD_DIM),
                    ln_g.reshape(SG_HEADS, SG_HEAD_DIM), ln_b.reshape(SG_HEADS, SG_HEAD_DIM))
    vh = vh.reshape(bsz, n, SG_CHUNK, SG_HEADS, SG_HEAD_DIM)
    mixed = jnp.einsum('gts,bnsgc->bntgc', w_s, vh) + b_s.T[:, :, None]
    return u * mixed.reshape(bsz, t, SG_WIDTH)

def token_mixers(p, hg_in, s0_f, s0_b, hg_norm_g, sc_w, sg_ln_g, sg_ln_b, sg_w, sg_b):
    v, k_f, k_b, lf_f, lf_b = hg_in
    q = jax.nn.silu(split_heads(p[..., O_Q:O_G].astype(F32))) * HG_DK ** -0.5
    o = hgrn2_bidir(q, v, k_f, k_b, lf_f, lf_b, s0_f, s0_b)
    o = o * lax.rsqrt(jnp.mean(o * o, axis=-1, keepdims=True) + EPS) * hg_norm_g.astype(F32)
    hg = (o.reshape(o.shape[0], o.shape[1], HG_WIDTH) * jax.nn.silu(p[..., O_G:O_SC].astype(F32))).astype(p.dtype)
    gate_b, gate_c, h_sc = jnp.split(p[..., O_SC:O_SG], 3, axis=-1)
    sc = gate_b * conv1d_centred(gate_c * h_sc, sc_w)
    u, v_sg = jnp.split(p[..., O_SG:], 2, axis=-1)
    sg = chunk_spatial_gate(u, v_sg, sg_ln_g, sg_ln_b, sg_w, sg_b)
    return jnp.concatenate([hg, sc, sg], axis=-1)

def dwconv3x3(img, w):
    rows, cols = img.shape[1], img.shape[2]
    pad = jnp.pad(img, ((0, 0), (1, 1), (1, 1), (0, 0)))
    out = pad[:, 0:rows, 0:cols] * w[0, 0]
    for di in range(3):
        for dj in range(3):
            if di or dj:
                out = out + pad[:, di:di + rows, dj:dj + cols] * w[di, dj]
    return out

def conv_ffn(h, w_up, conv_w, conv_b, w_down, grid_rows):
    a, g = jnp.split(h @ w_up, 2, axis=-1)
    bsz, t, f = a.shape
    a = dwconv3x3(a.reshape(bsz, grid_rows, t // grid_rows, f), conv_w).reshape(bsz, t, f) + conv_b
    return (jax.nn.gelu(a, approximate=False) * g) @ w_down

def _normal(k, shape, scale):
    return jax.random.normal(k, shape, F32) * scale

def second_inputs(seed: int = 0) -> dict:
    key = jax.random.key(seed)
    ks = jax.random.split(key, 23)
    return {
        'x': _normal(ks[0], (BATCH, SEQ, D_MODEL), 1.0),
        'c': _normal(ks[1], (BATCH, D_MODEL), 1.0),
        'ctx': _normal(ks[2], (BATCH, CTX_LEN, D_MODEL), 1.0),
        'c_ctx': _normal(ks[3], (D_MODEL,), 1.0),
        'ada_w': _normal(ks[4], (DEPTH, D_MODEL, N_MOD * D_MODEL), 0.5 * D_MODEL ** -0.5),
        'ada_b': _normal(ks[5], (DEPTH, N_MOD * D_MODEL), 0.02),
        'w_in': _normal(ks[6], (DEPTH, D_MODEL, IN_COLS), D_MODEL ** -0.5),
        'hg_lb': _normal(ks[7], (DEPTH, 2, HG_WIDTH), 1.0),
        'hg_norm_g': 1.0 + _normal(ks[8], (DEPTH, HG_DK), 0.02),
        'sc_conv_w': _normal(ks[9], (DEPTH, SC_TAPS, SC_WIDTH), SC_TAPS ** -0.5),
        'sg_ln_g': 1.0 + _normal(ks[10], (DEPTH, SG_WIDTH), 0.02),
        'sg_ln_b': _normal(ks[11], (DEPTH, SG_WIDTH), 0.02),
        'sg_w': _normal(ks[12], (DEPTH, SG_HEADS, SG_CHUNK, SG_CHUNK), 0.5 * SG_CHUNK ** -0.5),
        'sg_b': 1.0 + _normal(ks[13], (DEPTH, SG_HEADS, SG_CHUNK), 0.02),
        'w_out': _normal(ks[14], (DEPTH, MIX_WIDTH, D_MODEL), BETA * MIX_WIDTH ** -0.5),
        'ln1_g': 1.0 + _normal(ks[15], (DEPTH, D_MODEL), 0.02),
        'ln1_b': _normal(ks[16], (DEPTH, D_MODEL), 0.02),
        'ffn_up': _normal(ks[17], (DEPTH, D_MODEL, 2 * D_FF), D_MODEL ** -0.5),
        'ffn_conv_w': _normal(ks[18], (DEPTH, 3, 3, D_FF), 1.0 / 3.0),
        'ffn_conv_b': _normal(ks[19], (DEPTH, D_FF), 0.02),
        'ffn_down': _normal(ks[20], (DEPTH, D_FF, D_MODEL), BETA * D_FF ** -0.5),
        'ln2_g': 1.0 + _normal(ks[21], (DEPTH, D_MODEL), 0.02),
        'ln2_b': _normal(ks[22], (DEPTH, D_MODEL), 0.02),
    }

def second_block(x, c, ctx, c_ctx, ada_w, ada_b, w_in, hg_lb, hg_norm_g, sc_conv_w, sg_ln_g, sg_ln_b,
              sg_w, sg_b, w_out, ln1_g, ln1_b, ffn_up, ffn_conv_w, ffn_conv_b, ffn_down, ln2_g, ln2_b):
    rows = x.shape[1] // GRID_W
    lower = hg_lower_bounds(hg_lb)
    silu_c = jax.nn.silu(c)
    silu_cc = jax.nn.silu(c_ctx)
    for l in range(DEPTH):
        last = l == DEPTH - 1
        mx = jnp.split((silu_c @ ada_w[l] + ada_b[l])[:, None, :], N_MOD, axis=-1)
        mc = jnp.split(silu_cc @ ada_w[l] + ada_b[l], N_MOD, axis=-1)
        lb_f, lb_b = lower[l, 0], lower[l, 1]
        px = modulate(x, mx[0], mx[1]) @ w_in[l]
        w_in_ctx = w_in[l][:, :HG_STATE_COLS] if last else w_in[l]
        pc = modulate(ctx, mc[0], mc[1]) @ w_in_ctx
        hg_x = hg_state_inputs(px[..., :HG_STATE_COLS], lb_f, lb_b)
        hg_c = hg_state_inputs(pc[..., :HG_STATE_COLS], lb_f, lb_b)
        v_c, kf_c, kb_c, lff_c, lfb_c = hg_c
        s_f = gla_final_state(kf_c, v_c, lff_c)
        s_b = gla_final_state(flip(kb_c), flip(v_c), flip(lfb_c))
        mix_args = (hg_norm_g[l], sc_conv_w[l], sg_ln_g[l], sg_ln_b[l], sg_w[l], sg_b[l])
        mix_x = token_mixers(px, hg_x, s_f, s_b, *mix_args)
        x_new = layer_norm(ALPHA * x + mx[2] * (mix_x @ w_out[l]), ln1_g[l], ln1_b[l])
        ffn_x = conv_ffn(modulate(x_new, mx[3], mx[4]), ffn_up[l], ffn_conv_w[l], ffn_conv_b[l], ffn_down[l], rows)
        x_new = layer_norm(ALPHA * x_new + mx[5] * ffn_x, ln2_g[l], ln2_b[l])
        if not last:
            zero = jnp.zeros_like(s_f)
            mix_c = token_mixers(pc, hg_c, zero, zero, *mix_args)
            ctx = layer_norm(ALPHA * ctx + mc[2] * (mix_c @ w_out[l]), ln1_g[l], ln1_b[l])
            ffn_c = conv_ffn(modulate(ctx, mc[3], mc[4]), ffn_up[l], ffn_conv_w[l], ffn_conv_b[l], ffn_down[l], 1)
            ctx = layer_norm(ALPHA * ctx + mc[5] * ffn_c, ln2_g[l], ln2_b[l])
        x = x_new
    return x


_first_inputs = second_inputs


def second_inputs(seed=0):
    import zlib

    import numpy as np

    out = dict(_first_inputs(seed))
    spreads = {}
    factors = {'ctx': 8.0,
     'c_ctx': 8.0,
     'ada_b': 3.909,
     'hg_norm_g': 8.0,
     'sg_ln_g': 8.0,
     'sg_ln_b': 8.0,
     'sg_b': 8.0,
     'ln1_g': 2.847,
     'ln1_b': 2.846,
     'ffn_conv_b': 8.0,
     'ln2_g': 2.741,
     'ln2_b': 2.828}
    for name, (base, spread) in spreads.items():
        noise = np.random.default_rng([zlib.crc32(name.encode()), seed]).standard_normal(out[name].shape)
        drawn = base * np.exp(spread * noise) if base else spread * noise
        out[name] = jnp.asarray(drawn.astype(out[name].dtype))
    for name, factor in factors.items():
        out[name] = (out[name] * factor).astype(out[name].dtype)
    return out


_narrow_inputs = second_inputs


def second_inputs(seed=0):

    out = dict(_narrow_inputs(seed))
    wider = {'ctx': 6.99,
     'c_ctx': 3.7,
     'hg_norm_g': 7.25,
     'sg_ln_g': 12.0,
     'sg_ln_b': 12.0,
     'sg_b': 6.68,
     'ln1_g': 3.23,
     'ln1_b': 3.22,
     'ffn_conv_b': 9.6,
     'ln2_g': 3.07,
     'ln2_b': 3.08}
    for name, times in wider.items():
        mean = out[name].mean()
        out[name] = (mean + times * (out[name] - mean)).astype(out[name].dtype)
    return out


def setup_inputs(seed=0):
    out = dict(first_inputs(seed))
    for name, value in second_inputs(seed + 1).items():
        if name != "x":
            out[name + "_2"] = value
    return out


def reference(
    x, c, w_mod, b_mod, norm1_w, w_in, lam_re, lam_im, log_dt, ssm_b_re, ssm_b_im, ssm_c_re,
    ssm_c_im, ssm_d, w_glu, b_glu, q_norm_w, k_norm_w, rel_bias, sinks, out_norm_ssm,
    out_norm_attn, w_out, norm2_w, w_up, conv_w, conv_b, w_down, c_2, ctx_2, c_ctx_2, ada_w_2,
    ada_b_2, w_in_2, hg_lb_2, hg_norm_g_2, sc_conv_w_2, sg_ln_g_2, sg_ln_b_2, sg_w_2, sg_b_2,
    w_out_2, ln1_g_2, ln1_b_2, ffn_up_2, ffn_conv_w_2, ffn_conv_b_2, ffn_down_2, ln2_g_2,
    ln2_b_2,
):
    x = first_block(
        x, c, w_mod, b_mod, norm1_w, w_in, lam_re, lam_im, log_dt, ssm_b_re, ssm_b_im, ssm_c_re,
        ssm_c_im, ssm_d, w_glu, b_glu, q_norm_w, k_norm_w, rel_bias, sinks, out_norm_ssm,
        out_norm_attn, w_out, norm2_w, w_up, conv_w, conv_b, w_down,
    )
    return second_block(
        x, c_2, ctx_2, c_ctx_2, ada_w_2, ada_b_2, w_in_2, hg_lb_2, hg_norm_g_2, sc_conv_w_2,
        sg_ln_g_2, sg_ln_b_2, sg_w_2, sg_b_2, w_out_2, ln1_g_2, ln1_b_2, ffn_up_2, ffn_conv_w_2,
        ffn_conv_b_2, ffn_down_2, ln2_g_2, ln2_b_2,
    )


_drawn_inputs = setup_inputs


def setup_inputs(seed=0):
    import zlib

    import numpy as np

    out = dict(_drawn_inputs(seed))
    spreads = {}
    factors = {'norm1_w': 3.841,
     'lam_re': 64.0,
     'lam_im': 29.76,
     'log_dt': 35.008,
     'ssm_b_re': 41.672,
     'ssm_b_im': 42.84,
     'ssm_c_re': 43.432,
     'ssm_c_im': 40.272,
     'b_glu': 8.0,
     'q_norm_w': 8.0,
     'k_norm_w': 8.0,
     'sinks': 173.711,
     'out_norm_ssm': 4.94,
     'out_norm_attn': 5.012,
     'norm2_w': 3.887,
     'conv_b': 8.0,
     'ctx_2': 85.911,
     'c_ctx_2': 5.48,
     'hg_norm_g_2': 2.819,
     'sg_ln_g_2': 2.716}
    for name, (base, spread) in spreads.items():
        noise = np.random.default_rng([zlib.crc32(name.encode()), seed]).standard_normal(out[name].shape)
        drawn = base * np.exp(spread * noise) if base else spread * noise
        out[name] = jnp.asarray(drawn.astype(out[name].dtype))
    for name, factor in factors.items():
        out[name] = (out[name] * factor).astype(out[name].dtype)
    return out
```

```python
import math
from contextlib import ExitStack

import numpy as np

import concourse.bass as bass
from concourse import mybir

F32 = mybir.dt.float32
I32 = mybir.dt.int32
U32 = mybir.dt.uint32
ALU = mybir.AluOpType
ACT = mybir.ActivationFunctionType
AX = mybir.AxisListType

P = 128
T = 1024
HALF = 512
D = 1024
KD = D // P
EPS = 1e-6

D_SSM, SSM_GROUP, N_GROUPS, SSM_STATE = 512, 16, 32, 64
U_TILES = D_SSM // P
S_TILES = N_GROUPS * SSM_STATE // P
SPU = S_TILES // U_TILES
HEAD_DIM, N_Q, N_KV = 64, 8, 2
D_ATTN = N_Q * HEAD_DIM
A_TILES = D_ATTN // P
KV_DIM = N_KV * HEAD_DIM
D_IN = D_SSM + D_ATTN + 2 * KV_DIM
WINDOW = 128
NB = T // WINDOW
N_BUCKETS, MAX_DISTANCE = 32, 128
NEG_INF = -1e30
D_FF = 2816
FT = D_FF // P
TAB = 32

GRID_W = 64
GRID_H = T // GRID_W
CTX = 256
TT = CTX + T
HG_DK, HG_HEADS, HG_WIDTH = 128, 4, 512
SC_WIDTH, SG_WIDTH, SG_HEADS, SG_HD = 256, 256, 4, 64
IN2 = 5 * HG_WIDTH + 3 * SC_WIDTH + 2 * SG_WIDTH
O_Q, O_G, O_SC = 3 * HG_WIDTH, 4 * HG_WIDTH, 5 * HG_WIDTH
O_SG = O_SC + 3 * SC_WIDTH
ALPHA = 2.0 ** 0.25
TINY = 1e-30
CHUNK = 128
LEVELS = [64, 32, 16, 8, 4, 2, 1]
NCH = TT // CHUNK
CCH = CTX // CHUNK


def bucket_of(n):
    n = np.maximum(n, 0)
    exact = N_BUCKETS // 2
    log_part = np.log(np.maximum(n, 1) / exact) / math.log(MAX_DISTANCE / exact)
    large = np.minimum(exact + (log_part * (N_BUCKETS - exact)).astype(np.int32), N_BUCKETS - 1)
    return np.where(n < exact, n, large).astype(np.int32)


RB = 384


def bucket_selection():
    sel = np.zeros((N_BUCKETS + 1, RB), np.float32)
    for i in range(RB):
        dist = 2 * WINDOW - 1 - i
        if 0 <= dist < WINDOW:
            sel[bucket_of(np.array([dist]))[0], i] = 1.0
        else:
            sel[N_BUCKETS, i] = NEG_INF
    return sel


VECTORS = [
    ("c", 8), ("c_2", 8), ("c_ctx_2", 8), ("b_mod", 48), ("norm1_w", 8), ("norm2_w", 8),
    ("lam_re", 16), ("lam_im", 16), ("ssm_d", 4), ("b_glu", 4),
    ("ada_b_2", 48), ("out_norm_ssm", 4), ("out_norm_attn", 4), ("conv_b", 44), ("conv_w", 132),
    ("q_norm_w", 1), ("k_norm_w", 1),
    ("hg_lb_2", 8), ("hg_norm_g_2", 1), ("sc_conv_w_2", 6), ("ln1_g_2", 8), ("ln1_b_2", 8),
    ("ln2_g_2", 8), ("ln2_b_2", 8), ("ffn_conv_b_2", 22), ("ffn_conv_w_2", 198),
]
ROW_OF, _r = {}, 0
for _name, _n in VECTORS:
    ROW_OF[_name] = _r
    _r += _n
N_ROWS = _r
N_VT = -(-N_ROWS // P)

ARENA = 30992


class Kernel:

    def __init__(self, nc, ins, out, ctx):
        self.nc, self.ins, self.out, self.ctx = nc, ins, out, ctx
        self.n_sems = 0
        self.stage_ctx, self.stage_sems = ctx, []
        self.vec = self.sb("vec", [P, N_VT * P])
        self.ident = self.sb("ident", [P, P])
        self.ones = self.sb("ones", [P, P])
        self.halves = self.sb("halves", [P, P])
        self.mod1 = self.sb("mod1", [P, 6, KD])
        self.mod2 = self.sb("mod2", [P, 6, KD, 2])
        self.gain = self.sb("gain", [P, 2, KD])
        self.cact = self.sb("cact", [P, 3, KD])
        self.xT = self.sb("xT", [P, KD, T])
        self.hT = self.sb("hT", [P, KD, TT])
        self.arena = self.sb("arena", [P, ARENA])
        self.sink = self.sb("sink", [P, N_Q])
        self.ssm_neg = self.sb("ssm_neg", [P, 5, S_TILES])
        self.masks = self.sb("masks", [P, 2, len(LEVELS), P])
        self.lower = self.sb("lower", [P, 2 * HG_HEADS])
        self.one_less = self.sb("one_less", [P, 2 * HG_HEADS])
        self.chunk_starts = self.ar(ARENA - TT - 1, TT + 1)
        self.ps = ctx.enter_context(nc.psum_tensor("ps", [P, 8, HALF], F32))
        self.w_in_loaded = self.sem("w_in_loaded")
        self.stage_ctx, self.stage_sems = ExitStack(), []

    def sb(self, name, shape, dt=F32):
        return self.ctx.enter_context(self.nc.sbuf_tensor(name, shape, dt))

    def sem(self, name):
        self.n_sems += 1
        s = self.stage_ctx.enter_context(self.nc.semaphore(f"{name}_{self.n_sems}"))
        self.stage_sems.append(s)
        return s

    def release_sems(self):
        with self.nc.Block() as block:
            @block.sync
            def _(sp):
                for s in self.stage_sems:
                    sp.sem_clear(s)
        self.stage_ctx.close()
        self.stage_ctx, self.stage_sems = ExitStack(), []

    def col(self, name, i=0, n=1):
        r = ROW_OF[name] + i
        return self.vec[:, r:r + n]

    def ar(self, at, *shape):
        n = int(np.prod(shape))
        assert at + n <= ARENA, (at, n)
        v = self.arena[:, at:at + n]
        names = "abcd"[:len(shape)]
        if len(shape) == 1:
            return v
        return v.rearrange(f"p ({' '.join(names)}) -> p {' '.join(names)}",
                           **{x: s for x, s in zip(names, shape)})


def chained(eng, sem, start=0):
    count = [start]

    def link(instruction):
        count[0] += 1
        instruction.then_inc(sem, 1)
        eng.wait_ge(sem, count[0])

    return link


def stage_load(k):
    nc, ins = k.nc, k.ins
    raw = k.ar(0, N_VT, P)
    x_rows = k.ar(N_VT * P, T // P, D)
    rows_in, x_in, made, turned, copied = map(k.sem, ("rows_in", "x_in", "made", "turned", "copied"))

    def row_view(name, n):
        a = ins[name]
        flat = a.rearrange(" ".join("abcd"[:len(a.shape)]) + " -> (" + " ".join("abcd"[:len(a.shape)]) + ")")
        return flat

    loads = []
    for name, n in VECTORS:
        flat, at, done = row_view(name, n), ROW_OF[name], 0
        while done < n:
            m = min(n - done, P - (at + done) % P)
            tile, row = divmod(at + done, P)
            if name in ("q_norm_w", "k_norm_w"):
                for half in range(2):
                    loads.append((raw[row:row + 1, tile, half * HEAD_DIM:(half + 1) * HEAD_DIM],
                                  flat.rearrange("(a b) -> a b", a=1)))
            else:
                loads.append((raw[row:row + m, tile, :],
                              flat[done * P:(done + m) * P].rearrange("(a b) -> a b", b=P)))
            done += m
    groups = [list(range(4 * g, 4 * g + 4)) for g in range(2)]

    with nc.Block() as block:
        @block.sync
        def _(sp):
            for t in range(T // P):
                sp.dma_start(x_rows[:, t, :], ins["x"][0, t * P:(t + 1) * P, :]).then_inc(x_in, 16)

        @block.gpsimd
        def _(pool):
            pool.memset(k.ident[:, :], 0.0).then_inc(made, 1)
            pool.memset(k.ones[:, :], 1.0).then_inc(made, 1)
            pool.memset(k.halves[:, :], 0.0).then_inc(made, 1)
            pool.wait_ge(made, 3)
            pool.affine_select(out=k.ident[:, :], in_=k.ident[:, :], compare_op=ALU.not_equal, fill=1.0,
                               base=0, pattern=[[-1, P]], channel_multiplier=1).then_inc(made, 1)
            pool.wait_ge(made, 4)
            pool.memset(k.halves[0:64, 0:64], 1.0).then_inc(made, 1)
            pool.memset(k.halves[64:128, 64:128], 1.0).then_inc(made, 1)

        @block.scalar
        def _(act):
            for dst, src in loads:
                act.dma_start(dst, src).then_inc(rows_in, 16)

        @block.tensor
        def _(pe):
            pe.wait_ge(made, 6)
            pe.wait_ge(rows_in, 16 * len(loads))
            for v in range(N_VT):
                n = min(P, N_ROWS - v * P)
                last = pe.transpose(k.ps[:, v // 4, (v % 4) * P:(v % 4) * P + n],
                                    raw[0:n, v, :], k.ident[0:n, 0:n])
            last.then_inc(turned, 1)
            pe.wait_ge(x_in, 16 * (T // P))
            unit = 0
            for f in range(KD):
                for g in groups:
                    if unit >= 6:
                        pe.wait_ge(copied, unit - 6 + 1 + 1)
                    bank = 2 + unit % 6
                    for n, t in enumerate(g):
                        last = pe.transpose(k.ps[:, bank, n * P:(n + 1) * P],
                                            x_rows[:, t, f * P:(f + 1) * P], k.ident[:, :])
                    last.then_inc(turned, 1)
                    unit += 1

        @block.vector
        def _(dve):
            dve.wait_ge(turned, 1)
            dve.tensor_copy(k.vec[:, 0:min(N_ROWS, 4 * P)], k.ps[:, 0, 0:min(N_ROWS, 4 * P)])
            dve.tensor_copy(k.vec[:, 4 * P:N_ROWS], k.ps[:, 1, 0:N_ROWS - 4 * P]).then_inc(copied, 1)
            for unit in range(2 * KD):
                f, g = divmod(unit, 2)
                dve.wait_ge(turned, unit + 2)
                dve.tensor_copy(k.xT[:, f, g * HALF:(g + 1) * HALF],
                                k.ps[:, 2 + unit % 6, :]).then_inc(copied, 1)


def stage_modulation(k):
    nc, ins = k.nc, k.ins
    w1, w2 = k.ar(0, KD, D), k.ar(KD * D, KD, D)
    c1 = k.cact[:, 0, :]
    silu_c, in1, in2, mm1, mm2, ev1, ev2 = map(k.sem, ("silu_c", "in1", "in2", "mm1", "mm2", "ev1", "ev2"))
    b1 = k.col("b_mod", 0, 48).rearrange("p (m f) -> p m f", m=6)
    b2 = k.col("ada_b_2", 0, 48).rearrange("p (m f) -> p m f", m=6)
    src1 = ins["w_mod"].rearrange("o (k p) (m n) -> m p (o k) n", p=P, m=6)
    src2 = ins["ada_w_2"].rearrange("o (k p) (m n) -> m p (o k) n", p=P, m=6)
    out1, out2 = k.ps[:, 0, 0:KD], k.ps[:, 1, 0:2 * KD].rearrange("p (f c) -> p f c", c=2)

    with nc.Block() as block:
        @block.sync
        def _(sp):
            with sp.Fori(0, 6) as m:
                sp.wait_ge(ev1, m + 1)
                sp.dma_start(w1, src1[m]).then_inc(in1, 16)
                sp.wait_ge(ev2, m + 1)
                sp.dma_start(w2, src2[m]).then_inc(in2, 16)

        @block.scalar
        def _(act):
            act.activation(k.cact[:, :, :], k.vec[:, 0:3 * KD].rearrange("p (c f) -> p c f", c=3),
                           ACT.Silu).then_inc(silu_c, 1)

        @block.tensor
        def _(pe):
            pe.wait_ge(silu_c, 1)
            with pe.Fori(0, 6) as m:
                pe.wait_ge(ev1, m + 1)
                pe.wait_ge(in1, m * 16 + 16)
                for f in range(KD):
                    for kt in range(KD):
                        last = pe.matmul(out1[:, f:f + 1], w1[:, kt, f * P:(f + 1) * P], c1[:, kt:kt + 1],
                                         start=kt == 0, stop=kt == KD - 1)
                last.then_inc(mm1, 1)
                pe.wait_ge(ev2, m + 1)
                pe.wait_ge(in2, m * 16 + 16)
                for f in range(KD):
                    for kt in range(KD):
                        last = pe.matmul(out2[:, f, :], w2[:, kt, f * P:(f + 1) * P], k.cact[:, 1:3, kt],
                                         start=kt == 0, stop=kt == KD - 1)
                last.then_inc(mm2, 1)

        @block.vector
        def _(dve):
            dve.sem_inc(ev1, 1)
            dve.sem_inc(ev2, 1)
            with dve.Fori(0, 6) as m:
                dve.wait_ge(mm1, m + 1)
                dve.tensor_tensor(k.mod1[:, m, :], out1, b1[:, m, :], ALU.add).then_inc(ev1, 1)
                dve.wait_ge(mm2, m + 1)
                for c in range(2):
                    last = dve.tensor_tensor(k.mod2[:, m, :, c], out2[:, :, c], b2[:, m, :], ALU.add)
                last.then_inc(ev2, 1)


def stage_norm(k, gain_index, src, dst, tiles, width, shift, weight, scale, centre=False, tokens=T, eps=EPS,
               tmp_at=0):
    nc = k.nc
    halves = [(a, min(a + HALF, tokens)) for a in range(0, tokens, HALF)]
    nh = len(halves)
    sq = k.ar(tmp_at, 2, T)
    rstd = k.ar(tmp_at + 2 * T, T)
    mean = k.ar(tmp_at + 3 * T, T)
    sqd, summed, stat, used, normed, meaned, centred, v_ord = map(
        k.sem, ("sqd", "summed", "stat", "used", "normed", "meaned", "centred", "v_ord"))

    def sum_bank(n):
        return k.ps[:, n, :]

    with nc.Block() as block:
        @block.tensor
        def _(pe):
            if centre:
                for n, (a, b) in enumerate(halves):
                    for t in range(tiles):
                        last = pe.matmul(sum_bank(2 + n)[:, 0:b - a], k.ones[:, :], src(t)[:, a:b],
                                         start=t == 0, stop=t == tiles - 1)
                last.then_inc(meaned, 1)
            for t in range(tiles):
                pe.wait_ge(sqd, t + 1)
                for n, (a, b) in enumerate(halves):
                    last = pe.matmul(sum_bank(n)[:, 0:b - a], k.ones[:, :], sq[:, t % 2, a:b],
                                     start=t == 0, stop=t == tiles - 1, skip_group_check=True)
                last.then_inc(used, 1)

        @block.scalar
        def _(act):
            for t in range(tiles):
                if t >= 2:
                    act.wait_ge(used, t - 1)
                if centre:
                    act.wait_ge(centred, t + 1)
                act.activation(sq[:, t % 2, 0:tokens], (dst if centre else src)(t), ACT.Square).then_inc(sqd, 1)
            act.wait_ge(stat, 1)
            act.activation(rstd[:, 0:tokens], rstd[:, 0:tokens], ACT.Sqrt).then_inc(stat, 1)
            for t in range(tiles):
                act.wait_ge(normed, t + 1)
                if shift is not None:
                    act.activation(dst(t), dst(t), ACT.Identity, bias=shift(t), scale=weight(t))
                elif weight is not None:
                    act.activation(dst(t), dst(t), ACT.Identity, scale=weight(t))

        @block.vector
        def _(dve):
            link = chained(dve, v_ord)
            if scale is not None:
                g = k.gain[:, gain_index, :]
                if scale[1] is None:
                    link(dve.tensor_scalar(g, scale[0], 1.0, None, ALU.add))
                else:
                    link(dve.tensor_scalar(g, scale[0], 1.0, None, ALU.add))
                    link(dve.tensor_tensor(g, g, scale[1], ALU.mult))
            if centre:
                dve.wait_ge(meaned, 1)
                for n, (a, b) in enumerate(halves):
                    last = dve.tensor_scalar(mean[:, a:b], sum_bank(2 + n)[:, 0:b - a], 1.0 / width, None, ALU.mult)
                    link(last)
                for t in range(tiles):
                    dve.tensor_tensor(dst(t), src(t), mean[:, 0:tokens], ALU.subtract).then_inc(centred, 1)
            dve.wait_ge(used, tiles)
            for n, (a, b) in enumerate(halves):
                last = dve.tensor_scalar(rstd[:, a:b], sum_bank(n)[:, 0:b - a], 1.0 / width, eps, ALU.mult, ALU.add)
            last.then_inc(stat, 1)
            dve.wait_ge(stat, 2)
            link(dve.reciprocal(rstd[:, 0:tokens], rstd[:, 0:tokens]))
            if centre:
                dve.wait_ge(centred, tiles)
            for t in range(tiles):
                dve.tensor_tensor(dst(t), (dst if centre else src)(t), rstd[:, 0:tokens], ALU.mult).then_inc(normed, 1)


def stage_norm1(k):
    stage_norm(k, 0, lambda t: k.xT[:, t, :], lambda t: k.hT[:, t, CTX:TT], KD, D,
               shift=lambda t: k.mod1[:, 0, t:t + 1], weight=lambda t: k.gain[:, 0, t:t + 1],
               scale=(k.mod1[:, 1, :], k.col("norm1_w", 0, KD)))


A_U = 0
A_Q = A_U + U_TILES * T
A_K = A_Q + A_TILES * T
A_V = A_K + N_KV * T
A_FREE = A_V + NB * KV_DIM
W_COLS = D_SSM + D_ATTN + 2 * KV_DIM + KV_DIM
A_WIN = A_FREE


def linear_units(k, pe, units, lhs, rhs, n_k, made, read, first_pair=0, pairs=4, before=None):
    for n in range(units):
        if before is not None:
            before(n)
        if n >= pairs:
            pe.wait_ge(read, n - pairs + 1)
        for half in range(2):
            bank = 2 * ((n % pairs) + first_pair) + half
            for kt in range(n_k):
                last = pe.matmul(k.ps[:, bank, :], lhs(n, kt), rhs(kt, half), start=kt == 0, stop=kt == n_k - 1)
        last.then_inc(made, 1)


def pair(k, n, pairs=4):
    b = 2 * (n % pairs)
    return k.ps[:, b:b + 2, :].rearrange("p b n -> p (b n)")


def stage_project(k):
    nc, ins = k.nc, k.ins
    w = k.ar(A_WIN, KD, W_COLS)
    u, q, kk = k.ar(A_U, U_TILES, T), k.ar(A_Q, A_TILES, T), k.ar(A_K, N_KV, T)
    v = k.ar(A_V, NB, KV_DIM)
    w_src = ins["w_in"].rearrange("o (k p) n -> p (o k) n", p=P)
    made, read, v_made = map(k.sem, ("made", "read", "v_made"))
    k_at = D_SSM + D_ATTN
    wv = w[:, :, k_at + 2 * KV_DIM:W_COLS]
    outs = [u[:, t, :] for t in range(U_TILES)] + [q[:, t, :] for t in range(A_TILES)] + \
           [kk[:, t, :] for t in range(N_KV)]
    units = len(outs)

    with nc.Block() as block:
        @block.sync
        def _(sp):
            sp.dma_start(w[:, :, 0:k_at], w_src[:, :, 0:k_at]).then_inc(k.w_in_loaded, 16)
            for g in range(N_KV):
                for copy in range(2):
                    to = k_at + (2 * g + copy) * HEAD_DIM
                    sp.dma_start(w[:, :, to:to + HEAD_DIM],
                                 w_src[:, :, k_at + g * HEAD_DIM:k_at + (g + 1) * HEAD_DIM])\
                        .then_inc(k.w_in_loaded, 16)
            sp.dma_start(wv, w_src[:, :, k_at + KV_DIM:D_IN]).then_inc(k.w_in_loaded, 16)

        @block.tensor
        def _(pe):
            pe.wait_ge(k.w_in_loaded, 6 * 16)
            linear_units(k, pe, units, lambda n, kt: w[:, kt, n * P:(n + 1) * P],
                         lambda kt, half: k.hT[:, kt, CTX + half * HALF:CTX + (half + 1) * HALF], KD, made, read)
            for n in range(2):
                pe.wait_ge(read, units - 4 + (n + 2) % 4 + 1)
                for t in range(4):
                    b = 4 * n + t
                    for kt in range(KD):
                        last = pe.matmul(k.ps[:, 2 * ((units + n) % 4), t * P:(t + 1) * P],
                                         k.hT[:, kt, CTX + b * P:CTX + (b + 1) * P], wv[:, kt, :],
                                         start=kt == 0, stop=kt == KD - 1)
                last.then_inc(v_made, 1)

        @block.vector
        def _(dve):
            for n in range(0, units, 2):
                dve.wait_ge(made, n + 1)
                dve.tensor_copy(outs[n], pair(k, n)).then_inc(read, 1)
                if n + 1 < units:
                    dve.wait_ge(made, n + 2)
                    dve.tensor_copy(outs[n + 1], pair(k, n + 1)).then_inc(read, 1)
            for n in range(2):
                dve.wait_ge(v_made, n + 1)
                dve.tensor_copy(v[:, 4 * n:4 * n + 4, :].rearrange("p a b -> p (a b)"),
                                k.ps[:, 2 * ((units + n) % 4), :])


def stage_qk_norm(k):
    nc = k.nc
    q, kk = k.ar(A_Q, A_TILES, T), k.ar(A_K, N_KV, T)
    sq, rstd = k.ar(A_FREE, 2, T), k.ar(A_FREE + 2 * T, 2, T)
    tiles = [(q[:, t, :], "q_norm_w") for t in range(A_TILES)] + [(kk[:, t, :], "k_norm_w") for t in range(N_KV)]
    sqd, summed, stat, root, v_ord = map(k.sem, ("sqd", "summed", "stat", "root", "v_ord"))

    with nc.Block() as block:
        @block.scalar
        def _(act):
            for n, (x, _) in enumerate(tiles):
                if n >= 2:
                    act.wait_ge(summed, n - 1)
                act.activation(sq[:, n % 2, :], x, ACT.Square).then_inc(sqd, 1)
                act.wait_ge(stat, n + 1)
                act.activation(rstd[:, n % 2, :], rstd[:, n % 2, :], ACT.Sqrt).then_inc(root, 1)

        @block.tensor
        def _(pe):
            for n in range(len(tiles)):
                pe.wait_ge(sqd, n + 1)
                if n >= 4:
                    pe.wait_ge(stat, n - 3)
                for half in range(2):
                    last = pe.matmul(k.ps[:, 2 * (n % 4) + half, :], k.halves[:, :],
                                     sq[:, n % 2, half * HALF:(half + 1) * HALF], start=True, stop=True)
                last.then_inc(summed, 1)

        @block.vector
        def _(dve):
            link = chained(dve, v_ord)
            for n, (x, w) in enumerate(tiles):
                r = rstd[:, n % 2, :]
                dve.wait_ge(summed, n + 1)
                dve.tensor_scalar(r, pair(k, n), 1.0 / HEAD_DIM, EPS, ALU.mult, ALU.add).then_inc(stat, 1)
                dve.wait_ge(root, n + 1)
                link(dve.reciprocal(r, r))
                link(dve.scalar_tensor_tensor(x, x, k.col(w), r, ALU.mult, ALU.mult))


A_Y = 0
A_BIAS = A_FREE
A_ATT = A_BIAS + N_Q * 2 * WINDOW


def stage_bias(k):
    nc, ins = k.nc, k.ins
    bias = k.ar(A_BIAS, N_Q, 2 * WINDOW)
    table, sel, rows = k.ar(A_ATT, N_Q), k.ar(A_ATT + 8, RB), k.ar(A_ATT + 8 + RB, RB)
    sink_row = k.ar(A_ATT + 8 + 2 * RB, N_Q)
    mirrored, flip = k.ar(A_ATT + 16 + 2 * RB, N_Q, 2 * WINDOW), k.ar(A_ATT + 16 + 2 * RB + N_Q * 2 * WINDOW, P)
    k.rows_dram = nc.dram_tensor("bias_rows", (N_Q, RB), F32)
    rows_dram = k.rows_dram.ap()
    loaded, ones_set, made, copied, stored, flip_set, fetched = map(
        k.sem, ("loaded", "ones_set", "made", "copied", "stored", "flip_set", "fetched"))

    with nc.Block() as block:
        @block.gpsimd
        def _(pool):
            pool.memset(flip, 0.0).then_inc(flip_set, 1)
            pool.wait_ge(flip_set, 1)
            pool.affine_select(out=flip, in_=flip, compare_op=ALU.not_equal, fill=1.0, base=1 - P,
                               pattern=[[1, P]], channel_multiplier=1).then_inc(flip_set, 1)

        @block.vector
        def _(dve):
            dve.memset(table[N_BUCKETS:N_BUCKETS + 1, :], 1.0).then_inc(ones_set, 1)
            dve.wait_ge(made, 1)
            dve.tensor_copy(rows[0:N_Q, :], k.ps[0:N_Q, 0, 0:RB]).then_inc(copied, 1)
            dve.wait_ge(made, 2)
            dve.tensor_copy(k.sink[:, :], k.ps[:, 1, 0:N_Q])
            dve.wait_ge(made, 3)
            dve.tensor_copy(bias.rearrange("p a b -> p (a b)"), k.ps[:, 2:6, :].rearrange("p b n -> p (b n)"))

        @block.tensor
        def _(pe):
            pe.wait_ge(loaded, 48)
            pe.wait_ge(ones_set, 1)
            pe.matmul(k.ps[0:N_Q, 0, 0:RB], table[0:N_BUCKETS + 1, :], sel[0:N_BUCKETS + 1, :],
                      start=True, stop=True).then_inc(made, 1)
            pe.matmul(k.ps[:, 1, 0:N_Q], k.ones[0:1, :], sink_row[0:1, :], start=True, stop=True).then_inc(made, 1)
            pe.wait_ge(flip_set, 2)
            pe.wait_ge(fetched, 16 * N_Q)
            for n in range(4):
                last = pe.matmul(k.ps[:, 2 + n, :], flip, mirrored[:, 2 * n:2 * n + 2, :].rearrange("p a b -> p (a b)"),
                                 start=True, stop=True)
            last.then_inc(made, 1)

        @block.sync
        def _(sp):
            sp.dma_start(table[0:N_BUCKETS, :], ins["rel_bias"]).then_inc(loaded, 16)
            sp.dma_start(sel[0:N_BUCKETS + 1, :], ins["bucket_sel"]).then_inc(loaded, 16)
            sp.dma_start(sink_row[0:1, :], ins["sinks"]).then_inc(loaded, 16)
            sp.wait_ge(copied, 1)
            sp.dma_start(rows_dram, rows[0:N_Q, :]).then_inc(stored, 16)
            sp.wait_ge(stored, 16)
            for h in range(N_Q):
                window = bass.AP(k.rows_dram, h * RB, [[1, P], [1, 2 * WINDOW]])
                sp.dma_start(mirrored[:, h, :], window).then_inc(fetched, 16)


def stage_attention(k):
    nc = k.nc
    q, kk, v = k.ar(A_Q, A_TILES, T), k.ar(A_K, N_KV, T), k.ar(A_V, NB, KV_DIM)
    bias = k.ar(A_BIAS, N_Q, 2 * WINDOW)
    logits = k.ar(A_ATT, 2, 2, 2 * WINDOW)
    probs = k.ar(A_ATT + 1024, 2, 2, 2 * WINDOW)
    probs_t = k.ar(A_ATT + 2048, 2, 4, P)
    small = k.ar(A_ATT + 3072, 6, 2)
    yT = k.ar(A_Q, A_TILES, T)
    scale = HEAD_DIM ** -0.5
    units = [(n, t) for n in range(NB) for t in range(A_TILES)]
    scored, softmaxed, turned, turned_read, mixed, mixed_read, maxed, exped, v_ord, sink_exp = map(
        k.sem, ("scored", "softmaxed", "turned", "turned_read", "mixed", "mixed_read", "maxed", "exped",
                "v_ord", "sink_exp"))

    def keys(n):
        return (0, WINDOW) if n == 0 else ((n - 1) * WINDOW, 2 * WINDOW)

    with nc.Block() as block:
        @block.tensor
        def _(pe):
            def scores(i):
                n, t = units[i]
                k0, nk = keys(n)
                if i >= 2:
                    pe.wait_ge(maxed, i - 1)
                for j in range(2):
                    h = 2 * t + j
                    rows = slice(64 * j, 64 * j + 64)
                    last = pe.matmul(k.ps[:, 2 * (i % 2) + j, 0:nk], q[rows, t, n * WINDOW:(n + 1) * WINDOW],
                                     kk[rows, h // (N_Q // N_KV), k0:k0 + nk], start=True, stop=True)
                last.then_inc(scored, 1)

            def mix(i):
                n, t = units[i]
                k0, nk = keys(n)
                pe.wait_ge(softmaxed, i + 1)
                if i >= 2:
                    pe.wait_ge(turned_read, i - 1)
                for j in range(2):
                    for b in range(nk // P):
                        last = pe.transpose(k.ps[:, 4 + i % 2, (2 * j + b) * P:(2 * j + b + 1) * P],
                                            probs[:, i % 2, j, b * P:(b + 1) * P], k.ident[:, :])
                last.then_inc(turned, 1)
                pe.wait_ge(turned_read, i + 1)
                if i >= 2:
                    pe.wait_ge(mixed_read, i - 1)
                for j in range(2):
                    h = 2 * t + j
                    g = h // (N_Q // N_KV)
                    for b in range(nk // P):
                        last = pe.matmul(k.ps[64 * j:64 * j + 64, 6 + i % 2, 0:P],
                                         v[:, k0 // P + b, g * 64:(g + 1) * 64], probs_t[:, i % 2, 2 * j + b, :],
                                         start=b == 0, stop=b == nk // P - 1)
                last.then_inc(mixed, 1)

            for i in range(len(units) + 1):
                if i < len(units):
                    scores(i)
                if i >= 1:
                    mix(i - 1)

        @block.scalar
        def _(act):
            for i, (n, t) in enumerate(units):
                k0, nk = keys(n)
                act.wait_ge(maxed, i + 1)
                for j in range(2):
                    act.activation(probs[:, i % 2, j, 0:nk], logits[:, i % 2, j, 0:nk], ACT.Exp,
                                   bias=small[:, 1, j:j + 1], accum_out=small[:, 2, j:j + 1])
                    last = act.activation(small[:, 3, j:j + 1], k.sink[:, 2 * t + j:2 * t + j + 1], ACT.Exp,
                                          bias=small[:, 1, j:j + 1])
                last.then_inc(exped, 1)
                act.wait_ge(turned, i + 1)
                act.activation(probs_t[:, i % 2, :, :] if nk > P else probs_t[:, i % 2, 0:4:2, :],
                               k.ps[:, 4 + i % 2, :].rearrange("p (a b) -> p a b", b=P) if nk > P else
                               k.ps[:, 4 + i % 2, :].rearrange("p (a b) -> p a b", b=P)[:, 0:4:2, :],
                               ACT.Copy).then_inc(turned_read, 1)

        @block.vector
        def _(dve):
            link = chained(dve, v_ord)

            def output(i):
                n, t = units[i]
                dve.wait_ge(mixed, i + 1)
                for j in range(2):
                    last = dve.tensor_copy(yT[64 * j:64 * j + 64, t, n * WINDOW:(n + 1) * WINDOW],
                                           k.ps[64 * j:64 * j + 64, 6 + i % 2, 0:P])
                last.then_inc(mixed_read, 1)

            for i, (n, t) in enumerate(units):
                k0, nk = keys(n)
                x = logits[:, i % 2, :, 0:nk]
                b = bias[:, 2 * t:2 * t + 2, 2 * WINDOW - nk:2 * WINDOW]
                dve.wait_ge(scored, i + 1)
                link(dve.scalar_tensor_tensor(x, k.ps[:, 2 * (i % 2):2 * (i % 2) + 2, 0:nk],
                                              scale, b, ALU.mult, ALU.add))
                link(dve.tensor_reduce(small[:, 0, :], x, AX.X, ALU.max))
                link(dve.tensor_tensor(small[:, 0, :], small[:, 0, :], k.sink[:, 2 * t:2 * t + 2], ALU.max))
                dve.tensor_scalar(small[:, 1, :], small[:, 0, :], -1.0, None, ALU.mult).then_inc(maxed, 1)
                if i >= 1:
                    output(i - 1)
                dve.wait_ge(exped, i + 1)
                link(dve.tensor_tensor(small[:, 4, :], small[:, 2, :], small[:, 3, :], ALU.add))
                link(dve.reciprocal(small[:, 5, :], small[:, 4, :]))
                for j in range(2):
                    last = dve.tensor_scalar(probs[:, i % 2, j, 0:nk], probs[:, i % 2, j, 0:nk],
                                             small[:, 5, j:j + 1], None, ALU.mult)
                last.then_inc(softmaxed, 1)
            output(len(units) - 1)


H_BT, H_CT = 0, 2 * S_TILES * P
H_TAB = 2 * H_CT
H_SMALL = H_TAB + 2 * S_TILES * TAB
A_W = A_K
A_IN = A_W + 4 * T
A_Z = A_IN + 4 * T
A_OUT = A_Z + 4 * T
A_S = A_OUT + 4 * T
LN2_HI, LN2_LO = 0.693359375, -2.12194440e-4
ROUND = 12582912.0
TWO_PI = (6.28125, 1.93500518798828125e-3, 3.01991598195e-7)
POWERS = [TAB << i for i in range(5)]


def views_hT(k):
    flat = k.hT[:, :, :].rearrange("p a b -> p (a b)")

    def at(start, *shape):
        v = flat[:, start:start + int(np.prod(shape))]
        if len(shape) == 1:
            return v
        names = "abcd"[:len(shape)]
        return v.rearrange(f"p ({' '.join(names)}) -> p {' '.join(names)}", **dict(zip(names, shape)))
    return at


def exp_steps(dve, link, out, x, n, r):
    link(dve.tensor_scalar(x, x, -104.0, 89.0, ALU.max, ALU.min))
    link(dve.tensor_scalar(n, x, 1.4426950408889634, ROUND, ALU.mult, ALU.add))
    link(dve.tensor_scalar(n, n, -ROUND, None, ALU.add))
    link(dve.scalar_tensor_tensor(r, n, -LN2_HI, x, ALU.mult, ALU.add))
    link(dve.scalar_tensor_tensor(r, n, -LN2_LO, r, ALU.mult, ALU.add))
    link(dve.tensor_scalar(out, r, 1.0 / math.factorial(8), None, ALU.mult))
    for i in range(7, 0, -1):
        link(dve.scalar_tensor_tensor(out, out, 1.0 / math.factorial(i), r, ALU.add, ALU.mult))
    link(dve.tensor_scalar(n, n, -127.0, 128.0, ALU.max, ALU.min))
    link(dve.tensor_scalar(r.bitcast(I32), n, 127.0, float(1 << 23), ALU.add, ALU.mult))
    link(dve.scalar_tensor_tensor(out, out, 1.0, r, ALU.add, ALU.mult))


def stage_ssm_params(k):
    nc, ins = k.nc, k.ins
    h = views_hT(k)
    bt, ct = h(H_BT, 2, S_TILES, P), h(H_CT, 2, S_TILES, P)
    tab = h(H_TAB, 2, S_TILES, TAB)
    small = h(H_SMALL, 32, S_TILES)
    b_raw, c_raw = k.ar(A_W, 2, S_TILES, SSM_GROUP), k.ar(A_W + 512, 2, U_TILES, SSM_STATE)
    b_wide, c_wide = k.ar(A_IN, 2, S_TILES, P), k.ar(A_Z, 2, S_TILES, P)
    row_mask = k.ar(A_W + 1024, 8)
    b_scaled, tmp = k.ar(A_OUT, 2, S_TILES, SSM_GROUP), k.ar(A_OUT + 512, 4, S_TILES * TAB)
    ldt, sel = k.ar(A_S, S_TILES), k.ar(A_S + 16, P)
    loaded, made, spread, wide, turned, copied, v_ord, b_ord = map(
        k.sem, ("loaded", "made", "spread", "wide", "turned", "copied", "v_ord", "b_ord"))
    s = lambda i: small[:, i, :]
    (LR, DT, TH, N, R, X2, SN, CS, SIN, CM1, COS, MAG, AIM, AM1, DEN, FR, FI, T1, T2) = range(19)
    k.mag = s(MAG)
    k.powers = small[:, 19:19 + 10, :]
    k.tab, k.bt, k.ct = tab, bt, ct
    k.neg_powers = k.ssm_neg[:, :, :]
    lam_re, lam_im = k.col("lam_re", 0, S_TILES), k.col("lam_im", 0, S_TILES)

    with nc.Block() as block:
        @block.sync
        def _(sp):
            sp.dma_start(ldt[0:2, :], ins["log_dt"].rearrange("o (t k) -> (o k) t", k=2),
                         allow_slow_non_contiguous=True).then_inc(loaded, 16)
            for c, name in enumerate(("ssm_b_re", "ssm_b_im")):
                for half in range(2):
                    sp.dma_start(b_raw[64 * half:64 * half + 64, c],
                                 ins[name].rearrange("o (t k) p h -> (o k) p t h", k=2)[half]).then_inc(loaded, 16)
            for c, name in enumerate(("ssm_c_re", "ssm_c_im")):
                sp.dma_start(c_raw[:, c], ins[name].rearrange("o (j g) h p -> (o g h) j p", g=8)).then_inc(loaded, 16)

        @block.gpsimd
        def _(pool):
            pool.memset(sel[:, :], 1.0).then_inc(made, 1)
            pool.memset(row_mask, 1.0).then_inc(made, 1)
            pool.memset(b_wide, 0.0).then_inc(made, 1)
            pool.wait_ge(made, 3)
            pool.affine_select(out=sel[0:2, :], in_=sel[0:2, :], compare_op=ALU.is_ge, fill=0.0, base=0,
                               pattern=[[1, P]], channel_multiplier=-64).then_inc(made, 1)
            pool.wait_ge(made, 4)
            pool.affine_select(out=sel[0:2, :], in_=sel[0:2, :], compare_op=ALU.is_ge, fill=0.0, base=63,
                               pattern=[[-1, P]], channel_multiplier=64).then_inc(made, 1)
            pool.affine_select(out=row_mask, in_=row_mask, compare_op=ALU.is_ge, fill=0.0, base=0,
                               pattern=[[-16, 8]], channel_multiplier=1).then_inc(made, 1)
            pool.wait_ge(made, 6)
            pool.affine_select(out=row_mask, in_=row_mask, compare_op=ALU.is_ge, fill=0.0, base=15,
                               pattern=[[16, 8]], channel_multiplier=-1).then_inc(made, 1)

        @block.tensor
        def _(pe):
            pe.wait_ge(made, 7)
            pe.wait_ge(loaded, 7 * 16)
            pe.matmul(k.ps[:, 0, 0:S_TILES], sel[0:2, :], ldt[0:2, :], start=True, stop=True).then_inc(spread, 1)
            pe.wait_ge(wide, 1)
            for n in range(16):
                c, g = divmod(n % 8, 4)
                if n >= 7:
                    pe.wait_ge(copied, n - 6)
                for i in range(4):
                    last = pe.transpose(k.ps[:, 1 + n % 7, i * P:(i + 1) * P],
                                        (b_wide if n < 8 else c_wide)[:, c, 4 * g + i, :], k.ident[:, :])
                last.then_inc(turned, 1)

        @block.scalar
        def _(act):
            for n in range(16):
                c, g = divmod(n % 8, 4)
                act.wait_ge(turned, n + 1)
                act.activation((bt if n < 8 else ct)[:, c, 4 * g:4 * g + 4, :].rearrange("p a b -> p (a b)"),
                               k.ps[:, 1 + n % 7, :], ACT.Copy).then_inc(copied, 1)

        @block.vector
        def _(dve):
            link = chained(dve, v_ord)
            tt, ts, stt = dve.tensor_tensor, dve.tensor_scalar, dve.scalar_tensor_tensor
            dve.wait_ge(spread, 1)
            link(dve.tensor_copy(s(T1), k.ps[:, 0, 0:S_TILES]))
            exp_steps(dve, link, s(DT), s(T1), s(N), s(R))
            link(ts(s(LR), lam_re, -1e-4, None, ALU.min))
            link(tt(s(T1), s(DT), s(LR), ALU.mult))
            exp_steps(dve, link, s(MAG), s(T1), s(N), s(R))
            link(tt(s(TH), s(DT), lam_im, ALU.mult))
            link(ts(s(N), s(TH), 1.0 / (2 * math.pi), ROUND, ALU.mult, ALU.add))
            link(ts(s(N), s(N), -ROUND, None, ALU.add))
            for part in TWO_PI:
                link(stt(s(TH), s(N), -part, s(TH), ALU.mult, ALU.add))
            link(ts(s(TH), s(TH), 0.5, None, ALU.mult))
            link(tt(s(X2), s(TH), s(TH), ALU.mult))
            for dst, first in ((SN, 13), (CS, 14)):
                sign = lambda i: -1.0 if (i // 2) % 2 else 1.0
                link(ts(s(dst), s(X2), sign(first) / math.factorial(first), None, ALU.mult))
                for i in range(first - 2, 1, -2):
                    link(stt(s(dst), s(dst), sign(i) / math.factorial(i), s(X2), ALU.add, ALU.mult))
            link(stt(s(SN), s(SN), 1.0, s(TH), ALU.add, ALU.mult))
            link(ts(s(CS), s(CS), 1.0, None, ALU.add))
            link(stt(s(SIN), s(SN), 2.0, s(CS), ALU.mult, ALU.mult))
            link(stt(s(CM1), s(SN), -2.0, s(SN), ALU.mult, ALU.mult))
            link(ts(s(COS), s(CM1), 1.0, None, ALU.add))
            link(tt(s(AIM), s(MAG), s(SIN), ALU.mult))
            link(tt(s(AM1), s(MAG), s(COS), ALU.mult))
            link(ts(s(AM1), s(AM1), -1.0, None, ALU.add))
            link(tt(s(DEN), s(LR), s(LR), ALU.mult))
            link(tt(s(T1), lam_im, lam_im, ALU.mult))
            link(tt(s(DEN), s(DEN), s(T1), ALU.add))
            link(dve.reciprocal(s(DEN), s(DEN)))
            link(tt(s(T1), s(AM1), s(LR), ALU.mult))
            link(tt(s(T2), s(AIM), lam_im, ALU.mult))
            link(tt(s(FR), s(T1), s(T2), ALU.add))
            link(tt(s(FR), s(FR), s(DEN), ALU.mult))
            link(tt(s(T1), s(AIM), s(LR), ALU.mult))
            link(tt(s(T2), s(AM1), lam_im, ALU.mult))
            link(tt(s(FI), s(T1), s(T2), ALU.subtract))
            link(tt(s(FI), s(FI), s(DEN), ALU.mult))
            shape = (P, S_TILES, SSM_GROUP)
            fr, fi = (s(i).unsqueeze(2).to_broadcast(shape) for i in (FR, FI))
            t1 = tmp[:, 0, 0:256].rearrange("p (a b) -> p a b", b=SSM_GROUP)
            t2 = tmp[:, 1, 0:256].rearrange("p (a b) -> p a b", b=SSM_GROUP)
            dve.wait_ge(loaded, 7 * 16)
            link(tt(t1, b_raw[:, 0], fr, ALU.mult))
            link(tt(t2, b_raw[:, 1], fi, ALU.mult))
            link(tt(b_scaled[:, 0], t1, t2, ALU.subtract))
            link(tt(t1, b_raw[:, 1], fr, ALU.mult))
            link(tt(t2, b_raw[:, 0], fi, ALU.mult))
            link(tt(b_scaled[:, 1], t1, t2, ALU.add))
            dve.wait_ge(made, 7)
            for c in range(2):
                for g in range(2):
                    rows = slice(64 * g, 64 * g + 64)
                    for i in range(SPU):
                        at = 32 * i + 16 * g
                        link(dve.tensor_copy(b_wide[rows, c, i:S_TILES:SPU, at:at + SSM_GROUP],
                                             b_scaled[rows, c, i:S_TILES:SPU, :]))
            for c in range(2):
                for i in range(SPU):
                    for g in range(2):
                        m = row_mask[:, 2 * i + g:2 * i + g + 1]
                        link(ts(c_wide[:, c, i:S_TILES:SPU, 64 * g:64 * g + 64], c_raw[:, c],
                                m, 1.0 if c == 0 else -1.0, ALU.mult, ALU.mult))
            dve.sem_inc(wide, 1)
            link(dve.memset(tab[:, 0, :, 0:1], 1.0))
            link(dve.memset(tab[:, 1, :, 0:1], 0.0))
            wr, wi = s(COS), s(SIN)
            n = 1
            while n < T:
                if n < TAB:
                    shape = (P, S_TILES, n)
                    br, bi = (w.unsqueeze(2).to_broadcast(shape) for w in (wr, wi))
                    t = [tmp[:, j, 0:S_TILES * n].rearrange("p (a b) -> p a b", b=n) for j in range(4)]
                    link(tt(t[0], tab[:, 0, :, 0:n], br, ALU.mult))
                    link(tt(t[1], tab[:, 1, :, 0:n], bi, ALU.mult))
                    link(tt(t[2], tab[:, 0, :, 0:n], bi, ALU.mult))
                    link(tt(t[3], tab[:, 1, :, 0:n], br, ALU.mult))
                    link(tt(tab[:, 0, :, n:2 * n], t[0], t[1], ALU.subtract))
                    link(tt(tab[:, 1, :, n:2 * n], t[2], t[3], ALU.add))
                else:
                    link(ts(k.neg_powers[:, POWERS.index(n), :], wi, -1.0, None, ALU.mult))
                n *= 2
                if n < T:
                    if n >= TAB:
                        i = POWERS.index(n)
                        nr, ni = k.powers[:, 2 * i, :], k.powers[:, 2 * i + 1, :]
                    else:
                        nr, ni = (s(SN), s(CS)) if (wr is not None and n in (2, 8)) else (s(X2), s(TH))
                    link(tt(s(T1), wr, wr, ALU.mult))
                    link(tt(s(T2), wi, wi, ALU.mult))
                    link(stt(ni, wr, 2.0, wi, ALU.mult, ALU.mult))
                    link(tt(nr, s(T1), s(T2), ALU.subtract))
                    wr, wi = nr, ni


def stage_ssm(k):
    nc = k.nc
    u = k.ar(A_U, U_TILES, T)
    tables, m_in, z, m_out, st = (k.ar(A_W, 2, 2, T), k.ar(A_IN, 4, T), k.ar(A_Z, 2, 2, T), k.ar(A_OUT, 4, T),
                                  k.ar(A_S, 2, 2, T))
    bu_made, in_done, in_added, scanned, out_done, out_added, y_made, y_sum, scaled, level, seeded = map(
        k.sem, ("bu_made", "in_done", "in_added", "scanned", "out_done", "out_added", "y_made",
                "y_sum", "scaled", "level", "seeded"))
    N = S_TILES
    L = len(POWERS)
    bu = [k.ps[:, 2 * c:2 * c + 2, :].rearrange("p b n -> p (b n)") for c in range(2)]

    def y_banks(j):
        return 4 + 2 * (j % 2)

    with nc.Block() as block:
        @block.tensor
        def _(pe):
            def inputs(i):
                if i >= 1:
                    pe.wait_ge(in_done, 2 * i)
                for c in range(2):
                    for half in range(2):
                        last = pe.matmul(k.ps[:, 2 * c + half, :], k.bt[:, c, i, :],
                                         u[:, i // SPU, half * HALF:(half + 1) * HALF], start=True, stop=True)
                last.then_inc(bu_made, 1)

            def outputs(i):
                j = i // SPU
                pe.wait_ge(out_added, 2 * i + 2)
                if i % SPU == 0 and j >= 2:
                    pe.wait_ge(y_sum, j - 1)
                for c in range(2):
                    for half in range(2):
                        last = pe.matmul(k.ps[:, y_banks(j) + half, :], k.ct[:, c, i, :],
                                         st[:, i % 2, c, half * HALF:(half + 1) * HALF],
                                         start=i % SPU == 0 and c == 0, stop=i % SPU == SPU - 1 and c == 1,
                                         skip_group_check=True)
                last.then_inc(y_made, 1)

            inputs(0)
            inputs(1)
            for i in range(N):
                if i + 2 < N:
                    inputs(i + 2)
                outputs(i)

        @block.scalar
        def _(act):
            def gelu(j):
                act.wait_ge(y_sum, j + 1)
                act.activation(u[:, j, :], u[:, j, :], ACT.Gelu_apprx_tanh)

            def table_level(i, l):
                w, n = tables[:, i % 2], POWERS[l]
                if l == 0:
                    if i >= 2:
                        act.wait_ge(out_done, i - 1)
                    act.activation(w[:, :, 0:TAB], k.tab[:, :, i, :], ACT.Copy).then_inc(seeded, 1)
                    act.wait_ge(seeded, i + 1)
                else:
                    act.wait_ge(level, L * i + l)
                act.activation(w[:, :, n:2 * n], w[:, :, 0:n], ACT.Copy,
                               scale=k.powers[:, 2 * l, i:i + 1]).then_inc(scaled, 1)

            for i in range(N):
                for l in range(L):
                    table_level(i, l)
                if i >= 2 * SPU - 1 and i % SPU == SPU - 1:
                    gelu(i // SPU - 1)
            gelu(U_TILES - 1)

        @block.vector
        def _(dve):
            def table_level(i, l):
                w, n = tables[:, i % 2], POWERS[l]
                dve.wait_ge(scaled, L * i + l + 1)
                dve.scalar_tensor_tensor(w[:, 0, n:2 * n], w[:, 1, 0:n], k.neg_powers[:, l, i:i + 1],
                                         w[:, 0, n:2 * n], ALU.mult, ALU.add)
                dve.scalar_tensor_tensor(w[:, 1, n:2 * n], w[:, 0, 0:n], k.powers[:, 2 * l + 1, i:i + 1],
                                         w[:, 1, n:2 * n], ALU.mult, ALU.add).then_inc(level, 1)

            def rotate_in(i):
                w = tables[:, i % 2]
                dve.wait_ge(level, L * i + L)
                dve.wait_ge(bu_made, i + 1)
                if i >= 1:
                    dve.wait_ge(in_added, 2 * i)
                dve.tensor_tensor(m_in[:, 0, :], bu[0], w[:, 0, :], ALU.mult)
                dve.tensor_tensor(m_in[:, 1, :], bu[1], w[:, 1, :], ALU.mult).then_inc(in_done, 1)
                dve.tensor_tensor(m_in[:, 2, :], bu[1], w[:, 0, :], ALU.mult)
                dve.tensor_tensor(m_in[:, 3, :], bu[0], w[:, 1, :], ALU.mult).then_inc(in_done, 1)

            def scan(i):
                for c in range(2):
                    dve.wait_ge(in_added, 2 * i + c + 1)
                    dve.tensor_tensor_scan(z[:, i % 2, c, :], k.mag[:, i:i + 1].to_broadcast((P, T)),
                                           z[:, i % 2, c, :], 0.0, ALU.mult, ALU.add).then_inc(scanned, 1)

            def rotate_out(i):
                w = tables[:, i % 2]
                dve.wait_ge(scanned, 2 * i + 2)
                if i >= 1:
                    dve.wait_ge(out_added, 2 * i)
                zz = z[:, i % 2]
                dve.tensor_tensor(m_out[:, 0, :], zz[:, 0, :], w[:, 0, :], ALU.mult)
                dve.tensor_tensor(m_out[:, 1, :], zz[:, 1, :], w[:, 1, :], ALU.mult)
                dve.tensor_tensor(m_out[:, 2, :], zz[:, 1, :], w[:, 0, :], ALU.mult)
                dve.tensor_tensor(m_out[:, 3, :], zz[:, 0, :], w[:, 1, :], ALU.mult).then_inc(out_done, 1)

            def skip(j):
                dve.wait_ge(y_made, SPU * (j + 1))
                dve.scalar_tensor_tensor(u[:, j, :], u[:, j, :], k.col("ssm_d", j),
                                         k.ps[:, y_banks(j):y_banks(j) + 2, :].rearrange("p b n -> p (b n)"),
                                         ALU.mult, ALU.add).then_inc(y_sum, 1)

            for l in range(L):
                table_level(0, l)
            rotate_in(0)
            for i in range(N):
                scan(i)
                rotate_out(i)
                if i + 1 < N:
                    for l in range(L):
                        table_level(i + 1, l)
                    rotate_in(i + 1)
                if i >= SPU and i % SPU == 1:
                    skip(i // SPU - 1)
            skip(U_TILES - 1)

        @block.gpsimd
        def _(pool):
            for i in range(N):
                if i >= 2:
                    pool.wait_ge(out_done, i - 1)
                pool.wait_ge(in_done, 2 * i + 1)
                pool.tensor_tensor(z[:, i % 2, 0, :], m_in[:, 0, :], m_in[:, 1, :], ALU.add).then_inc(in_added, 1)
                pool.wait_ge(in_done, 2 * i + 2)
                pool.tensor_tensor(z[:, i % 2, 1, :], m_in[:, 2, :], m_in[:, 3, :], ALU.subtract).then_inc(in_added, 1)
                pool.wait_ge(out_done, i + 1)
                if i >= 2:
                    pool.wait_ge(y_made, i - 1)
                pool.tensor_tensor(st[:, i % 2, 0, :], m_out[:, 0, :], m_out[:, 1, :], ALU.subtract).then_inc(out_added, 1)
                pool.tensor_tensor(st[:, i % 2, 1, :], m_out[:, 2, :], m_out[:, 3, :], ALU.add).then_inc(out_added, 1)


A_WG = A_K


def stage_glu(k):
    nc, ins = k.nc, k.ins
    z = k.ar(A_U, U_TILES, T)
    w, gate = k.ar(A_WG, U_TILES, D_SSM), k.ar(A_WG + U_TILES * D_SSM, U_TILES, T)
    loaded, made, gated = map(k.sem, ("loaded", "made", "gated"))
    with nc.Block() as block:
        @block.sync
        def _(sp):
            sp.dma_start(w, ins["w_glu"].rearrange("o (k p) n -> p (o k) n", p=P)).then_inc(loaded, 16)

        @block.tensor
        def _(pe):
            pe.wait_ge(loaded, 16)
            linear_units(k, pe, U_TILES, lambda n, kt: w[:, kt, n * P:(n + 1) * P],
                         lambda kt, half: z[:, kt, half * HALF:(half + 1) * HALF], U_TILES, made, None)

        @block.scalar
        def _(act):
            for n in range(U_TILES):
                act.wait_ge(made, n + 1)
                act.activation(gate[:, n, :], pair(k, n), ACT.Sigmoid, bias=k.col("b_glu", n)).then_inc(gated, 1)

        @block.vector
        def _(dve):
            dve.wait_ge(made, U_TILES)
            for n in range(U_TILES):
                dve.wait_ge(gated, n + 1)
                dve.tensor_tensor(z[:, n, :], z[:, n, :], gate[:, n, :], ALU.mult)


def stage_mixer_norms(k):
    stage_norm(k, None, lambda t: k.ar(A_U, U_TILES, T)[:, t, :], lambda t: k.hT[:, t, 0:T], U_TILES, D_SSM,
               shift=None, weight=lambda t: k.col("out_norm_ssm", t), scale=None, tmp_at=A_K)
    stage_norm(k, None, lambda t: k.ar(A_Q, A_TILES, T)[:, t, :], lambda t: k.hT[:, U_TILES + t, 0:T], A_TILES, D_ATTN,
               shift=None, weight=lambda t: k.col("out_norm_attn", t), scale=None, tmp_at=A_K)


def stage_out_projection(k, name, gate, residual_scale=None, src_at=None):
    nc, ins = k.nc, k.ins
    w = k.ar(A_K, KD, D)
    mixed = k.hT if src_at is None else k.ar(src_at, KD, T)
    src = ins[name].rearrange("o (k p) n -> p (o k) n", p=P)
    made, read, v_ord = map(k.sem, ("made", "read", "v_ord"))
    loaded = [k.sem(f"loaded{g}") for g in range(4)]
    with nc.Block() as block:
        @block.sync
        def _(sp):
            for g in range(4):
                sp.dma_start(w[:, :, g * 256:(g + 1) * 256], src[:, :, g * 256:(g + 1) * 256]).then_inc(loaded[g], 16)

        @block.tensor
        def _(pe):
            linear_units(k, pe, KD, lambda n, kt: w[:, kt, n * P:(n + 1) * P],
                         lambda kt, half: mixed[:, kt, half * HALF:(half + 1) * HALF], KD, made, read,
                         before=lambda n: pe.wait_ge(loaded[n // 2], 16))

        @block.vector
        def _(dve):
            link = chained(dve, v_ord)
            for n in range(KD):
                x = k.xT[:, n, :]
                if residual_scale is not None:
                    link(dve.tensor_scalar(x, x, residual_scale, None, ALU.mult))
                dve.wait_ge(made, n + 1)
                dve.scalar_tensor_tensor(x, pair(k, n), gate(n), x, ALU.mult, ALU.add).then_inc(read, 1)


def stage_out1(k):
    stage_out_projection(k, "w_out", lambda n: k.mod1[:, 2, n:n + 1])


F_G = 0
F_W = F_G + FT * T
F_C = F_W + 4 * KD * P


def ffn_up(k, w_name, n_taps, convolve, finish, h_at):
    nc, ins = k.nc, k.ins
    g, w, conv = k.ar(F_G, FT, T), k.ar(F_W, 4, KD, P), k.ar(F_C, 4, T)
    src = ins[w_name].rearrange("o (k p) (s j n) -> j s p (o k) n", p=P, s=2, n=P)
    loaded, made, centre, conved, acted, done = (
        [k.sem(f"{name}{b}") for b in range(2)] for name in ("loaded", "made", "centre", "conved", "acted", "done"))
    v_ord = k.sem("v_ord")

    def ps(b, s):
        bank = 4 * b + 2 * s
        return k.ps[:, bank:bank + 2, :].rearrange("p b n -> p (b n)")

    with nc.Block() as block:
        @block.sync
        def _(sp):
            with sp.Fori(0, FT // 2) as i:
                for b in range(2):
                    sp.wait_ge(made[b], i + 1)
                    for s in range(2):
                        sp.dma_start(w[:, 2 * b + s], src[2 * i + b, s]).then_inc(loaded[b], 16)

        @block.tensor
        def _(pe):
            pe.sem_inc(made[0], 1)
            pe.sem_inc(made[1], 1)
            with pe.Fori(0, FT // 2) as i:
                for b in range(2):
                    pe.wait_ge(loaded[b], i * 32 + 32)
                    pe.wait_ge(done[b], i + 1)
                    for s in range(2):
                        for half in range(2):
                            for kt in range(KD):
                                last = pe.matmul(k.ps[:, 4 * b + 2 * s + half, :], w[:, 2 * b + s, kt, :],
                                                 k.hT[:, kt, h_at + half * HALF:h_at + (half + 1) * HALF],
                                                 start=kt == 0, stop=kt == KD - 1)
                    last.then_inc(made[b], 1)

        @block.scalar
        def _(act):
            with act.Fori(0, FT // 2) as i:
                for b in range(2):
                    act.wait_ge(made[b], i + 2)
                    act.wait_ge(done[b], i + 1)
                    convolve(k, "scalar", act, 2 * i + b, [conv[:, 2 * b + s, :] for s in range(2)],
                             [ps(b, s) for s in range(2)], centre[b])
                    act.wait_ge(conved[b], i + 1)
                    finish(k, "scalar", act, [conv[:, 2 * b + s, :] for s in range(2)], None, None, acted[b])

        @block.vector
        def _(dve):
            dve.sem_inc(done[0], 1)
            dve.sem_inc(done[1], 1)
            with dve.Fori(0, FT // 2) as i:
                for b in range(2):
                    dve.wait_ge(centre[b], i + 1)
                    c = [conv[:, 2 * b + s, :] for s in range(2)]
                    p = [ps(b, s) for s in range(2)]
                    convolve(k, "vector", dve, 2 * i + b, c, p, (v_ord, i * (2 * n_taps) + b * n_taps, conved[b]))
                    dve.wait_ge(acted[b], i + 1)
                    finish(k, "vector", dve, c, p, g[:, 2 * i + b, :], done[b])


def ffn_down(k, w_name, gate, residual_scale):
    nc, ins = k.nc, k.ins
    g = k.ar(F_G, FT, T)
    w = views_hT(k)(0, 2, FT, P)
    src = ins[w_name].rearrange("o (k p) (m n) -> m p (o k) n", p=P, n=P)
    loaded, made, done, scaled = ([k.sem(f"{name}{b}") for b in range(2)] for name in ("loaded", "made", "done", "scaled"))
    with nc.Block() as block:
        @block.sync
        def _(sp):
            with sp.Fori(0, KD // 2) as i:
                for b in range(2):
                    sp.wait_ge(made[b], i + 1)
                    sp.dma_start(w[:, b], src[2 * i + b]).then_inc(loaded[b], 16)

        @block.tensor
        def _(pe):
            pe.sem_inc(made[0], 1)
            pe.sem_inc(made[1], 1)
            with pe.Fori(0, KD // 2) as i:
                for b in range(2):
                    pe.wait_ge(loaded[b], i * 16 + 16)
                    pe.wait_ge(done[b], i + 1)
                    for half in range(2):
                        for kt in range(FT):
                            last = pe.matmul(k.ps[:, 2 * b + half, :], w[:, b, kt, :],
                                             g[:, kt, half * HALF:(half + 1) * HALF], start=kt == 0, stop=kt == FT - 1)
                    last.then_inc(made[b], 1)

        @block.vector
        def _(dve):
            dve.sem_inc(done[0], 1)
            dve.sem_inc(done[1], 1)
            with dve.Fori(0, KD // 2) as i:
                for b in range(2):
                    x = k.xT[:, 2 * i + b, :]
                    if residual_scale is not None:
                        dve.tensor_scalar(x, x, residual_scale, None, ALU.mult).then_inc(scaled[b], 1)
                        dve.wait_ge(scaled[b], i + 1)
                    dve.wait_ge(made[b], i + 2)
                    dve.scalar_tensor_tensor(x, pair(k, b), gate(2 * i + b), x, ALU.mult, ALU.add).then_inc(done[b], 1)


def conv_causal(k, engine, eng, j, c, p, sems):
    w = k.col("conv_w", 0, 6 * FT).rearrange("p (t s j) -> p t s j", t=3, s=2)
    bias = k.col("conv_b", 0, 2 * FT).rearrange("p (s j) -> p s j", s=2)
    if engine == "scalar":
        for s in range(2):
            last = eng.activation(c[s], p[s], ACT.Identity, bias=bias[:, s, bass.ds(j, 1)], scale=w[:, 2, s, bass.ds(j, 1)])
        last.then_inc(sems, 1)
        return
    v_ord, base, conved = sems
    n = 0
    for tap in (1, 0):
        lag = 2 - tap
        for s in range(2):
            if tap == 0:
                eng.wait_ge(v_ord, base + s + 1)
            last = eng.scalar_tensor_tensor(c[s][:, lag:T], p[s][:, 0:T - lag], w[:, tap, s, bass.ds(j, 1)],
                                            c[s][:, lag:T], ALU.mult, ALU.add)
            n += 1
            last.then_inc(v_ord, 1)
    eng.wait_ge(v_ord, base + n)
    eng.sem_inc(conved, 1)


def finish_silu(k, engine, eng, c, p, g, sem):
    if engine == "scalar":
        eng.activation(c[1], c[1], ACT.Silu).then_inc(sem, 1)
    else:
        eng.tensor_tensor(g, c[0], c[1], ALU.mult).then_inc(sem, 1)


def conv_grid(k, engine, eng, j, c, p, sems):
    w = k.col("ffn_conv_w_2", 0, 9 * FT).rearrange("p (t j) -> p t j", t=9)
    if engine == "scalar":
        eng.activation(c[0], p[0], ACT.Identity, bias=k.col("ffn_conv_b_2", 0, FT)[:, bass.ds(j, 1)],
                       scale=w[:, 4, bass.ds(j, 1)]).then_inc(sems, 1)
        return
    v_ord, base, conved = sems
    out = c[0].rearrange("p (r c) -> p r c", c=GRID_W)
    src = p[0].rearrange("p (r c) -> p r c", c=GRID_W)
    n = 0
    for di in (-1, 0, 1):
        for dj in (-1, 0, 1):
            if di == dj == 0:
                continue
            r0, r1 = max(0, -di), GRID_H - max(0, di)
            c0, c1 = max(0, -dj), GRID_W - max(0, dj)
            to = out[:, r0:r1, c0:c1]
            eng.scalar_tensor_tensor(to, src[:, r0 + di:r1 + di, c0 + dj:c1 + dj],
                                     w[:, 3 * (di + 1) + dj + 1, bass.ds(j, 1)], to, ALU.mult, ALU.add).then_inc(v_ord, 1)
            n += 1
            eng.wait_ge(v_ord, base + n)
    eng.sem_inc(conved, 1)


def finish_gelu(k, engine, eng, c, p, g, sem):
    if engine == "scalar":
        eng.activation(c[0], c[0], ACT.Gelu).then_inc(sem, 1)
    else:
        eng.tensor_tensor(g, c[0], p[1], ALU.mult).then_inc(sem, 1)


def stage_norm2(k):
    stage_norm(k, 0, lambda t: k.xT[:, t, :], lambda t: k.hT[:, t, CTX:TT], KD, D,
               shift=lambda t: k.mod1[:, 3, t:t + 1], weight=lambda t: k.gain[:, 0, t:t + 1],
               scale=(k.mod1[:, 4, :], k.col("norm2_w", 0, KD)))


def stage_up1(k):
    ffn_up(k, "w_up", 4, conv_causal, finish_silu, CTX)


def stage_down1(k):
    ffn_down(k, "w_down", lambda j: k.mod1[:, 5, bass.ds(j, 1)], None)


B_MIX = 0
B_FREE = KD * T
LN_TINY = math.log(TINY)


def stage_context(k):
    nc, ins = k.nc, k.ins
    rows = k.ar(0, CCH, D)
    loaded, turned, ones_set, masked, v_ord, exped, subtracted = map(
        k.sem, ("loaded", "turned", "ones_set", "masked", "v_ord", "exped", "subtracted"))
    p_exp = k.ar(CCH * D, 2 * HG_HEADS)
    p_sum = k.ar(CCH * D + 8, 2 * HG_HEADS)
    with nc.Block() as block:
        @block.sync
        def _(sp):
            sp.dma_start(rows, ins["ctx_2"].rearrange("o (t p) d -> p (o t) d", p=P)).then_inc(loaded, 16)

        @block.tensor
        def _(pe):
            pe.wait_ge(loaded, 16)
            for f in range(KD):
                for t in range(CCH):
                    last = pe.transpose(k.ps[:, f // 2, (f % 2) * CTX + t * P:(f % 2) * CTX + (t + 1) * P],
                                        rows[:, t, f * P:(f + 1) * P], k.ident[:, :])
            last.then_inc(turned, 1)

        @block.scalar
        def _(act):
            act.wait_ge(subtracted, 1)
            act.activation(p_exp, p_exp, ACT.Exp).then_inc(exped, 1)

        @block.vector
        def _(dve):
            link = chained(dve, v_ord)
            lb = k.col("hg_lb_2", 0, 2 * HG_HEADS)
            dve.tensor_tensor(p_exp, lb, lb, ALU.subtract).then_inc(subtracted, 1)
            dve.wait_ge(exped, 1)
            link(dve.reciprocal(p_sum, p_exp))
            link(dve.tensor_tensor(p_exp, p_exp, p_sum, ALU.mult))
            link(dve.tensor_tensor(k.lower[:, :], p_exp, p_exp, ALU.subtract))
            link(dve.tensor_scalar(k.one_less[:, :], k.lower[:, :], -1.0, 1.0, ALU.mult, ALU.add))
            dve.wait_ge(turned, 1)
            for f in range(0, KD, 2):
                dve.tensor_copy(k.hT[:, f:f + 2, 0:CTX],
                                k.ps[:, f // 2, :].rearrange("p (a b) -> p a b", a=2))

        @block.gpsimd
        def _(pool):
            pool.memset(k.masks[:, :, :, :], 0.0).then_inc(ones_set, 1)
            pool.wait_ge(ones_set, 1)
            n = 0
            for l, m in enumerate(LEVELS):
                for d in range(2):
                    quarter = k.masks[:, d, l, :].rearrange("p (b h r) -> p b h r", h=2, r=m)[:, :, 1 - d, :]
                    pool.memset(quarter, 1.0).then_inc(masked, 1)
                    n += 1
                    pool.wait_ge(masked, n)
                    for base, sign in ((-m * d, 1), (m * d + m - 1, -1)):
                        pool.affine_select(out=quarter, in_=quarter, compare_op=ALU.is_ge, fill=0.0, base=base,
                                           pattern=[[-2 * m * sign, P // (2 * m)], [0, m]],
                                           channel_multiplier=sign).then_inc(masked, 1)
                        n += 1
                        pool.wait_ge(masked, n)


def stage_modulate2(k):
    for c, (a, b) in enumerate(((CTX, TT), (0, CTX))):
        stage_norm(k, 0, (lambda t: k.xT[:, t, :]) if c == 0 else (lambda t: k.hT[:, t, 0:CTX]),
                   lambda t, a=a, b=b: k.hT[:, t, a:b], KD, D,
                   shift=lambda t, c=c: k.mod2[:, 0, t, c:c + 1], weight=lambda t: k.gain[:, 0, t:t + 1],
                   scale=(k.mod2[:, 1, :, c], None), centre=True, tokens=b - a, tmp_at=B_FREE)


def stage_short_conv(k):
    nc, ins = k.nc, k.ins
    n_t = SC_WIDTH // P
    w = k.ar(B_FREE, KD, 3 * SC_WIDTH)
    gate_c, x, y = (k.ar(B_FREE + KD * 3 * SC_WIDTH + i * n_t * T, n_t, T) for i in range(3))
    mix = k.ar(B_MIX, KD, T)
    loaded, made, copied, used, x_ready, centre, v_ord = map(
        k.sem, ("loaded", "made", "copied", "used", "x_ready", "centre", "v_ord"))
    parts = [(part, t) for t in range(n_t) for part in (1, 2, 0)]
    with nc.Block() as block:
        @block.sync
        def _(sp):
            sp.dma_start(w, ins["w_in_2"].rearrange("o (k p) n -> p (o k) n", p=P)[:, :, O_SC:O_SG]).then_inc(loaded, 16)

        @block.tensor
        def _(pe):
            pe.wait_ge(loaded, 16)
            for n, (part, t) in enumerate(parts):
                if n >= 4:
                    pe.wait_ge(copied, 1)
                    pe.wait_ge(used, n - 4)
                c = part * SC_WIDTH + t * P
                for half in range(2):
                    for kt in range(KD):
                        last = pe.matmul(k.ps[:, 2 * (n % 4) + half, :], w[:, kt, c:c + P],
                                         k.hT[:, kt, CTX + half * HALF:CTX + (half + 1) * HALF],
                                         start=kt == 0, stop=kt == KD - 1)
                last.then_inc(made, 1)

        @block.scalar
        def _(act):
            for t in range(n_t):
                act.wait_ge(made, 3 * t + 1)
                act.activation(gate_c[:, t, :], pair(k, 3 * t), ACT.Copy).then_inc(copied, 1)
                act.wait_ge(x_ready, t + 1)
                act.activation(y[:, t, :], x[:, t, :], ACT.Copy, scale=k.col("sc_conv_w_2", n_t + t)).then_inc(centre, 1)

        @block.vector
        def _(dve):
            link = chained(dve, v_ord)
            for t in range(n_t):
                dve.wait_ge(copied, t + 1)
                dve.wait_ge(made, 3 * t + 2)
                ins_ = dve.tensor_tensor(x[:, t, :], pair(k, 3 * t + 1), gate_c[:, t, :], ALU.mult)
                ins_.then_inc(x_ready, 1)
                dve.wait_ge(centre, t + 1)
                dve.sem_inc(used, 1)
                link(dve.scalar_tensor_tensor(y[:, t, 1:T], x[:, t, 0:T - 1], k.col("sc_conv_w_2", t),
                                              y[:, t, 1:T], ALU.mult, ALU.add))
                link(dve.scalar_tensor_tensor(y[:, t, 0:T - 1], x[:, t, 1:T], k.col("sc_conv_w_2", 2 * n_t + t),
                                              y[:, t, 0:T - 1], ALU.mult, ALU.add))
                dve.wait_ge(made, 3 * t + 3)
                dve.tensor_tensor(mix[:, HG_HEADS + t, :], pair(k, 3 * t + 2), y[:, t, :], ALU.mult).then_inc(used, 1)


def stage_spatial_gate(k):
    nc, ins = k.nc, k.ins
    n_t, nb = SG_WIDTH // P, T // P
    at = B_FREE
    w = k.ar(at, KD, 2 * SG_WIDTH); at += KD * 2 * SG_WIDTH
    u = k.ar(at, n_t, T); at += n_t * T
    v = k.ar(at, nb, SG_WIDTH); at += nb * SG_WIDTH
    sq = k.ar(at, nb, SG_WIDTH); at += nb * SG_WIDTH
    ws = k.ar(at, SG_HEADS, P); at += SG_HEADS * P
    ws_t = k.ar(at, SG_HEADS, P); at += SG_HEADS * P
    gb = k.ar(at, 2, SG_WIDTH); at += 2 * SG_WIDTH
    rows = k.ar(at, 2 * SG_WIDTH + SG_HEADS * P); at += 2 * SG_WIDTH + SG_HEADS * P
    stats = k.ar(at, 2, nb * SG_HEADS); at += 2 * nb * SG_HEADS
    mix = k.ar(B_MIX, KD, T)
    loaded, made, v_made, prep, copied, normed, mixed, v_ord, rooted, to_root = map(
        k.sem, ("loaded", "made", "v_made", "prep", "copied", "normed", "mixed", "v_ord", "rooted", "to_root"))
    with nc.Block() as block:
        @block.sync
        def _(sp):
            sp.dma_start(w, ins["w_in_2"].rearrange("o (k p) n -> p (o k) n", p=P)[:, :, O_SG:IN2]).then_inc(loaded, 16)
            sp.dma_start(ws, ins["sg_w_2"].rearrange("o g t s -> t (o g) s")).then_inc(loaded, 16)
            sp.dma_start(rows[0:1, 0:SG_WIDTH], ins["sg_ln_g_2"]).then_inc(loaded, 16)
            sp.dma_start(rows[0:1, SG_WIDTH:2 * SG_WIDTH], ins["sg_ln_b_2"]).then_inc(loaded, 16)
            sp.dma_start(rows[0:1, 2 * SG_WIDTH:], ins["sg_b_2"].rearrange("o g t -> o (g t)")).then_inc(loaded, 16)

        @block.tensor
        def _(pe):
            pe.wait_ge(loaded, 5 * 16)
            for b in range(nb):
                for kt in range(KD):
                    last = pe.matmul(k.ps[:, b // 2, (b % 2) * SG_WIDTH:(b % 2 + 1) * SG_WIDTH],
                                     k.hT[:, kt, CTX + b * P:CTX + (b + 1) * P], w[:, kt, SG_WIDTH:2 * SG_WIDTH],
                                     start=kt == 0, stop=kt == KD - 1)
            last.then_inc(v_made, 1)
            for g in range(SG_HEADS):
                last = pe.transpose(k.ps[:, 4, g * P:(g + 1) * P], ws[:, g, :], k.ident[:, :])
            last.then_inc(prep, 1)
            pe.matmul(k.ps[:, 5, :], k.ones[0:1, :], rows[0:1, 0:2 * SG_WIDTH], start=True, stop=True).then_inc(prep, 1)
            pe.wait_ge(copied, 6)
            for t in range(n_t):
                for half in range(2):
                    for kt in range(KD):
                        last = pe.matmul(k.ps[:, 2 * t + half, :], w[:, kt, t * P:(t + 1) * P],
                                         k.hT[:, kt, CTX + half * HALF:CTX + (half + 1) * HALF],
                                         start=kt == 0, stop=kt == KD - 1)
                last.then_inc(made, 1)
            pe.wait_ge(normed, 1)
            for g in range(SG_HEADS):
                t, r = divmod(g, 2)
                out_rows = slice(64 * r, 64 * r + 64)
                for half in range(2):
                    bank = 4 + 2 * t + half
                    b_row = rows[0:1, 2 * SG_WIDTH + g * P:2 * SG_WIDTH + (g + 1) * P]
                    for i in range(4):
                        cols = slice(i * P, (i + 1) * P)
                        pe.matmul(k.ps[out_rows, bank, cols], k.ones[0:1, 0:SG_HD], b_row, start=True, stop=False,
                                  skip_group_check=True)
                        last = pe.matmul(k.ps[out_rows, bank, cols],
                                         v[:, 4 * half + i, g * SG_HD:(g + 1) * SG_HD], ws_t[:, g, :],
                                         start=False, stop=True, skip_group_check=True)
            last.then_inc(mixed, 1)

        @block.scalar
        def _(act):
            act.wait_ge(v_made, 1)
            for b in range(4):
                act.activation(v[:, 2 * b:2 * b + 2, :].rearrange("p a b -> p (a b)"), k.ps[:, b, :], ACT.Copy).then_inc(copied, 1)
            act.wait_ge(prep, 1)
            act.activation(ws_t.rearrange("p a b -> p (a b)"), k.ps[:, 4, :], ACT.Copy).then_inc(copied, 1)
            act.wait_ge(prep, 2)
            act.activation(gb.rearrange("p a b -> p (a b)"), k.ps[:, 5, :], ACT.Copy).then_inc(copied, 1)
            for t in range(n_t):
                act.wait_ge(made, t + 1)
                act.activation(u[:, t, :], pair(k, t), ACT.Copy).then_inc(copied, 1)
            act.wait_ge(to_root, 1)
            act.activation(stats[:, 1, :], stats[:, 1, :], ACT.Sqrt).then_inc(rooted, 1)

        @block.vector
        def _(dve):
            link = chained(dve, v_ord)
            dve.wait_ge(copied, 6)
            vg = v.rearrange("p b (g c) -> p (b g) c", c=SG_HD)
            sg = sq.rearrange("p b (g c) -> p (b g) c", c=SG_HD)
            mean, var = (stats[:, i, :].unsqueeze(2).to_broadcast((P, nb * SG_HEADS, SG_HD)) for i in range(2))
            link(dve.tensor_reduce(stats[:, 0, :], vg, AX.X, ALU.add))
            link(dve.tensor_scalar(stats[:, 0, :], stats[:, 0, :], 1.0 / SG_HD, None, ALU.mult))
            link(dve.tensor_tensor(vg, vg, mean, ALU.subtract))
            link(dve.tensor_tensor(sg, vg, vg, ALU.mult))
            link(dve.tensor_reduce(stats[:, 1, :], sg, AX.X, ALU.add))
            dve.tensor_scalar(stats[:, 1, :], stats[:, 1, :], 1.0 / SG_HD, EPS, ALU.mult, ALU.add).then_inc(to_root, 1)
            dve.wait_ge(rooted, 1)
            link(dve.reciprocal(stats[:, 1, :], stats[:, 1, :]))
            link(dve.tensor_tensor(vg, vg, var, ALU.mult))
            for i, op in enumerate((ALU.mult, ALU.add)):
                link(dve.tensor_tensor(v, v, gb[:, i:i + 1, :].to_broadcast((P, nb, SG_WIDTH)), op))
            dve.sem_inc(normed, 1)
            dve.wait_ge(mixed, 1)
            for t in range(n_t):
                dve.wait_ge(copied, 7 + t)
                dve.tensor_tensor(mix[:, HG_HEADS + 2 + t, :],
                                  k.ps[:, 4 + 2 * t:6 + 2 * t, :].rearrange("p b n -> p (b n)"), u[:, t, :], ALU.mult)


HEAD_JOBS = ["q", "g", "v0", "v1"] + \
            [f"{name}{d}" for d in range(2) for name in
             ["za", "zb", "kta", "ktb", "kva", "kvb", "lev7_"] + [f"lev{l}_" for l in range(len(LEVELS))]] + ["ss"]


def stage_hgrn(k):
    nc, ins = k.nc, k.ins
    at = [B_FREE]

    def take(*shape):
        v = k.ar(at[0], *shape)
        at[0] += int(np.prod(shape))
        return v

    w = take(5, KD, P)
    vals = take(NCH, P)
    q, gate = take(T), take(T)
    z, l1 = take(TT), take(TT)
    keys, b = take(TT), take(TT)
    x = take(2, T)
    att = take(T)
    qh, kh = take(T), take(NCH, P)
    kh_t = take(NCH, P)
    states = take(T // CHUNK, P)
    state0 = take(2, P)
    chunk_decay = take(NCH)
    starts = k.chunk_starts[:, :]
    mix = k.ar(B_MIX, KD, T)
    src = ins["w_in_2"][:, :, 0:5 * HG_WIDTH].rearrange("o (k p) (s j n) -> j s p (o k) n", p=P, s=5, n=P)
    names = ("loaded", "silu_done", "q_scaled", "v_done", "z_copied", "l_ready", "sp_ready", "k_raw", "lt_ready", "k_ready",
             "b_ready", "kh_sub", "kh_exp", "kh_ready", "kt_done", "kv_done", "g_exp", "qh_exp", "qh_ready", "zeroed",
             "sub_done", "exp_done", "x_ready", "selected", "o_made", "sq_done", "stat", "root", "a_ord", "v_ord",
             "states_ready")
    S = {n: k.sem(n) for n in names}
    made = [k.sem(f"made{i}") for i in range(3)]
    read = [k.sem(f"read{i}") for i in range(3)]
    o_ps = k.ps[:, 6:8, :].rearrange("p b n -> p (b n)")
    mask_u = k.masks[:, :, :, :].bitcast(U32)
    ident_u = k.ident[:, :].bitcast(U32)
    NL = len(LEVELS)

    def slot(job):
        n = HEAD_JOBS.index(job)
        return n % 3, n // 3

    def banks(job):
        s, _ = slot(job)
        return k.ps[:, 2 * s:2 * s + 2, :].rearrange("p b n -> p (b n)")

    def wait_free(pe, job):
        s, use = slot(job)
        if use >= 1:
            pe.wait_ge(read[s], use)

    def wait_made(eng, job):
        s, use = slot(job)
        eng.wait_ge(made[s], use + 1)

    def x_tokens(t):
        return t[:, CTX:TT]

    def halves_of(v, m):
        r = v.rearrange("p (b h r) -> p b h r", h=2, r=m)
        return r[:, :, 0, :], r[:, :, 1, :]

    with nc.Fori(0, HG_HEADS) as h:
        with nc.Block() as block:
            @block.sync
            def _(sp):
                for s in range(5):
                    sp.dma_start(w[:, s], src[h, s]).then_inc(S["loaded"], 16)
                sp.wait_ge(S["loaded"], 5 * 16)

            @block.tensor
            def _(pe):
                def feature_job(job, s, first, last_col):
                    wait_free(pe, job)
                    out, n = banks(job), last_col - first
                    for a in range(0, n, HALF):
                        e = min(a + HALF, n)
                        for kt in range(KD):
                            last = pe.matmul(out[:, a:e], w[:, s, kt, :], k.hT[:, kt, first + a:first + e],
                                             start=kt == 0, stop=kt == KD - 1)
                    last.then_inc(made[slot(job)[0]], 1)

                def value_job(job, chunks):
                    wait_free(pe, job)
                    for i, c in enumerate(chunks):
                        for kt in range(KD):
                            last = pe.matmul(banks(job)[:, i * P:(i + 1) * P], k.hT[:, kt, c * P:(c + 1) * P],
                                             w[:, 0, kt, :], start=kt == 0, stop=kt == KD - 1)
                    last.then_inc(made[slot(job)[0]], 1)

                def chunk_job(job, chunks, fn):
                    wait_free(pe, job)
                    for i, c in enumerate(chunks):
                        last = fn(banks(job)[:, i * P:(i + 1) * P], c)
                    last.then_inc(made[slot(job)[0]], 1)

                pe.wait_ge(S["loaded"], 5 * 16)
                feature_job("q", 3, CTX, TT)
                feature_job("g", 4, CTX, TT)
                value_job("v0", range(8))
                value_job("v1", range(8, NCH))
                for d in range(2):
                    if d == 0:
                        feature_job("za0", 1, 0, T)
                        feature_job("zb0", 1, T, TT)
                    pe.wait_ge(S["kh_ready"], d + 1)
                    for job, chunks in ((f"kta{d}", range(8)), (f"ktb{d}", range(8, NCH))):
                        chunk_job(job, chunks, lambda out, c: pe.transpose(out, kh[:, c, :], k.ident[:, :]))
                    pe.wait_ge(S["kt_done"], 2 * d + 2)
                    pe.wait_ge(S["v_done"], 2)
                    for job, chunks in ((f"kva{d}", range(8)), (f"kvb{d}", range(8, NCH))):
                        chunk_job(job, chunks, lambda out, c: pe.matmul(out, kh_t[:, c, :], vals[:, c, :],
                                                                        start=True, stop=True))
                    pe.wait_ge(S["k_ready"], d + 1)
                    pe.wait_ge(S["q_scaled"], 1)
                    chunk_job(f"lev7_{d}", range(T // P), lambda out, c: pe.matmul(
                        out, keys[:, CTX + c * P:CTX + (c + 1) * P], q[:, c * P:(c + 1) * P], start=True, stop=True))
                    for l in range(NL):
                        pe.wait_ge(S["x_ready"], d * NL + l + 1)
                        chunk_job(f"lev{l}_{d}", range(T // P), lambda out, c: pe.matmul(
                            out, x[:, l % 2, c * P:(c + 1) * P], x[:, l % 2, c * P:(c + 1) * P], start=True, stop=True))
                    if d == 0:
                        feature_job("za1", 2, 0, T)
                        feature_job("zb1", 2, T, TT)
                    pe.wait_ge(S["states_ready"], d + 1)
                    pe.wait_ge(S["qh_ready"], d + 1)
                    for c in range(T // P):
                        pe.matmul(o_ps[:, c * P:(c + 1) * P], states[:, c, :], qh[:, c * P:(c + 1) * P],
                                  start=d == 0 and c % 4 == 0, stop=False, skip_group_check=True)
                    pe.wait_ge(S["selected"], d + 1)
                    for c in range(T // P):
                        last = pe.matmul(o_ps[:, c * P:(c + 1) * P], vals[:, CCH + c, :], att[:, c * P:(c + 1) * P],
                                         start=False, stop=d == 1, skip_group_check=True)
                    last.then_inc(S["o_made"], 1)
                pe.wait_ge(S["sq_done"], 1)
                wait_free(pe, "ss")
                for half in range(2):
                    last = pe.matmul(banks("ss")[:, half * HALF:(half + 1) * HALF], k.ones[:, :],
                                     x[:, 0, half * HALF:(half + 1) * HALF], start=True, stop=True)
                last.then_inc(made[slot("ss")[0]], 1)

            @block.scalar
            def _(act):
                link = chained(act, S["a_ord"])

                def take_out(job, dst, n, func, done):
                    wait_made(act, job)
                    s, _ = slot(job)
                    act.activation(dst, banks(job)[:, 0:n], func).then_inc(read[s], 1)
                    if done is not None:
                        act.wait_ge(read[s], slot(job)[1] + 1)
                        act.sem_inc(done, 1)

                take_out("q", q, T, ACT.Silu, S["silu_done"])
                take_out("g", gate, T, ACT.Silu, S["silu_done"])
                take_out("v0", vals[:, 0:8, :].rearrange("p a b -> p (a b)"), T, ACT.Copy, S["v_done"])
                take_out("v1", vals[:, 8:NCH, :].rearrange("p a b -> p (a b)"), 2 * P, ACT.Copy, S["v_done"])
                for d in range(2):
                    if d == 1:
                        act.wait_ge(S["b_ready"], 1)
                    take_out(f"za{d}", z[:, 0:T], T, ACT.Copy, S["z_copied"])
                    take_out(f"zb{d}", z[:, T:TT], TT - T, ACT.Copy, S["z_copied"])
                    link(act.activation(l1, z, ACT.Abs))
                    link(act.activation(l1, l1, ACT.Exp, scale=-1.0))
                    act.activation(l1, l1, ACT.Ln, bias=1.0).then_inc(S["l_ready"], 1)
                    act.wait_ge(S["sp_ready"], d + 1)
                    act.activation(keys, keys, ACT.Exp, scale=-1.0).then_inc(S["k_raw"], 1)
                    link(act.activation(z, z, ACT.Exp, scale=-1.0))
                    act.activation(z, z, ACT.Ln, bias=1.0,
                                   scale=k.lower[:, bass.ds(h + d * HG_HEADS, 1)]).then_inc(S["lt_ready"], 1)
                    act.wait_ge(S["kh_sub"], d + 1)
                    act.activation(kh.rearrange("p a b -> p (a b)"), kh.rearrange("p a b -> p (a b)"), ACT.Exp)\
                        .then_inc(S["kh_exp"], 1)
                    edge = b.rearrange("p (c r) -> p c r", r=CHUNK)[:, :, CHUNK - 1 if d == 0 else 0]
                    if d == 1:
                        act.wait_ge(S["states_ready"], 1)
                    act.activation(chunk_decay, edge, ACT.Exp).then_inc(S["g_exp"], 1)
                    if d == 1:
                        act.wait_ge(S["o_made"], 1)
                    act.activation(qh, x_tokens(b), ACT.Exp).then_inc(S["qh_exp"], 1)
                    for job, c0, c1 in ((f"kta{d}", 0, 8), (f"ktb{d}", 8, NCH)):
                        take_out(job, kh_t[:, c0:c1, :].rearrange("p a b -> p (a b)"), (c1 - c0) * P, ACT.Copy, S["kt_done"])
                    for l in range(NL):
                        act.wait_ge(S["sub_done"], d * NL + l + 1)
                        act.activation(x[:, l % 2, :], x[:, l % 2, :], ACT.Exp).then_inc(S["exp_done"], 1)
                act.wait_ge(S["o_made"], 2)
                act.activation(x[:, 0, :], o_ps, ACT.Square).then_inc(S["sq_done"], 1)
                act.wait_ge(S["stat"], 1)
                act.activation(x[:, 1, :], x[:, 1, :], ACT.Sqrt).then_inc(S["root"], 1)

            @block.gpsimd
            def _(pool):
                pool.memset(att, 0.0).then_inc(S["zeroed"], 1)
                pool.wait_ge(S["o_made"], 1)
                pool.memset(att, 0.0).then_inc(S["zeroed"], 1)

            @block.vector
            def _(dve):
                link = chained(dve, S["v_ord"])
                dve.wait_ge(S["silu_done"], 1)
                dve.tensor_scalar(q, q, HG_DK ** -0.5, None, ALU.mult).then_inc(S["q_scaled"], 1)
                dve.wait_ge(S["q_scaled"], 1)
                for d in range(2):
                    dve.wait_ge(S["l_ready"], d + 1)
                    if d == 1:
                        dve.wait_ge(S["g_exp"], 1)
                        dve.wait_ge(S["qh_exp"], 1)
                    link(dve.scalar_tensor_tensor(b, z, 0.0, l1, ALU.min, ALU.subtract))
                    link(dve.scalar_tensor_tensor(keys, z, 0.0, l1, ALU.max, ALU.add))
                    link(dve.tensor_scalar(z, z, -44.0, None, ALU.max))
                    dve.sem_inc(S["sp_ready"], 1)
                    dve.wait_ge(S["lt_ready"], d + 1)
                    link(dve.tensor_tensor(b, b, z, ALU.add))
                    link(dve.tensor_scalar(b, b, LN_TINY, 0.0, ALU.max, ALU.min))
                    if d == 0:
                        scan = dve.tensor_tensor_scan(b, starts[:, 0:TT], b, 0.0, ALU.mult, ALU.add)
                    else:
                        scan = dve.tensor_tensor_scan(b[:, ::-1], starts[:, 1:TT + 1][:, ::-1], b[:, ::-1], 0.0,
                                                      ALU.mult, ALU.add)
                    scan.then_inc(S["b_ready"], 1)
                    dve.wait_ge(S["k_raw"], d + 1)
                    dve.tensor_scalar(keys, keys, k.one_less[:, bass.ds(h + d * HG_HEADS, 1)], None, ALU.mult)\
                       .then_inc(S["k_ready"], 1)
                    dve.wait_ge(S["b_ready"], d + 1)
                    bc = b.rearrange("p (c r) -> p c r", r=CHUNK)
                    edge = bc[:, :, CHUNK - 1:CHUNK] if d == 0 else bc[:, :, 0:1]
                    if d == 1:
                        dve.wait_ge(S["kt_done"], 2)
                    dve.tensor_tensor(kh, edge.to_broadcast((P, NCH, CHUNK)), bc, ALU.subtract).then_inc(S["kh_sub"], 1)
                    dve.wait_ge(S["k_ready"], d + 1)
                    dve.wait_ge(S["kh_exp"], d + 1)
                    dve.tensor_tensor(kh, kh, keys.rearrange("p (c r) -> p c r", r=CHUNK), ALU.mult).then_inc(S["kh_ready"], 1)
                    dve.wait_ge(S["qh_exp"], d + 1)
                    dve.tensor_tensor(qh, qh, q, ALU.mult).then_inc(S["qh_ready"], 1)

                    def subtract(l):
                        m = LEVELS[l]
                        left, right = halves_of(x_tokens(b), m)
                        xl, xr = halves_of(x[:, l % 2, :], m)
                        if d == 0:
                            mid = left[:, :, m - 1:m].to_broadcast((P, T // (2 * m), m))
                            dve.tensor_tensor(xl, mid, left, ALU.subtract)
                            last = dve.tensor_tensor(xr, right, mid, ALU.subtract)
                        else:
                            mid = right[:, :, 0:1].to_broadcast((P, T // (2 * m), m))
                            dve.tensor_tensor(xl, left, mid, ALU.subtract)
                            last = dve.tensor_tensor(xr, mid, right, ALU.subtract)
                        last.then_inc(S["sub_done"], 1)

                    def weigh(l):
                        m = LEVELS[l]
                        dve.wait_ge(S["exp_done"], d * NL + l + 1)
                        sides = halves_of(x[:, l % 2, :], m)
                        k_side, q_side = d, 1 - d
                        dve.tensor_tensor(sides[k_side], sides[k_side], halves_of(x_tokens(keys), m)[k_side], ALU.mult)
                        dve.tensor_tensor(sides[q_side], sides[q_side], halves_of(q, m)[q_side], ALU.mult)\
                           .then_inc(S["x_ready"], 1)

                    def select(l):
                        job = f"lev{l}_{d}"
                        mask = (ident_u if l == NL else mask_u[:, d, l, :]).unsqueeze(1).to_broadcast((P, T // P, P))
                        wait_made(dve, job)
                        if l != NL:
                            s_, use = slot(f"lev{NL if l == 0 else l - 1}_{d}")
                            dve.wait_ge(read[s_], use + 1)
                        dve.copy_predicated(att.rearrange("p (c r) -> p c r", r=P), mask,
                                            banks(job).rearrange("p (c r) -> p c r", r=P)).then_inc(read[slot(job)[0]], 1)

                    subtract(0)
                    dve.wait_ge(S["g_exp"], d + 1)
                    for job in (f"kva{d}", f"kvb{d}"):
                        wait_made(dve, job)
                    kv = lambda c: banks(f"kva{d}" if c < 8 else f"kvb{d}")[:, (c % 8) * P:(c % 8 + 1) * P]
                    order = list(range(NCH)) if d == 0 else list(range(CCH - 1, -1, -1)) + list(range(NCH - 1, CCH - 1, -1))
                    if d == 1:
                        dve.wait_ge(S["o_made"], 1)
                    prev = None
                    for n, c in enumerate(order[:-1]):
                        to = order[n + 1]
                        dst = states[:, to - CCH, :] if to >= CCH else state0[:, 0, :]
                        if prev is None:
                            link(dve.tensor_copy(dst, kv(c)))
                        else:
                            link(dve.scalar_tensor_tensor(dst, prev, chunk_decay[:, c:c + 1], kv(c), ALU.mult, ALU.add))
                        prev = dst
                    dve.sem_inc(S["states_ready"], 1)
                    for job in (f"kva{d}", f"kvb{d}"):
                        dve.sem_inc(read[slot(job)[0]], 1)
                    dve.wait_ge(S["zeroed"], d + 1)
                    select(NL)
                    for l in range(NL):
                        if l + 1 < NL:
                            if l >= 1:
                                wait_made(dve, f"lev{l - 1}_{d}")
                            subtract(l + 1)
                        weigh(l)
                        if l >= 1:
                            select(l - 1)
                    select(NL - 1)
                    s_, use = slot(f"lev{NL - 1}_{d}")
                    dve.wait_ge(read[s_], use + 1)
                    dve.sem_inc(S["selected"], 1)
                wait_made(dve, "ss")
                dve.tensor_scalar(x[:, 1, :], banks("ss"), 1.0 / HG_DK, EPS, ALU.mult, ALU.add).then_inc(S["stat"], 1)
                dve.wait_ge(S["root"], 1)
                link(dve.reciprocal(x[:, 1, :], x[:, 1, :]))
                link(dve.tensor_tensor(x[:, 1, :], o_ps, x[:, 1, :], ALU.mult))
                dve.wait_ge(S["silu_done"], 2)
                dve.scalar_tensor_tensor(mix[:, h, :], x[:, 1, :], k.col("hg_norm_g_2"), gate, ALU.mult, ALU.mult)

        with nc.Block() as block:
            @block.sync
            def _(sp):
                for s in list(S.values()) + made + read:
                    sp.sem_clear(s)


def stage_starts(k):
    set_ = k.sem("starts_set")
    with k.nc.Block() as block:
        @block.gpsimd
        def _(pool):
            pool.memset(k.chunk_starts[:, :], 1.0).then_inc(set_, 1)
            pool.wait_ge(set_, 1)
            pool.memset(k.chunk_starts[:, 0:TT + 1:CHUNK], 0.0).then_inc(set_, 1)


def stage_mix_norm2(k):
    pass


def stage_out2(k):
    stage_out_projection(k, "w_out_2", lambda n: k.mod2[:, 2, n, 0:1], ALPHA, src_at=B_MIX)


def stage_ln(k, g, b):
    stage_norm(k, 0, lambda t: k.xT[:, t, :], lambda t: k.xT[:, t, :], KD, D,
               shift=lambda t: k.col(b, t), weight=lambda t: k.col(g, t), scale=None, centre=True, tmp_at=0)


def stage_ln1(k):
    stage_ln(k, "ln1_g_2", "ln1_b_2")


def stage_modulate_ffn2(k):
    stage_norm(k, 0, lambda t: k.xT[:, t, :], lambda t: k.hT[:, t, CTX:TT], KD, D,
               shift=lambda t: k.mod2[:, 3, t, 0:1], weight=lambda t: k.gain[:, 0, t:t + 1],
               scale=(k.mod2[:, 4, :, 0], None), centre=True, tmp_at=0)


def stage_up2(k):
    ffn_up(k, "ffn_up_2", 8, conv_grid, finish_gelu, CTX)


def stage_down2(k):
    ffn_down(k, "ffn_down_2", lambda j: k.mod2[:, 5, bass.ds(j, 1), 0], ALPHA)


def stage_ln2(k):
    stage_ln(k, "ln2_g_2", "ln2_b_2")


def stage_store(k):
    nc = k.nc
    rows = k.ar(0, T // P, D)
    turned, copied, stored = map(k.sem, ("turned", "copied", "stored"))
    with nc.Block() as block:
        @block.tensor
        def _(pe):
            for n in range(2 * (T // P)):
                t, g = divmod(n, 2)
                if n >= 8:
                    pe.wait_ge(copied, n - 7)
                for i in range(4):
                    f = 4 * g + i
                    last = pe.transpose(k.ps[:, n % 8, i * P:(i + 1) * P], k.xT[:, f, t * P:(t + 1) * P], k.ident[:, :])
                last.then_inc(turned, 1)

        @block.vector
        def _(dve):
            for n in range(2 * (T // P)):
                t, g = divmod(n, 2)
                dve.wait_ge(turned, n + 1)
                dve.tensor_copy(rows[:, t, g * HALF:(g + 1) * HALF], k.ps[:, n % 8, :]).then_inc(copied, 1)

        @block.sync
        def _(sp):
            for t in range(T // P):
                sp.wait_ge(copied, 2 * t + 2)
                sp.dma_start(k.out[0, t * P:(t + 1) * P, :], rows[:, t, :]).then_inc(stored, 16)
            sp.wait_ge(stored, 16 * (T // P))


STAGES = [
    stage_load, stage_modulation,
    stage_norm1, stage_project, stage_qk_norm, stage_bias, stage_attention, stage_ssm_params, stage_ssm, stage_glu,
    stage_mixer_norms, stage_out1, stage_norm2, stage_up1, stage_down1,
    stage_starts, stage_context, stage_modulate2, stage_short_conv, stage_spatial_gate, stage_hgrn,
    stage_out2, stage_ln1, stage_modulate_ffn2, stage_up2, stage_down2, stage_ln2, stage_store,
]


MAX_STAGE_SEMS = 90


def build_program(nc, ins, out):
    with ExitStack() as ctx:
        k = Kernel(nc, ins, out, ctx)
        for stage in STAGES:
            stage(k)
            if len(k.stage_sems) > MAX_STAGE_SEMS:
                k.release_sems()
        k.stage_ctx.close()


def lay_out(inputs):
    arrays = {name: np.ascontiguousarray(a) for name, a in inputs.items()}
    arrays["bucket_sel"] = bucket_selection()
    return arrays


def kernel(**inputs):
    import concourse.bacc as bacc
    from concourse.bass_utils import run_bass_kernel_spmd

    nc = bacc.Bacc("TRN2", target_bir_lowering=False, num_devices=1)
    arrays = lay_out(inputs)
    ins = {name: nc.dram_tensor(f"{name}_dram", a.shape, mybir.dt.from_np(a.dtype), kind="ExternalInput").ap()
           for name, a in arrays.items()}
    out = nc.dram_tensor("out_dram", (1, T, D), F32, kind="ExternalOutput").ap()
    build_program(nc, ins, out)
    r = run_bass_kernel_spmd(nc, [{f"{name}_dram": a for name, a in arrays.items()}], core_ids=[0])
    return r.results[0]["out_dram"]
```

```python
import math
from contextlib import ExitStack

import numpy as np

import concourse.bass as bass
from concourse import mybir

F32 = mybir.dt.float32
BF16 = mybir.dt.bfloat16
I32 = mybir.dt.int32
U32 = mybir.dt.uint32
ALU = mybir.AluOpType
ACT = mybir.ActivationFunctionType
AX = mybir.AxisListType

P = 128
T = 1024
HALF = 512
D = 1024
KD = D // P
EPS = 1e-6

D_SSM, SSM_GROUP, N_GROUPS, SSM_STATE = 512, 16, 32, 64
U_TILES = D_SSM // P
S_TILES = N_GROUPS * SSM_STATE // P
SPU = S_TILES // U_TILES
HEAD_DIM, N_Q, N_KV = 64, 8, 2
D_ATTN = N_Q * HEAD_DIM
A_TILES = D_ATTN // P
KV_DIM = N_KV * HEAD_DIM
D_IN = D_SSM + D_ATTN + 2 * KV_DIM
WINDOW = 128
NB = T // WINDOW
N_BUCKETS, MAX_DISTANCE = 32, 128
NEG_INF = -1e30
D_FF = 2816
FT = D_FF // P
TAB = 32

GRID_W = 64
GRID_H = T // GRID_W
CTX = 256
TT = CTX + T
HG_DK, HG_HEADS, HG_WIDTH = 128, 4, 512
SC_WIDTH, SG_WIDTH, SG_HEADS, SG_HD = 256, 256, 4, 64
IN2 = 5 * HG_WIDTH + 3 * SC_WIDTH + 2 * SG_WIDTH
O_Q, O_G, O_SC = 3 * HG_WIDTH, 4 * HG_WIDTH, 5 * HG_WIDTH
O_SG = O_SC + 3 * SC_WIDTH
ALPHA = 2.0 ** 0.25
TINY = 1e-30
CHUNK = 128
LEVELS = [64, 32, 16, 8, 4, 2, 1]
NCH = TT // CHUNK
CCH = CTX // CHUNK


def bucket_of(n):
    n = np.maximum(n, 0)
    exact = N_BUCKETS // 2
    log_part = np.log(np.maximum(n, 1) / exact) / math.log(MAX_DISTANCE / exact)
    large = np.minimum(exact + (log_part * (N_BUCKETS - exact)).astype(np.int32), N_BUCKETS - 1)
    return np.where(n < exact, n, large).astype(np.int32)


RB = 384


def bucket_selection():
    sel = np.zeros((N_BUCKETS + 1, RB), np.float32)
    for i in range(RB):
        dist = 2 * WINDOW - 1 - i
        if 0 <= dist < WINDOW:
            sel[bucket_of(np.array([dist]))[0], i] = 1.0
        else:
            sel[N_BUCKETS, i] = NEG_INF
    return sel


VECTORS = [
    ("c", 8), ("c_2", 8), ("c_ctx_2", 8), ("b_mod", 48), ("norm1_w", 8), ("norm2_w", 8),
    ("lam_re", 16), ("lam_im", 16), ("ssm_d", 4), ("b_glu", 4),
    ("ada_b_2", 48), ("out_norm_ssm", 4), ("out_norm_attn", 4), ("conv_b", 44), ("conv_w", 132),
    ("q_norm_w", 1), ("k_norm_w", 1),
    ("hg_lb_2", 8), ("hg_norm_g_2", 1), ("sc_conv_w_2", 6), ("ln1_g_2", 8), ("ln1_b_2", 8),
    ("ln2_g_2", 8), ("ln2_b_2", 8), ("ffn_conv_b_2", 22), ("ffn_conv_w_2", 198),
]
ROW_OF, _r = {}, 0
for _name, _n in VECTORS:
    ROW_OF[_name] = _r
    _r += _n
N_ROWS = _r
N_VT = -(-N_ROWS // P)

ARENA = 31400


class Kernel:

    def __init__(self, nc, ins, out, ctx):
        self.nc, self.ins, self.out, self.ctx = nc, ins, out, ctx
        self.n_sems = 0
        self.stage_ctx, self.stage_sems = ctx, []
        self.vec = self.sb("vec", [P, N_VT * P])
        self.ident = self.sb("ident", [P, P])
        self.ones = self.sb("ones", [P, P])
        self.halves = self.sb("halves", [P, P])
        self.mod1 = self.sb("mod1", [P, 6, KD])
        self.mod2 = self.sb("mod2", [P, 6, KD, 2])
        self.gain = self.sb("gain", [P, 2, KD])
        self.cact = self.sb("cact", [P, 3, KD])
        self.xT = self.sb("xT", [P, KD, T])
        self.hT = self.sb("hT", [P, 2, KD, TT], BF16)
        self.eps = self.sb("eps", [P, 1])
        self.arena = self.sb("arena", [P, ARENA])
        self.sink = self.sb("sink", [P, N_Q])
        self.ssm_neg = self.sb("ssm_neg", [P, 5, S_TILES])
        self.masks = self.sb("masks", [P, 2, len(LEVELS), P])
        self.lower = self.sb("lower", [P, 2 * HG_HEADS])
        self.one_less = self.sb("one_less", [P, 2 * HG_HEADS])
        self.raw_up = views_hT(self)(0, 2, KD, TT // 2)[:, :, :, T // 2:TT // 2]
        self.chunk_starts = self.ar(ARENA - TT - 1, TT + 1)
        self.ps = ctx.enter_context(nc.psum_tensor("ps", [P, 8, HALF], F32))
        self.w_in_loaded = self.sem("w_in_loaded")
        self.stage_ctx, self.stage_sems = ExitStack(), []

    def sb(self, name, shape, dt=F32):
        return self.ctx.enter_context(self.nc.sbuf_tensor(name, shape, dt))

    def sem(self, name):
        self.n_sems += 1
        s = self.stage_ctx.enter_context(self.nc.semaphore(f"{name}_{self.n_sems}"))
        self.stage_sems.append(s)
        return s

    def release_sems(self):
        with self.nc.Block() as block:
            @block.sync
            def _(sp):
                for s in self.stage_sems:
                    sp.sem_clear(s)
        self.stage_ctx.close()
        self.stage_ctx, self.stage_sems = ExitStack(), []

    def col(self, name, i=0, n=1):
        r = ROW_OF[name] + i
        return self.vec[:, r:r + n]

    def ar(self, at, *shape):
        n = int(np.prod(shape))
        assert at + n <= ARENA, (at, n)
        v = self.arena[:, at:at + n]
        names = "abcd"[:len(shape)]
        if len(shape) == 1:
            return v
        return v.rearrange(f"p ({' '.join(names)}) -> p {' '.join(names)}",
                           **{x: s for x, s in zip(names, shape)})


PASSES = ((0, 0), (0, 1), (1, 0))


def split_matmuls(pe, outs, lhs, rhs, n_k, start=True, stop=True):
    for kt in range(n_k):
        for a, b in PASSES:
            for i, out in enumerate(outs):
                last = pe.matmul(out, lhs(a, kt), rhs(b, kt, i), start=start and kt == 0 and (a, b) == (0, 0),
                                 stop=stop and kt == n_k - 1 and (a, b) == PASSES[-1], skip_group_check=True)
    return last


class WeightStream:

    def __init__(self, k, sources, used, raw_at, split_at, n_k=KD, width=P, whole=(), n_raw=2):
        self.sources, self.used, self.n_k, self.width, self.whole = sources, used, n_k, width, whole
        self.n_raw = n_raw
        self.exact = k.ar(split_at, 2, n_k, width)
        self.arrived = [16 * sum(len(x) for x in sources[n % n_raw:n + 1:n_raw]) for n in range(len(sources))]
        self.raw = k.ar(raw_at, n_raw, n_k, width)
        self.parts = k.ar(split_at, 2, n_k, width).rearrange("p a k n -> p (a k n)").bitcast(BF16)\
            .rearrange("p (r s k n) -> p r s k n", r=2, s=2, k=n_k)
        self.loaded = [k.sem(f"weights_in{i}") for i in range(n_raw)]
        self.hi_done, self.lo_done = map(k.sem, ("hi_done", "lo_done"))

    def load(self, sp, n):
        r = n % self.n_raw
        if n >= self.n_raw:
            sp.wait_ge(self.lo_done, n - self.n_raw + 1)
        w = self.width // len(self.sources[n])
        for i, piece in enumerate(self.sources[n]):
            sp.dma_start(self.raw[:, r, :, i * w:(i + 1) * w], piece).then_inc(self.loaded[r], 16)

    def hi(self, act, n):
        if n >= 2 and self.used is not None:
            act.wait_ge(self.used, n - 1)
        act.wait_ge(self.loaded[n % self.n_raw], self.arrived[n])
        act.activation(self.exact[:, n % 2] if n in self.whole else self.parts[:, n % 2, 0], self.raw[:, n % self.n_raw], ACT.Copy)\
           .then_inc(self.hi_done, 1)

    def lo(self, dve, n):
        dve.wait_ge(self.hi_done, n + 1)
        if n in self.whole:
            if n >= 1:
                dve.wait_ge(self.lo_done, n)
            dve.sem_inc(self.lo_done, 1)
            return
        dve.tensor_tensor(self.parts[:, n % 2, 1], self.raw[:, n % self.n_raw], self.parts[:, n % 2, 0], ALU.subtract)\
           .then_inc(self.lo_done, 1)

    def ready(self, pe, n):
        pe.wait_ge(self.lo_done, n + 1)

    def part(self, n, part, kt):
        return self.parts[:, n % 2, part, kt, :]


def chained(eng, sem, start=0):
    count = [start]

    def link(instruction):
        count[0] += 1
        instruction.then_inc(sem, 1)
        eng.wait_ge(sem, count[0])

    return link


def stage_load(k):
    nc, ins = k.nc, k.ins
    raw = k.ar(0, N_VT, P)
    x_rows = k.ar(N_VT * P, T // P, D)
    rows_in, x_in, made, turned, copied = map(k.sem, ("rows_in", "x_in", "made", "turned", "copied"))

    def row_view(name, n):
        a = ins[name]
        flat = a.rearrange(" ".join("abcd"[:len(a.shape)]) + " -> (" + " ".join("abcd"[:len(a.shape)]) + ")")
        return flat

    loads = []
    for name, n in VECTORS:
        flat, at, done = row_view(name, n), ROW_OF[name], 0
        while done < n:
            m = min(n - done, P - (at + done) % P)
            tile, row = divmod(at + done, P)
            if name in ("q_norm_w", "k_norm_w"):
                for half in range(2):
                    loads.append((raw[row:row + 1, tile, half * HEAD_DIM:(half + 1) * HEAD_DIM],
                                  flat.rearrange("(a b) -> a b", a=1)))
            else:
                loads.append((raw[row:row + m, tile, :],
                              flat[done * P:(done + m) * P].rearrange("(a b) -> a b", b=P)))
            done += m
    groups = [list(range(4 * g, 4 * g + 4)) for g in range(2)]

    with nc.Block() as block:
        @block.sync
        def _(sp):
            for t in range(T // P):
                sp.dma_start(x_rows[:, t, :], ins["x"][0, t * P:(t + 1) * P, :]).then_inc(x_in, 16)

        @block.gpsimd
        def _(pool):
            pool.memset(k.ident[:, :], 0.0).then_inc(made, 1)
            pool.memset(k.ones[:, :], 1.0).then_inc(made, 1)
            pool.memset(k.eps[:, :], EPS).then_inc(made, 1)
            pool.memset(k.halves[:, :], 0.0).then_inc(made, 1)
            pool.wait_ge(made, 4)
            pool.affine_select(out=k.ident[:, :], in_=k.ident[:, :], compare_op=ALU.not_equal, fill=1.0,
                               base=0, pattern=[[-1, P]], channel_multiplier=1).then_inc(made, 1)
            pool.wait_ge(made, 5)
            pool.memset(k.halves[0:64, 0:64], 1.0).then_inc(made, 1)
            pool.memset(k.halves[64:128, 64:128], 1.0).then_inc(made, 1)

        @block.scalar
        def _(act):
            for dst, src in loads:
                act.dma_start(dst, src).then_inc(rows_in, 16)

        @block.tensor
        def _(pe):
            pe.wait_ge(made, 7)
            pe.wait_ge(rows_in, 16 * len(loads))
            for v in range(N_VT):
                n = min(P, N_ROWS - v * P)
                last = pe.transpose(k.ps[:, v // 4, (v % 4) * P:(v % 4) * P + n],
                                    raw[0:n, v, :], k.ident[0:n, 0:n])
            last.then_inc(turned, 1)
            pe.wait_ge(x_in, 16 * (T // P))
            unit = 0
            for f in range(KD):
                for g in groups:
                    if unit >= 6:
                        pe.wait_ge(copied, unit - 6 + 1 + 1)
                    bank = 2 + unit % 6
                    for n, t in enumerate(g):
                        last = pe.transpose(k.ps[:, bank, n * P:(n + 1) * P],
                                            x_rows[:, t, f * P:(f + 1) * P], k.ident[:, :])
                    last.then_inc(turned, 1)
                    unit += 1

        @block.vector
        def _(dve):
            dve.wait_ge(turned, 1)
            dve.tensor_copy(k.vec[:, 0:min(N_ROWS, 4 * P)], k.ps[:, 0, 0:min(N_ROWS, 4 * P)])
            dve.tensor_copy(k.vec[:, 4 * P:N_ROWS], k.ps[:, 1, 0:N_ROWS - 4 * P]).then_inc(copied, 1)
            for unit in range(2 * KD):
                f, g = divmod(unit, 2)
                dve.wait_ge(turned, unit + 2)
                dve.tensor_copy(k.xT[:, f, g * HALF:(g + 1) * HALF],
                                k.ps[:, 2 + unit % 6, :]).then_inc(copied, 1)


def stage_modulation(k):
    nc, ins = k.nc, k.ins
    w1, w2 = k.ar(0, KD, D), k.ar(KD * D, KD, D)
    c1 = k.cact[:, 0, :]
    silu_c, in1, in2, mm1, mm2, ev1, ev2 = map(k.sem, ("silu_c", "in1", "in2", "mm1", "mm2", "ev1", "ev2"))
    b1 = k.col("b_mod", 0, 48).rearrange("p (m f) -> p m f", m=6)
    b2 = k.col("ada_b_2", 0, 48).rearrange("p (m f) -> p m f", m=6)
    src1 = ins["w_mod"].rearrange("o (k p) (m n) -> m p (o k) n", p=P, m=6)
    src2 = ins["ada_w_2"].rearrange("o (k p) (m n) -> m p (o k) n", p=P, m=6)
    out1, out2 = k.ps[:, 0, 0:KD], k.ps[:, 1, 0:2 * KD].rearrange("p (f c) -> p f c", c=2)

    with nc.Block() as block:
        @block.sync
        def _(sp):
            with sp.Fori(0, 6) as m:
                sp.wait_ge(ev1, m + 1)
                sp.dma_start(w1, src1[m]).then_inc(in1, 16)
                sp.wait_ge(ev2, m + 1)
                sp.dma_start(w2, src2[m]).then_inc(in2, 16)

        @block.scalar
        def _(act):
            act.activation(k.cact[:, :, :], k.vec[:, 0:3 * KD].rearrange("p (c f) -> p c f", c=3),
                           ACT.Silu).then_inc(silu_c, 1)

        @block.tensor
        def _(pe):
            pe.wait_ge(silu_c, 1)
            with pe.Fori(0, 6) as m:
                pe.wait_ge(ev1, m + 1)
                pe.wait_ge(in1, m * 16 + 16)
                for f in range(KD):
                    for kt in range(KD):
                        last = pe.matmul(out1[:, f:f + 1], w1[:, kt, f * P:(f + 1) * P], c1[:, kt:kt + 1],
                                         start=kt == 0, stop=kt == KD - 1)
                last.then_inc(mm1, 1)
                pe.wait_ge(ev2, m + 1)
                pe.wait_ge(in2, m * 16 + 16)
                for f in range(KD):
                    for kt in range(KD):
                        last = pe.matmul(out2[:, f, :], w2[:, kt, f * P:(f + 1) * P], k.cact[:, 1:3, kt],
                                         start=kt == 0, stop=kt == KD - 1)
                last.then_inc(mm2, 1)

        @block.vector
        def _(dve):
            dve.sem_inc(ev1, 1)
            dve.sem_inc(ev2, 1)
            with dve.Fori(0, 6) as m:
                dve.wait_ge(mm1, m + 1)
                dve.tensor_tensor(k.mod1[:, m, :], out1, b1[:, m, :], ALU.add).then_inc(ev1, 1)
                dve.wait_ge(mm2, m + 1)
                for c in range(2):
                    last = dve.tensor_tensor(k.mod2[:, m, :, c], out2[:, :, c], b2[:, m, :], ALU.add)
                last.then_inc(ev2, 1)


def stage_norm(k, gain_index, src, dst, tiles, width, shift, weight, scale, centre=False, tokens=T, eps=EPS,
               tmp_at=0, split=None):
    nc = k.nc
    halves = [(a, min(a + HALF, tokens)) for a in range(0, tokens, HALF)]
    nh = len(halves)
    sq = k.ar(tmp_at, 2, T)
    rstd = k.ar(tmp_at + 2 * T, T)
    mean = k.ar(tmp_at + 3 * T, T)
    sqd, stat, used, normed, meaned, centred, v_ord, final, hi_done = map(
        k.sem, ("sqd", "stat", "used", "normed", "meaned", "centred", "v_ord", "final", "hi_done"))

    def sum_bank(n):
        return k.ps[:, n, :]

    with nc.Block() as block:
        @block.tensor
        def _(pe):
            if centre:
                for n, (a, b) in enumerate(halves):
                    for t in range(tiles):
                        last = pe.matmul(sum_bank(2 + n)[:, 0:b - a], k.ones[:, :], src(t)[:, a:b],
                                         start=t == 0, stop=t == tiles - 1)
                last.then_inc(meaned, 1)
            for t in range(tiles):
                pe.wait_ge(sqd, t + 1)
                for n, (a, b) in enumerate(halves):
                    last = pe.matmul(sum_bank(n)[:, 0:b - a], k.ones[:, :], sq[:, t % 2, a:b],
                                     start=t == 0, stop=t == tiles - 1, skip_group_check=True)
                last.then_inc(used, 1)

        @block.scalar
        def _(act):
            for t in range(tiles):
                if t >= 2:
                    act.wait_ge(used, t - 1)
                if centre:
                    act.wait_ge(centred, t + 1)
                act.activation(sq[:, t % 2, 0:tokens], (dst if centre else src)(t), ACT.Square).then_inc(sqd, 1)
            act.wait_ge(stat, 1)
            act.activation(rstd[:, 0:tokens], rstd[:, 0:tokens], ACT.Sqrt).then_inc(stat, 1)
            for t in range(tiles):
                act.wait_ge(normed, t + 1)
                if shift is not None:
                    act.activation(dst(t), dst(t), ACT.Identity, bias=shift(t), scale=weight(t)).then_inc(final, 1)
                else:
                    act.activation(dst(t), dst(t), ACT.Identity, scale=weight(t)).then_inc(final, 1)
                if split is not None:
                    act.wait_ge(final, t + 1)
                    act.activation(split(t, 0), dst(t), ACT.Copy).then_inc(hi_done, 1)

        @block.vector
        def _(dve):
            link = chained(dve, v_ord)
            if scale is not None:
                g = k.gain[:, gain_index, :]
                if scale[1] is None:
                    link(dve.tensor_scalar(g, scale[0], 1.0, None, ALU.add))
                else:
                    link(dve.tensor_scalar(g, scale[0], 1.0, None, ALU.add))
                    link(dve.tensor_tensor(g, g, scale[1], ALU.mult))
            if centre:
                dve.wait_ge(meaned, 1)
                for n, (a, b) in enumerate(halves):
                    last = dve.tensor_scalar(mean[:, a:b], sum_bank(2 + n)[:, 0:b - a], 1.0 / width, None, ALU.mult)
                    link(last)
                for t in range(tiles):
                    dve.tensor_tensor(dst(t), src(t), mean[:, 0:tokens], ALU.subtract).then_inc(centred, 1)
            dve.wait_ge(used, tiles)
            for n, (a, b) in enumerate(halves):
                last = dve.tensor_scalar(rstd[:, a:b], sum_bank(n)[:, 0:b - a], 1.0 / width, eps, ALU.mult, ALU.add)
            last.then_inc(stat, 1)
            dve.wait_ge(stat, 2)
            link(dve.reciprocal(rstd[:, 0:tokens], rstd[:, 0:tokens]))
            if centre:
                dve.wait_ge(centred, tiles)
            for t in range(tiles + 2):
                if t < tiles:
                    dve.tensor_tensor(dst(t), (dst if centre else src)(t), rstd[:, 0:tokens], ALU.mult)\
                       .then_inc(normed, 1)
                if split is not None and t >= 2:
                    dve.wait_ge(hi_done, t - 1)
                    dve.tensor_tensor(split(t - 2, 1), dst(t - 2), split(t - 2, 0), ALU.subtract)


def stage_norm1(k):
    stage_norm(k, 0, lambda t: k.xT[:, t, :], lambda t: k.ar(A_H, KD, T)[:, t, :], KD, D,
               shift=lambda t: k.mod1[:, 0, t:t + 1], weight=lambda t: k.gain[:, 0, t:t + 1],
               scale=(k.mod1[:, 1, :], k.col("norm1_w", 0, KD)), split=lambda t, s: k.hT[:, s, t, CTX:TT])


A_U = 0
A_Q = A_U + U_TILES * T
A_K = A_Q + A_TILES * T
A_V = A_K + N_KV * T
A_FREE = A_V + NB * KV_DIM
A_H = ARENA - KD * T
A_STREAM = A_FREE


def stream_units(k, pe, stream, units, rhs, made, read):
    for n in range(units):
        stream.ready(pe, n)
        if n >= 4:
            pe.wait_ge(read, n - 3)
        if n in stream.whole:
            for half in range(2):
                for kt in range(stream.n_k):
                    last = pe.matmul(k.ps[:, 2 * (n % 4) + half, :], stream.exact[:, n % 2, kt, :], rhs(None, kt, half),
                                     start=kt == 0, stop=kt == stream.n_k - 1)
            last.then_inc(made, 1)
            continue
        split_matmuls(pe, [k.ps[:, 2 * (n % 4) + half, :] for half in range(2)], lambda s, kt: stream.part(n, s, kt),
                      rhs, stream.n_k).then_inc(made, 1)


def pair(k, n, pairs=4):
    b = 2 * (n % pairs)
    return k.ps[:, b:b + 2, :].rearrange("p b n -> p (b n)")


def stage_project(k):
    nc, ins = k.nc, k.ins
    u, q, kk = k.ar(A_U, U_TILES, T), k.ar(A_Q, A_TILES, T), k.ar(A_K, N_KV, T)
    v = k.ar(A_V, NB, KV_DIM)
    w_src = ins["w_in"].rearrange("o (k p) n -> p (o k) n", p=P)
    made, read, v_made = map(k.sem, ("made", "read", "v_made"))
    k_at = D_SSM + D_ATTN
    outs = [u[:, t, :] for t in range(U_TILES)] + [q[:, t, :] for t in range(A_TILES)] + \
           [kk[:, t, :] for t in range(N_KV)]
    units = len(outs)
    sources = [[w_src[:, :, n * P:(n + 1) * P]] for n in range(U_TILES + A_TILES)]
    sources += [[w_src[:, :, k_at + g * HEAD_DIM:k_at + (g + 1) * HEAD_DIM]] * 2 for g in range(N_KV)]
    sources += [[w_src[:, :, k_at + KV_DIM:D_IN]]]
    stream = WeightStream(k, sources, made, A_STREAM, A_STREAM + 2 * KD * P, whole=range(U_TILES, units))
    h = k.ar(A_H, KD, T)

    def activations(part, kt, half):
        if part is None:
            return h[:, kt, half * HALF:(half + 1) * HALF]
        return k.hT[:, part, kt, CTX + half * HALF:CTX + (half + 1) * HALF]

    with nc.Block() as block:
        @block.sync
        def _(sp):
            for n in range(units + 1):
                stream.load(sp, n)

        @block.tensor
        def _(pe):
            stream_units(k, pe, stream, units, activations, made, read)
            stream.ready(pe, units)
            for n in range(2):
                pe.wait_ge(read, units - 4 + (n + 2) % 4 + 1)
                for t in range(4):
                    b = 4 * n + t
                    last = split_matmuls(pe, [k.ps[:, 2 * ((units + n) % 4), t * P:(t + 1) * P]],
                                         lambda s, kt: k.hT[:, s, kt, CTX + b * P:CTX + (b + 1) * P],
                                         lambda s, kt, i: stream.part(units, s, kt), KD)
                last.then_inc(v_made, 1)

        @block.scalar
        def _(act):
            for n in range(units + 1):
                stream.hi(act, n)

        @block.vector
        def _(dve):
            stream.lo(dve, 0)
            for n in range(units):
                stream.lo(dve, n + 1)
                dve.wait_ge(made, n + 1)
                dve.tensor_copy(outs[n], pair(k, n)).then_inc(read, 1)
            for n in range(2):
                dve.wait_ge(v_made, n + 1)
                dve.tensor_copy(v[:, 4 * n:4 * n + 4, :].rearrange("p a b -> p (a b)"),
                                k.ps[:, 2 * ((units + n) % 4), :])


def stage_qk_norm(k):
    nc = k.nc
    q, kk = k.ar(A_Q, A_TILES, T), k.ar(A_K, N_KV, T)
    sq, rstd = k.ar(A_FREE, 2, T), k.ar(A_FREE + 2 * T, 2, T)
    tiles = [(q[:, t, :], "q_norm_w") for t in range(A_TILES)] + [(kk[:, t, :], "k_norm_w") for t in range(N_KV)]
    sqd, summed, stat, root, v_ord = map(k.sem, ("sqd", "summed", "stat", "root", "v_ord"))

    with nc.Block() as block:
        @block.scalar
        def _(act):
            for n, (x, _) in enumerate(tiles):
                if n >= 2:
                    act.wait_ge(summed, n - 1)
                act.activation(sq[:, n % 2, :], x, ACT.Square).then_inc(sqd, 1)
                act.wait_ge(stat, n + 1)
                act.activation(rstd[:, n % 2, :], rstd[:, n % 2, :], ACT.Sqrt).then_inc(root, 1)

        @block.tensor
        def _(pe):
            for n in range(len(tiles)):
                pe.wait_ge(sqd, n + 1)
                if n >= 4:
                    pe.wait_ge(stat, n - 3)
                for half in range(2):
                    last = pe.matmul(k.ps[:, 2 * (n % 4) + half, :], k.halves[:, :],
                                     sq[:, n % 2, half * HALF:(half + 1) * HALF], start=True, stop=True)
                last.then_inc(summed, 1)

        @block.vector
        def _(dve):
            link = chained(dve, v_ord)
            for n, (x, w) in enumerate(tiles):
                r = rstd[:, n % 2, :]
                dve.wait_ge(summed, n + 1)
                dve.tensor_scalar(r, pair(k, n), 1.0 / HEAD_DIM, EPS, ALU.mult, ALU.add).then_inc(stat, 1)
                dve.wait_ge(root, n + 1)
                link(dve.reciprocal(r, r))
                link(dve.scalar_tensor_tensor(x, x, k.col(w), r, ALU.mult, ALU.mult))


A_Y = 0
A_BIAS = A_FREE
A_ATT = A_BIAS + N_Q * 2 * WINDOW


def stage_bias(k):
    nc, ins = k.nc, k.ins
    bias = k.ar(A_BIAS, N_Q, 2 * WINDOW)
    table, sel, rows = k.ar(A_ATT, N_Q), k.ar(A_ATT + 8, RB), k.ar(A_ATT + 8 + RB, RB)
    sink_row = k.ar(A_ATT + 8 + 2 * RB, N_Q)
    mirrored, flip = k.ar(A_ATT + 16 + 2 * RB, N_Q, 2 * WINDOW), k.ar(A_ATT + 16 + 2 * RB + N_Q * 2 * WINDOW, P)
    k.rows_dram = nc.dram_tensor("bias_rows", (N_Q, RB), F32)
    rows_dram = k.rows_dram.ap()
    loaded, ones_set, made, copied, stored, flip_set, fetched = map(
        k.sem, ("loaded", "ones_set", "made", "copied", "stored", "flip_set", "fetched"))

    with nc.Block() as block:
        @block.gpsimd
        def _(pool):
            pool.memset(flip, 0.0).then_inc(flip_set, 1)
            pool.wait_ge(flip_set, 1)
            pool.affine_select(out=flip, in_=flip, compare_op=ALU.not_equal, fill=1.0, base=1 - P,
                               pattern=[[1, P]], channel_multiplier=1).then_inc(flip_set, 1)

        @block.vector
        def _(dve):
            dve.memset(table[N_BUCKETS:N_BUCKETS + 1, :], 1.0).then_inc(ones_set, 1)
            dve.wait_ge(made, 1)
            dve.tensor_copy(rows[0:N_Q, :], k.ps[0:N_Q, 0, 0:RB]).then_inc(copied, 1)
            dve.wait_ge(made, 2)
            dve.tensor_copy(k.sink[:, :], k.ps[:, 1, 0:N_Q])
            dve.wait_ge(made, 3)
            dve.tensor_copy(bias.rearrange("p a b -> p (a b)"), k.ps[:, 2:6, :].rearrange("p b n -> p (b n)"))

        @block.tensor
        def _(pe):
            pe.wait_ge(loaded, 48)
            pe.wait_ge(ones_set, 1)
            pe.matmul(k.ps[0:N_Q, 0, 0:RB], table[0:N_BUCKETS + 1, :], sel[0:N_BUCKETS + 1, :],
                      start=True, stop=True).then_inc(made, 1)
            pe.matmul(k.ps[:, 1, 0:N_Q], k.ones[0:1, :], sink_row[0:1, :], start=True, stop=True).then_inc(made, 1)
            pe.wait_ge(flip_set, 2)
            pe.wait_ge(fetched, 16 * N_Q)
            for n in range(4):
                last = pe.matmul(k.ps[:, 2 + n, :], flip, mirrored[:, 2 * n:2 * n + 2, :].rearrange("p a b -> p (a b)"),
                                 start=True, stop=True)
            last.then_inc(made, 1)

        @block.sync
        def _(sp):
            sp.dma_start(table[0:N_BUCKETS, :], ins["rel_bias"]).then_inc(loaded, 16)
            sp.dma_start(sel[0:N_BUCKETS + 1, :], ins["bucket_sel"]).then_inc(loaded, 16)
            sp.dma_start(sink_row[0:1, :], ins["sinks"]).then_inc(loaded, 16)
            sp.wait_ge(copied, 1)
            sp.dma_start(rows_dram, rows[0:N_Q, :]).then_inc(stored, 16)
            sp.wait_ge(stored, 16)
            for h in range(N_Q):
                window = bass.AP(k.rows_dram, h * RB, [[1, P], [1, 2 * WINDOW]])
                sp.dma_start(mirrored[:, h, :], window).then_inc(fetched, 16)


def stage_attention(k):
    nc = k.nc
    q, kk, v = k.ar(A_Q, A_TILES, T), k.ar(A_K, N_KV, T), k.ar(A_V, NB, KV_DIM)
    bias = k.ar(A_BIAS, N_Q, 2 * WINDOW)
    logits = k.ar(A_ATT, 2, 2, 2 * WINDOW)
    probs = k.ar(A_ATT + 1024, 2, 2, 2 * WINDOW)
    probs_t = k.ar(A_ATT + 2048, 2, 4, P)
    small = k.ar(A_ATT + 3072, 6, 2)
    yT = k.ar(A_Q, A_TILES, T)
    scale = HEAD_DIM ** -0.5
    units = [(n, t) for n in range(NB) for t in range(A_TILES)]
    scored, softmaxed, turned, turned_read, mixed, mixed_read, maxed, exped, v_ord, sink_exp = map(
        k.sem, ("scored", "softmaxed", "turned", "turned_read", "mixed", "mixed_read", "maxed", "exped",
                "v_ord", "sink_exp"))

    def keys(n):
        return (0, WINDOW) if n == 0 else ((n - 1) * WINDOW, 2 * WINDOW)

    with nc.Block() as block:
        @block.tensor
        def _(pe):
            def scores(i):
                n, t = units[i]
                k0, nk = keys(n)
                if i >= 2:
                    pe.wait_ge(maxed, i - 1)
                for j in range(2):
                    h = 2 * t + j
                    rows = slice(64 * j, 64 * j + 64)
                    last = pe.matmul(k.ps[:, 2 * (i % 2) + j, 0:nk], q[rows, t, n * WINDOW:(n + 1) * WINDOW],
                                     kk[rows, h // (N_Q // N_KV), k0:k0 + nk], start=True, stop=True)
                last.then_inc(scored, 1)

            def mix(i):
                n, t = units[i]
                k0, nk = keys(n)
                pe.wait_ge(softmaxed, i + 1)
                if i >= 2:
                    pe.wait_ge(turned_read, i - 1)
                for j in range(2):
                    for b in range(nk // P):
                        last = pe.transpose(k.ps[:, 4 + i % 2, (2 * j + b) * P:(2 * j + b + 1) * P],
                                            probs[:, i % 2, j, b * P:(b + 1) * P], k.ident[:, :])
                last.then_inc(turned, 1)
                pe.wait_ge(turned_read, i + 1)
                if i >= 2:
                    pe.wait_ge(mixed_read, i - 1)
                for j in range(2):
                    h = 2 * t + j
                    g = h // (N_Q // N_KV)
                    for b in range(nk // P):
                        last = pe.matmul(k.ps[64 * j:64 * j + 64, 6 + i % 2, 0:P],
                                         v[:, k0 // P + b, g * 64:(g + 1) * 64], probs_t[:, i % 2, 2 * j + b, :],
                                         start=b == 0, stop=b == nk // P - 1)
                last.then_inc(mixed, 1)

            for i in range(len(units) + 1):
                if i < len(units):
                    scores(i)
                if i >= 1:
                    mix(i - 1)

        @block.scalar
        def _(act):
            for i, (n, t) in enumerate(units):
                k0, nk = keys(n)
                act.wait_ge(maxed, i + 1)
                for j in range(2):
                    act.activation(probs[:, i % 2, j, 0:nk], logits[:, i % 2, j, 0:nk], ACT.Exp,
                                   bias=small[:, 1, j:j + 1], accum_out=small[:, 2, j:j + 1])
                    last = act.activation(small[:, 3, j:j + 1], k.sink[:, 2 * t + j:2 * t + j + 1], ACT.Exp,
                                          bias=small[:, 1, j:j + 1])
                last.then_inc(exped, 1)
                act.wait_ge(turned, i + 1)
                act.activation(probs_t[:, i % 2, :, :] if nk > P else probs_t[:, i % 2, 0:4:2, :],
                               k.ps[:, 4 + i % 2, :].rearrange("p (a b) -> p a b", b=P) if nk > P else
                               k.ps[:, 4 + i % 2, :].rearrange("p (a b) -> p a b", b=P)[:, 0:4:2, :],
                               ACT.Copy).then_inc(turned_read, 1)

        @block.vector
        def _(dve):
            link = chained(dve, v_ord)

            def output(i):
                n, t = units[i]
                dve.wait_ge(mixed, i + 1)
                for j in range(2):
                    last = dve.tensor_copy(yT[64 * j:64 * j + 64, t, n * WINDOW:(n + 1) * WINDOW],
                                           k.ps[64 * j:64 * j + 64, 6 + i % 2, 0:P])
                last.then_inc(mixed_read, 1)

            for i, (n, t) in enumerate(units):
                k0, nk = keys(n)
                x = logits[:, i % 2, :, 0:nk]
                b = bias[:, 2 * t:2 * t + 2, 2 * WINDOW - nk:2 * WINDOW]
                dve.wait_ge(scored, i + 1)
                link(dve.scalar_tensor_tensor(x, k.ps[:, 2 * (i % 2):2 * (i % 2) + 2, 0:nk],
                                              scale, b, ALU.mult, ALU.add))
                link(dve.tensor_reduce(small[:, 0, :], x, AX.X, ALU.max))
                link(dve.tensor_tensor(small[:, 0, :], small[:, 0, :], k.sink[:, 2 * t:2 * t + 2], ALU.max))
                dve.tensor_scalar(small[:, 1, :], small[:, 0, :], -1.0, None, ALU.mult).then_inc(maxed, 1)
                if i >= 1:
                    output(i - 1)
                dve.wait_ge(exped, i + 1)
                link(dve.tensor_tensor(small[:, 4, :], small[:, 2, :], small[:, 3, :], ALU.add))
                link(dve.reciprocal(small[:, 5, :], small[:, 4, :]))
                for j in range(2):
                    last = dve.tensor_scalar(probs[:, i % 2, j, 0:nk], probs[:, i % 2, j, 0:nk],
                                             small[:, 5, j:j + 1], None, ALU.mult)
                last.then_inc(softmaxed, 1)
            output(len(units) - 1)


H_BT, H_CT = 0, 2 * S_TILES * P
H_TAB = 2 * H_CT
H_SMALL = H_TAB + 2 * S_TILES * TAB
A_W = A_K
A_IN = A_W + 4 * T
A_Z = A_IN + 4 * T
A_OUT = A_Z + 4 * T
A_S = A_OUT + 4 * T
LN2_HI, LN2_LO = 0.693359375, -2.12194440e-4
ROUND = 12582912.0
TWO_PI = (6.28125, 1.93500518798828125e-3, 3.01991598195e-7)
POWERS = [TAB << i for i in range(5)]


def views_hT(k):
    flat = k.hT[:, :, :, :].rearrange("p s a b -> p (s a b)").bitcast(F32)

    def at(start, *shape):
        v = flat[:, start:start + int(np.prod(shape))]
        if len(shape) == 1:
            return v
        names = "abcd"[:len(shape)]
        return v.rearrange(f"p ({' '.join(names)}) -> p {' '.join(names)}", **dict(zip(names, shape)))
    return at


def exp_steps(dve, link, out, x, n, r):
    link(dve.tensor_scalar(x, x, -104.0, 89.0, ALU.max, ALU.min))
    link(dve.tensor_scalar(n, x, 1.4426950408889634, ROUND, ALU.mult, ALU.add))
    link(dve.tensor_scalar(n, n, -ROUND, None, ALU.add))
    link(dve.scalar_tensor_tensor(r, n, -LN2_HI, x, ALU.mult, ALU.add))
    link(dve.scalar_tensor_tensor(r, n, -LN2_LO, r, ALU.mult, ALU.add))
    link(dve.tensor_scalar(out, r, 1.0 / math.factorial(8), None, ALU.mult))
    for i in range(7, 0, -1):
        link(dve.scalar_tensor_tensor(out, out, 1.0 / math.factorial(i), r, ALU.add, ALU.mult))
    link(dve.tensor_scalar(n, n, -127.0, 128.0, ALU.max, ALU.min))
    link(dve.tensor_scalar(r.bitcast(I32), n, 127.0, float(1 << 23), ALU.add, ALU.mult))
    link(dve.scalar_tensor_tensor(out, out, 1.0, r, ALU.add, ALU.mult))


def stage_ssm_params(k):
    nc, ins = k.nc, k.ins
    h = views_hT(k)
    bt, ct = h(H_BT, 2, S_TILES, P), h(H_CT, 2, S_TILES, P)
    tab = h(H_TAB, 2, S_TILES, TAB)
    small = h(H_SMALL, 32, S_TILES)
    b_raw, c_raw = k.ar(A_W, 2, S_TILES, SSM_GROUP), k.ar(A_W + 512, 2, U_TILES, SSM_STATE)
    b_wide, c_wide = k.ar(A_IN, 2, S_TILES, P), k.ar(A_Z, 2, S_TILES, P)
    row_mask = k.ar(A_W + 1024, 8)
    b_scaled, tmp = k.ar(A_OUT, 2, S_TILES, SSM_GROUP), k.ar(A_OUT + 512, 4, S_TILES * TAB)
    ldt, sel = k.ar(A_S, S_TILES), k.ar(A_S + 16, P)
    loaded, made, spread, wide, turned, copied, v_ord, b_ord = map(
        k.sem, ("loaded", "made", "spread", "wide", "turned", "copied", "v_ord", "b_ord"))
    s = lambda i: small[:, i, :]
    (LR, DT, TH, N, R, X2, SN, CS, SIN, CM1, COS, MAG, AIM, AM1, DEN, FR, FI, T1, T2) = range(19)
    k.mag = s(MAG)
    k.powers = small[:, 19:19 + 10, :]
    k.tab, k.bt, k.ct = tab, bt, ct
    k.neg_powers = k.ssm_neg[:, :, :]
    lam_re, lam_im = k.col("lam_re", 0, S_TILES), k.col("lam_im", 0, S_TILES)

    with nc.Block() as block:
        @block.sync
        def _(sp):
            sp.dma_start(ldt[0:2, :], ins["log_dt"].rearrange("o (t k) -> (o k) t", k=2),
                         allow_slow_non_contiguous=True).then_inc(loaded, 16)
            for c, name in enumerate(("ssm_b_re", "ssm_b_im")):
                for half in range(2):
                    sp.dma_start(b_raw[64 * half:64 * half + 64, c],
                                 ins[name].rearrange("o (t k) p h -> (o k) p t h", k=2)[half]).then_inc(loaded, 16)
            for c, name in enumerate(("ssm_c_re", "ssm_c_im")):
                sp.dma_start(c_raw[:, c], ins[name].rearrange("o (j g) h p -> (o g h) j p", g=8)).then_inc(loaded, 16)

        @block.gpsimd
        def _(pool):
            pool.memset(sel[:, :], 1.0).then_inc(made, 1)
            pool.memset(row_mask, 1.0).then_inc(made, 1)
            pool.memset(b_wide, 0.0).then_inc(made, 1)
            pool.wait_ge(made, 3)
            pool.affine_select(out=sel[0:2, :], in_=sel[0:2, :], compare_op=ALU.is_ge, fill=0.0, base=0,
                               pattern=[[1, P]], channel_multiplier=-64).then_inc(made, 1)
            pool.wait_ge(made, 4)
            pool.affine_select(out=sel[0:2, :], in_=sel[0:2, :], compare_op=ALU.is_ge, fill=0.0, base=63,
                               pattern=[[-1, P]], channel_multiplier=64).then_inc(made, 1)
            pool.affine_select(out=row_mask, in_=row_mask, compare_op=ALU.is_ge, fill=0.0, base=0,
                               pattern=[[-16, 8]], channel_multiplier=1).then_inc(made, 1)
            pool.wait_ge(made, 6)
            pool.affine_select(out=row_mask, in_=row_mask, compare_op=ALU.is_ge, fill=0.0, base=15,
                               pattern=[[16, 8]], channel_multiplier=-1).then_inc(made, 1)

        @block.tensor
        def _(pe):
            pe.wait_ge(made, 7)
            pe.wait_ge(loaded, 7 * 16)
            pe.matmul(k.ps[:, 0, 0:S_TILES], sel[0:2, :], ldt[0:2, :], start=True, stop=True).then_inc(spread, 1)
            pe.wait_ge(wide, 1)
            for n in range(16):
                c, g = divmod(n % 8, 4)
                if n >= 7:
                    pe.wait_ge(copied, n - 6)
                for i in range(4):
                    last = pe.transpose(k.ps[:, 1 + n % 7, i * P:(i + 1) * P],
                                        (b_wide if n < 8 else c_wide)[:, c, 4 * g + i, :], k.ident[:, :])
                last.then_inc(turned, 1)

        @block.scalar
        def _(act):
            for n in range(16):
                c, g = divmod(n % 8, 4)
                act.wait_ge(turned, n + 1)
                act.activation((bt if n < 8 else ct)[:, c, 4 * g:4 * g + 4, :].rearrange("p a b -> p (a b)"),
                               k.ps[:, 1 + n % 7, :], ACT.Copy).then_inc(copied, 1)

        @block.vector
        def _(dve):
            link = chained(dve, v_ord)
            tt, ts, stt = dve.tensor_tensor, dve.tensor_scalar, dve.scalar_tensor_tensor
            dve.wait_ge(spread, 1)
            link(dve.tensor_copy(s(T1), k.ps[:, 0, 0:S_TILES]))
            exp_steps(dve, link, s(DT), s(T1), s(N), s(R))
            link(ts(s(LR), lam_re, -1e-4, None, ALU.min))
            link(tt(s(T1), s(DT), s(LR), ALU.mult))
            exp_steps(dve, link, s(MAG), s(T1), s(N), s(R))
            link(tt(s(TH), s(DT), lam_im, ALU.mult))
            link(ts(s(N), s(TH), 1.0 / (2 * math.pi), ROUND, ALU.mult, ALU.add))
            link(ts(s(N), s(N), -ROUND, None, ALU.add))
            for part in TWO_PI:
                link(stt(s(TH), s(N), -part, s(TH), ALU.mult, ALU.add))
            link(ts(s(TH), s(TH), 0.5, None, ALU.mult))
            link(tt(s(X2), s(TH), s(TH), ALU.mult))
            for dst, first in ((SN, 13), (CS, 14)):
                sign = lambda i: -1.0 if (i // 2) % 2 else 1.0
                link(ts(s(dst), s(X2), sign(first) / math.factorial(first), None, ALU.mult))
                for i in range(first - 2, 1, -2):
                    link(stt(s(dst), s(dst), sign(i) / math.factorial(i), s(X2), ALU.add, ALU.mult))
            link(stt(s(SN), s(SN), 1.0, s(TH), ALU.add, ALU.mult))
            link(ts(s(CS), s(CS), 1.0, None, ALU.add))
            link(stt(s(SIN), s(SN), 2.0, s(CS), ALU.mult, ALU.mult))
            link(stt(s(CM1), s(SN), -2.0, s(SN), ALU.mult, ALU.mult))
            link(ts(s(COS), s(CM1), 1.0, None, ALU.add))
            link(tt(s(AIM), s(MAG), s(SIN), ALU.mult))
            link(tt(s(AM1), s(MAG), s(COS), ALU.mult))
            link(ts(s(AM1), s(AM1), -1.0, None, ALU.add))
            link(tt(s(DEN), s(LR), s(LR), ALU.mult))
            link(tt(s(T1), lam_im, lam_im, ALU.mult))
            link(tt(s(DEN), s(DEN), s(T1), ALU.add))
            link(dve.reciprocal(s(DEN), s(DEN)))
            link(tt(s(T1), s(AM1), s(LR), ALU.mult))
            link(tt(s(T2), s(AIM), lam_im, ALU.mult))
            link(tt(s(FR), s(T1), s(T2), ALU.add))
            link(tt(s(FR), s(FR), s(DEN), ALU.mult))
            link(tt(s(T1), s(AIM), s(LR), ALU.mult))
            link(tt(s(T2), s(AM1), lam_im, ALU.mult))
            link(tt(s(FI), s(T1), s(T2), ALU.subtract))
            link(tt(s(FI), s(FI), s(DEN), ALU.mult))
            shape = (P, S_TILES, SSM_GROUP)
            fr, fi = (s(i).unsqueeze(2).to_broadcast(shape) for i in (FR, FI))
            t1 = tmp[:, 0, 0:256].rearrange("p (a b) -> p a b", b=SSM_GROUP)
            t2 = tmp[:, 1, 0:256].rearrange("p (a b) -> p a b", b=SSM_GROUP)
            dve.wait_ge(loaded, 7 * 16)
            link(tt(t1, b_raw[:, 0], fr, ALU.mult))
            link(tt(t2, b_raw[:, 1], fi, ALU.mult))
            link(tt(b_scaled[:, 0], t1, t2, ALU.subtract))
            link(tt(t1, b_raw[:, 1], fr, ALU.mult))
            link(tt(t2, b_raw[:, 0], fi, ALU.mult))
            link(tt(b_scaled[:, 1], t1, t2, ALU.add))
            dve.wait_ge(made, 7)
            for c in range(2):
                for g in range(2):
                    rows = slice(64 * g, 64 * g + 64)
                    for i in range(SPU):
                        at = 32 * i + 16 * g
                        link(dve.tensor_copy(b_wide[rows, c, i:S_TILES:SPU, at:at + SSM_GROUP],
                                             b_scaled[rows, c, i:S_TILES:SPU, :]))
            for c in range(2):
                for i in range(SPU):
                    for g in range(2):
                        m = row_mask[:, 2 * i + g:2 * i + g + 1]
                        link(ts(c_wide[:, c, i:S_TILES:SPU, 64 * g:64 * g + 64], c_raw[:, c],
                                m, 1.0 if c == 0 else -1.0, ALU.mult, ALU.mult))
            dve.sem_inc(wide, 1)
            link(dve.memset(tab[:, 0, :, 0:1], 1.0))
            link(dve.memset(tab[:, 1, :, 0:1], 0.0))
            wr, wi = s(COS), s(SIN)
            n = 1
            while n < T:
                if n < TAB:
                    shape = (P, S_TILES, n)
                    br, bi = (w.unsqueeze(2).to_broadcast(shape) for w in (wr, wi))
                    t = [tmp[:, j, 0:S_TILES * n].rearrange("p (a b) -> p a b", b=n) for j in range(4)]
                    link(tt(t[0], tab[:, 0, :, 0:n], br, ALU.mult))
                    link(tt(t[1], tab[:, 1, :, 0:n], bi, ALU.mult))
                    link(tt(t[2], tab[:, 0, :, 0:n], bi, ALU.mult))
                    link(tt(t[3], tab[:, 1, :, 0:n], br, ALU.mult))
                    link(tt(tab[:, 0, :, n:2 * n], t[0], t[1], ALU.subtract))
                    link(tt(tab[:, 1, :, n:2 * n], t[2], t[3], ALU.add))
                else:
                    link(ts(k.neg_powers[:, POWERS.index(n), :], wi, -1.0, None, ALU.mult))
                n *= 2
                if n < T:
                    if n >= TAB:
                        i = POWERS.index(n)
                        nr, ni = k.powers[:, 2 * i, :], k.powers[:, 2 * i + 1, :]
                    else:
                        nr, ni = (s(SN), s(CS)) if (wr is not None and n in (2, 8)) else (s(X2), s(TH))
                    link(tt(s(T1), wr, wr, ALU.mult))
                    link(tt(s(T2), wi, wi, ALU.mult))
                    link(stt(ni, wr, 2.0, wi, ALU.mult, ALU.mult))
                    link(tt(nr, s(T1), s(T2), ALU.subtract))
                    wr, wi = nr, ni


def stage_ssm(k):
    nc = k.nc
    u = k.ar(A_U, U_TILES, T)
    tables, m_in, z, m_out, st = (k.ar(A_W, 2, 2, T), k.ar(A_IN, 4, T), k.ar(A_Z, 2, 2, T), k.ar(A_OUT, 4, T),
                                  k.ar(A_S, 2, 2, T))
    bu_made, in_done, in_added, scanned, out_done, out_added, y_made, y_sum, scaled, level, seeded = map(
        k.sem, ("bu_made", "in_done", "in_added", "scanned", "out_done", "out_added", "y_made",
                "y_sum", "scaled", "level", "seeded"))
    N = S_TILES
    L = len(POWERS)
    bu = [k.ps[:, 2 * c:2 * c + 2, :].rearrange("p b n -> p (b n)") for c in range(2)]

    def y_banks(j):
        return 4 + 2 * (j % 2)

    with nc.Block() as block:
        @block.tensor
        def _(pe):
            def inputs(i):
                if i >= 1:
                    pe.wait_ge(in_done, 2 * i)
                for c in range(2):
                    for half in range(2):
                        last = pe.matmul(k.ps[:, 2 * c + half, :], k.bt[:, c, i, :],
                                         u[:, i // SPU, half * HALF:(half + 1) * HALF], start=True, stop=True)
                last.then_inc(bu_made, 1)

            def outputs(i):
                j = i // SPU
                pe.wait_ge(out_added, 2 * i + 2)
                if i % SPU == 0 and j >= 2:
                    pe.wait_ge(y_sum, j - 1)
                for c in range(2):
                    for half in range(2):
                        last = pe.matmul(k.ps[:, y_banks(j) + half, :], k.ct[:, c, i, :],
                                         st[:, i % 2, c, half * HALF:(half + 1) * HALF],
                                         start=i % SPU == 0 and c == 0, stop=i % SPU == SPU - 1 and c == 1,
                                         skip_group_check=True)
                last.then_inc(y_made, 1)

            inputs(0)
            inputs(1)
            for i in range(N):
                if i + 2 < N:
                    inputs(i + 2)
                outputs(i)

        @block.scalar
        def _(act):
            def gelu(j):
                act.wait_ge(y_sum, j + 1)
                act.activation(u[:, j, :], u[:, j, :], ACT.Gelu_apprx_tanh)

            def table_level(i, l):
                w, n = tables[:, i % 2], POWERS[l]
                if l == 0:
                    if i >= 2:
                        act.wait_ge(out_done, i - 1)
                    act.activation(w[:, :, 0:TAB], k.tab[:, :, i, :], ACT.Copy).then_inc(seeded, 1)
                    act.wait_ge(seeded, i + 1)
                else:
                    act.wait_ge(level, L * i + l)
                act.activation(w[:, :, n:2 * n], w[:, :, 0:n], ACT.Copy,
                               scale=k.powers[:, 2 * l, i:i + 1]).then_inc(scaled, 1)

            for i in range(N):
                for l in range(L):
                    table_level(i, l)
                if i >= 2 * SPU - 1 and i % SPU == SPU - 1:
                    gelu(i // SPU - 1)
            gelu(U_TILES - 1)

        @block.vector
        def _(dve):
            def table_level(i, l):
                w, n = tables[:, i % 2], POWERS[l]
                dve.wait_ge(scaled, L * i + l + 1)
                dve.scalar_tensor_tensor(w[:, 0, n:2 * n], w[:, 1, 0:n], k.neg_powers[:, l, i:i + 1],
                                         w[:, 0, n:2 * n], ALU.mult, ALU.add)
                dve.scalar_tensor_tensor(w[:, 1, n:2 * n], w[:, 0, 0:n], k.powers[:, 2 * l + 1, i:i + 1],
                                         w[:, 1, n:2 * n], ALU.mult, ALU.add).then_inc(level, 1)

            def rotate_in(i):
                w = tables[:, i % 2]
                dve.wait_ge(level, L * i + L)
                dve.wait_ge(bu_made, i + 1)
                if i >= 1:
                    dve.wait_ge(in_added, 2 * i)
                dve.tensor_tensor(m_in[:, 0, :], bu[0], w[:, 0, :], ALU.mult)
                dve.tensor_tensor(m_in[:, 1, :], bu[1], w[:, 1, :], ALU.mult).then_inc(in_done, 1)
                dve.tensor_tensor(m_in[:, 2, :], bu[1], w[:, 0, :], ALU.mult)
                dve.tensor_tensor(m_in[:, 3, :], bu[0], w[:, 1, :], ALU.mult).then_inc(in_done, 1)

            def scan(i):
                for c in range(2):
                    dve.wait_ge(in_added, 2 * i + c + 1)
                    dve.tensor_tensor_scan(z[:, i % 2, c, :], k.mag[:, i:i + 1].to_broadcast((P, T)),
                                           z[:, i % 2, c, :], 0.0, ALU.mult, ALU.add).then_inc(scanned, 1)

            def rotate_out(i):
                w = tables[:, i % 2]
                dve.wait_ge(scanned, 2 * i + 2)
                if i >= 1:
                    dve.wait_ge(out_added, 2 * i)
                zz = z[:, i % 2]
                dve.tensor_tensor(m_out[:, 0, :], zz[:, 0, :], w[:, 0, :], ALU.mult)
                dve.tensor_tensor(m_out[:, 1, :], zz[:, 1, :], w[:, 1, :], ALU.mult)
                dve.tensor_tensor(m_out[:, 2, :], zz[:, 1, :], w[:, 0, :], ALU.mult)
                dve.tensor_tensor(m_out[:, 3, :], zz[:, 0, :], w[:, 1, :], ALU.mult).then_inc(out_done, 1)

            def skip(j):
                dve.wait_ge(y_made, SPU * (j + 1))
                dve.scalar_tensor_tensor(u[:, j, :], u[:, j, :], k.col("ssm_d", j),
                                         k.ps[:, y_banks(j):y_banks(j) + 2, :].rearrange("p b n -> p (b n)"),
                                         ALU.mult, ALU.add).then_inc(y_sum, 1)

            for l in range(L):
                table_level(0, l)
            rotate_in(0)
            for i in range(N):
                scan(i)
                rotate_out(i)
                if i + 1 < N:
                    for l in range(L):
                        table_level(i + 1, l)
                    rotate_in(i + 1)
                if i >= SPU and i % SPU == 1:
                    skip(i // SPU - 1)
            skip(U_TILES - 1)

        @block.gpsimd
        def _(pool):
            for i in range(N):
                if i >= 2:
                    pool.wait_ge(out_done, i - 1)
                pool.wait_ge(in_done, 2 * i + 1)
                pool.tensor_tensor(z[:, i % 2, 0, :], m_in[:, 0, :], m_in[:, 1, :], ALU.add).then_inc(in_added, 1)
                pool.wait_ge(in_done, 2 * i + 2)
                pool.tensor_tensor(z[:, i % 2, 1, :], m_in[:, 2, :], m_in[:, 3, :], ALU.subtract).then_inc(in_added, 1)
                pool.wait_ge(out_done, i + 1)
                if i >= 2:
                    pool.wait_ge(y_made, i - 1)
                pool.tensor_tensor(st[:, i % 2, 0, :], m_out[:, 0, :], m_out[:, 1, :], ALU.subtract).then_inc(out_added, 1)
                pool.tensor_tensor(st[:, i % 2, 1, :], m_out[:, 2, :], m_out[:, 3, :], ALU.add).then_inc(out_added, 1)


A_WG = A_K


def split_tiles(k, act, dve, n, src, part, hi_done, lo_done):
    for t in range(n):
        if act is not None:
            act.activation(part(0, t), src(t), ACT.Copy).then_inc(hi_done, 1)
        else:
            dve.wait_ge(hi_done, t + 1)
            dve.tensor_tensor(part(1, t), src(t), part(0, t), ALU.subtract).then_inc(lo_done, 1)


def stage_glu(k):
    nc, ins = k.nc, k.ins
    z = k.ar(A_U, U_TILES, T)
    zs = lambda s, t: k.hT[:, s, t, 0:T]
    gate = k.ar(A_WG + U_TILES * D_SSM, U_TILES, T)
    made, gated, z_hi, z_lo = map(k.sem, ("made", "gated", "z_hi", "z_lo"))
    src = ins["w_glu"].rearrange("o (k p) n -> p (o k) n", p=P)
    stream = WeightStream(k, [[src[:, :, n * P:(n + 1) * P]] for n in range(U_TILES)], made,
                          A_WG + 2 * U_TILES * D_SSM + U_TILES * T, A_WG, n_k=U_TILES)
    with nc.Block() as block:
        @block.sync
        def _(sp):
            for n in range(U_TILES):
                stream.load(sp, n)

        @block.tensor
        def _(pe):
            pe.wait_ge(z_lo, U_TILES)
            stream_units(k, pe, stream, U_TILES, lambda s, kt, half: zs(s, kt)[:, half * HALF:(half + 1) * HALF],
                         made, None)

        @block.scalar
        def _(act):
            split_tiles(k, act, None, U_TILES, lambda t: z[:, t, :], zs, z_hi, z_lo)
            for n in range(U_TILES):
                stream.hi(act, n)
                if n >= 1:
                    act.wait_ge(made, n)
                    act.activation(gate[:, n - 1, :], pair(k, n - 1), ACT.Sigmoid, bias=k.col("b_glu", n - 1)).then_inc(gated, 1)
            act.wait_ge(made, U_TILES)
            act.activation(gate[:, U_TILES - 1, :], pair(k, U_TILES - 1), ACT.Sigmoid,
                           bias=k.col("b_glu", U_TILES - 1)).then_inc(gated, 1)

        @block.vector
        def _(dve):
            split_tiles(k, None, dve, U_TILES, lambda t: z[:, t, :], zs, z_hi, z_lo)
            for n in range(U_TILES):
                stream.lo(dve, n)
            for n in range(U_TILES):
                dve.wait_ge(gated, n + 1)
                dve.tensor_tensor(z[:, n, :], z[:, n, :], gate[:, n, :], ALU.mult)


def stage_mixer_norms(k):
    stage_norm(k, None, lambda t: k.ar(A_U, U_TILES, T)[:, t, :], lambda t: k.ar(A_K + 4 * T, U_TILES, T)[:, t, :],
               U_TILES, D_SSM, shift=None, weight=lambda t: k.col("out_norm_ssm", t), scale=None, tmp_at=A_K,
               split=lambda t, s: k.hT[:, s, t, 0:T])
    stage_norm(k, None, lambda t: k.ar(A_Q, A_TILES, T)[:, t, :], lambda t: k.ar(A_K + 4 * T, U_TILES, T)[:, t, :],
               A_TILES, D_ATTN, shift=None, weight=lambda t: k.col("out_norm_attn", t), scale=None, tmp_at=A_K,
               split=lambda t, s: k.hT[:, s, U_TILES + t, 0:T])


def stage_out_projection(k, name, gate, residual_scale=None, src_at=None):
    nc, ins = k.nc, k.ins
    parts = lambda s, t: k.hT[:, s, t, 0:T]
    src = ins[name].rearrange("o (k p) n -> p (o k) n", p=P)
    made, read, v_ord, mix_hi, mix_lo = map(k.sem, ("made", "read", "v_ord", "mix_hi", "mix_lo"))
    stream = WeightStream(k, [[src[:, :, n * P:(n + 1) * P]] for n in range(KD)], made, A_K, A_K + 2 * KD * P)
    with nc.Block() as block:
        @block.sync
        def _(sp):
            for n in range(KD):
                stream.load(sp, n)

        @block.tensor
        def _(pe):
            if src_at is not None:
                pe.wait_ge(mix_lo, KD)
            stream_units(k, pe, stream, KD, lambda s, kt, half: parts(s, kt)[:, half * HALF:(half + 1) * HALF], made, read)

        @block.scalar
        def _(act):
            if src_at is not None:
                split_tiles(k, act, None, KD, lambda t: k.ar(src_at, KD, T)[:, t, :], parts, mix_hi, mix_lo)
            for n in range(KD):
                stream.hi(act, n)

        @block.vector
        def _(dve):
            link = chained(dve, v_ord)
            if src_at is not None:
                split_tiles(k, None, dve, KD, lambda t: k.ar(src_at, KD, T)[:, t, :], parts, mix_hi, mix_lo)
            stream.lo(dve, 0)
            for n in range(KD):
                x = k.xT[:, n, :]
                if n + 1 < KD:
                    stream.lo(dve, n + 1)
                if residual_scale is not None:
                    link(dve.tensor_scalar(x, x, residual_scale, None, ALU.mult))
                dve.wait_ge(made, n + 1)
                dve.scalar_tensor_tensor(x, pair(k, n), gate(n), x, ALU.mult, ALU.add).then_inc(read, 1)


def stage_out1(k):
    stage_out_projection(k, "w_out", lambda n: k.mod1[:, 2, n:n + 1])


F_G = 0
F_S = F_G + FT * T
F_C = F_S + 4 * KD * P


def ffn_up(k, w_name, n_taps, convolve, finish):
    nc, ins = k.nc, k.ins
    g = k.ar(F_G, FT, T).rearrange("p a t -> p (a t)").bitcast(BF16).rearrange("p (s a t) -> p s a t", s=2, t=T)
    raw = k.raw_up
    w = k.ar(F_S, 4 * KD * P).bitcast(BF16).rearrange("p (b s h k n) -> p b s h k n", b=2, s=2, h=2, n=P)
    conv = k.ar(F_C, 4, T)
    src = ins[w_name].rearrange("o (k p) (s j n) -> j s p (o k) n", p=P, s=2, n=P)
    loaded, hi, lo, made, centre, conved, acted, g_hi, done = (
        [k.sem(f"{name}{b}") for b in range(2)] for name in
        ("loaded", "hi", "lo", "made", "centre", "conved", "acted", "g_hi", "done"))
    v_ord = k.sem("v_ord")

    def ps(b, s):
        bank = 4 * b + 2 * s
        return k.ps[:, bank:bank + 2, :].rearrange("p b n -> p (b n)")

    with nc.Block() as block:
        @block.sync
        def _(sp):
            with sp.Fori(0, FT // 2) as i:
                for b in range(2):
                    sp.wait_ge(lo[1 - b], i + 1)
                    for s in range(2):
                        sp.dma_start(raw[:, s], src[2 * i + b, s]).then_inc(loaded[b], 16)

        @block.tensor
        def _(pe):
            pe.sem_inc(made[0], 1)
            pe.sem_inc(made[1], 1)
            with pe.Fori(0, FT // 2) as i:
                for b in range(2):
                    pe.wait_ge(lo[b], i + 1 + b)
                    pe.wait_ge(done[b], i + 1)
                    for s in range(2):
                        last = split_matmuls(pe, [k.ps[:, 4 * b + 2 * s + half, :] for half in range(2)],
                                             lambda part, kt: w[:, b, s, part, kt, :],
                                             lambda part, kt, half: k.hT[:, part, kt, half * HALF:(half + 1) * HALF], KD)
                    last.then_inc(made[b], 1)

        @block.scalar
        def _(act):
            def split_hi(i, b):
                act.wait_ge(loaded[b], i * 32 + 32)
                act.wait_ge(made[b], i + 1)
                act.activation(w[:, b, :, 0], raw, ACT.Copy).then_inc(hi[b], 1)

            def unit(i, b):
                c = [conv[:, 2 * b + s, :] for s in range(2)]
                act.wait_ge(made[b], i + 2)
                act.wait_ge(done[b], i + 1)
                convolve(k, "scalar", act, 2 * i + b, c, [ps(b, s) for s in range(2)], centre[b])
                act.wait_ge(conved[b], i + 1)
                finish(k, "scalar", act, c, None, None, acted[b])
                act.wait_ge(g_hi[b], 2 * i + 1)
                act.activation(g[:, 0, 2 * i + b, :], c[0], ACT.Copy).then_inc(g_hi[b], 1)

            split_hi(0, 0)
            with act.Fori(0, FT // 2 - 1) as i:
                split_hi(i, 1)
                unit(i, 0)
                split_hi(i + 1, 0)
                unit(i, 1)
            split_hi(FT // 2 - 1, 1)
            unit(FT // 2 - 1, 0)
            unit(FT // 2 - 1, 1)

        @block.vector
        def _(dve):
            def split_lo(i, b):
                dve.wait_ge(hi[b], i + 1)
                dve.tensor_tensor(w[:, b, :, 1], raw, w[:, b, :, 0], ALU.subtract).then_inc(lo[b], 1)

            def unit(i, b):
                dve.wait_ge(centre[b], i + 1)
                c = [conv[:, 2 * b + s, :] for s in range(2)]
                p = [ps(b, s) for s in range(2)]
                convolve(k, "vector", dve, 2 * i + b, c, p, (v_ord, i * (2 * n_taps) + b * n_taps, conved[b]))
                dve.wait_ge(acted[b], i + 1)
                finish(k, "vector", dve, c, p, c[0], g_hi[b])
                dve.wait_ge(g_hi[b], 2 * i + 2)
                dve.tensor_tensor(g[:, 1, 2 * i + b, :], c[0], g[:, 0, 2 * i + b, :], ALU.subtract).then_inc(done[b], 1)

            dve.sem_inc(done[0], 1)
            dve.sem_inc(done[1], 1)
            dve.sem_inc(lo[1], 1)
            split_lo(0, 0)
            with dve.Fori(0, FT // 2 - 1) as i:
                split_lo(i, 1)
                unit(i, 0)
                split_lo(i + 1, 0)
                unit(i, 1)
            split_lo(FT // 2 - 1, 1)
            unit(FT // 2 - 1, 0)
            unit(FT // 2 - 1, 1)


def ffn_down(k, w_name, gate, residual_scale):
    nc, ins = k.nc, k.ins
    g = k.ar(F_G, FT, T).rearrange("p a t -> p (a t)").bitcast(BF16).rearrange("p (s a t) -> p s a t", s=2, t=T)
    h = views_hT(k)
    raw = h(0, FT, P)
    w = h(FT * P, 2 * FT * P).bitcast(BF16).rearrange("p (b h k n) -> p b h k n", b=2, h=2, n=P)
    src = ins[w_name].rearrange("o (k p) (m n) -> m p (o k) n", p=P, n=P)
    loaded, hi, lo, made, done, scaled = (
        [k.sem(f"{name}{b}") for b in range(2)] for name in ("loaded", "hi", "lo", "made", "done", "scaled"))
    with nc.Block() as block:
        @block.sync
        def _(sp):
            with sp.Fori(0, KD // 2) as i:
                for b in range(2):
                    sp.wait_ge(lo[1 - b], i + 1)
                    sp.dma_start(raw, src[2 * i + b]).then_inc(loaded[b], 16)

        @block.tensor
        def _(pe):
            pe.sem_inc(made[0], 1)
            pe.sem_inc(made[1], 1)
            with pe.Fori(0, KD // 2) as i:
                for b in range(2):
                    pe.wait_ge(lo[b], i + 1 + b)
                    pe.wait_ge(done[b], i + 1)
                    split_matmuls(pe, [k.ps[:, 2 * b + half, :] for half in range(2)],
                                  lambda part, kt: w[:, b, part, kt, :],
                                  lambda part, kt, half: g[:, part, kt, half * HALF:(half + 1) * HALF], FT)\
                        .then_inc(made[b], 1)

        @block.scalar
        def _(act):
            with act.Fori(0, KD // 2) as i:
                for b in range(2):
                    act.wait_ge(loaded[b], i * 16 + 16)
                    act.wait_ge(made[b], i + 1)
                    act.activation(w[:, b, 0], raw, ACT.Copy).then_inc(hi[b], 1)

        @block.vector
        def _(dve):
            def output(i, b):
                x = k.xT[:, 2 * i + b, :]
                if residual_scale is not None:
                    dve.tensor_scalar(x, x, residual_scale, None, ALU.mult).then_inc(scaled[b], 1)
                    dve.wait_ge(scaled[b], i + 1)
                dve.wait_ge(made[b], i + 2)
                dve.scalar_tensor_tensor(x, pair(k, b), gate(2 * i + b), x, ALU.mult, ALU.add).then_inc(done[b], 1)

            def split_lo(b, i):
                dve.wait_ge(hi[b], i + 1)
                dve.tensor_tensor(w[:, b, 1], raw, w[:, b, 0], ALU.subtract).then_inc(lo[b], 1)

            dve.sem_inc(done[0], 1)
            dve.sem_inc(done[1], 1)
            dve.sem_inc(lo[1], 1)
            split_lo(0, 0)
            split_lo(1, 0)
            with dve.Fori(0, KD // 2 - 1) as i:
                output(i, 0)
                split_lo(0, i + 1)
                output(i, 1)
                split_lo(1, i + 1)
            output(KD // 2 - 1, 0)
            output(KD // 2 - 1, 1)


def conv_causal(k, engine, eng, j, c, p, sems):
    w = k.col("conv_w", 0, 6 * FT).rearrange("p (t s j) -> p t s j", t=3, s=2)
    bias = k.col("conv_b", 0, 2 * FT).rearrange("p (s j) -> p s j", s=2)
    if engine == "scalar":
        for s in range(2):
            last = eng.activation(c[s], p[s], ACT.Identity, bias=bias[:, s, bass.ds(j, 1)], scale=w[:, 2, s, bass.ds(j, 1)])
        last.then_inc(sems, 1)
        return
    v_ord, base, conved = sems
    n = 0
    for tap in (1, 0):
        lag = 2 - tap
        for s in range(2):
            if tap == 0:
                eng.wait_ge(v_ord, base + s + 1)
            last = eng.scalar_tensor_tensor(c[s][:, lag:T], p[s][:, 0:T - lag], w[:, tap, s, bass.ds(j, 1)],
                                            c[s][:, lag:T], ALU.mult, ALU.add)
            n += 1
            last.then_inc(v_ord, 1)
    eng.wait_ge(v_ord, base + n)
    eng.sem_inc(conved, 1)


def finish_silu(k, engine, eng, c, p, g, sem):
    if engine == "scalar":
        eng.activation(c[1], c[1], ACT.Silu).then_inc(sem, 1)
    else:
        eng.tensor_tensor(g, c[0], c[1], ALU.mult).then_inc(sem, 1)


def conv_grid(k, engine, eng, j, c, p, sems):
    w = k.col("ffn_conv_w_2", 0, 9 * FT).rearrange("p (t j) -> p t j", t=9)
    if engine == "scalar":
        eng.activation(c[0], p[0], ACT.Identity, bias=k.col("ffn_conv_b_2", 0, FT)[:, bass.ds(j, 1)],
                       scale=w[:, 4, bass.ds(j, 1)]).then_inc(sems, 1)
        return
    v_ord, base, conved = sems
    out = c[0].rearrange("p (r c) -> p r c", c=GRID_W)
    src = p[0].rearrange("p (r c) -> p r c", c=GRID_W)
    n = 0
    for di in (-1, 0, 1):
        for dj in (-1, 0, 1):
            if di == dj == 0:
                continue
            r0, r1 = max(0, -di), GRID_H - max(0, di)
            c0, c1 = max(0, -dj), GRID_W - max(0, dj)
            to = out[:, r0:r1, c0:c1]
            eng.scalar_tensor_tensor(to, src[:, r0 + di:r1 + di, c0 + dj:c1 + dj],
                                     w[:, 3 * (di + 1) + dj + 1, bass.ds(j, 1)], to, ALU.mult, ALU.add).then_inc(v_ord, 1)
            n += 1
            eng.wait_ge(v_ord, base + n)
    eng.sem_inc(conved, 1)


def finish_gelu(k, engine, eng, c, p, g, sem):
    if engine == "scalar":
        eng.activation(c[0], c[0], ACT.Gelu).then_inc(sem, 1)
    else:
        eng.tensor_tensor(g, c[0], p[1], ALU.mult).then_inc(sem, 1)


def stage_norm2(k):
    stage_norm(k, 0, lambda t: k.xT[:, t, :], lambda t: k.ar(4 * T, KD, T)[:, t, :], KD, D,
               shift=lambda t: k.mod1[:, 3, t:t + 1], weight=lambda t: k.gain[:, 0, t:t + 1],
               scale=(k.mod1[:, 4, :], k.col("norm2_w", 0, KD)), split=lambda t, s: k.hT[:, s, t, 0:T])


def stage_up1(k):
    ffn_up(k, "w_up", 4, conv_causal, finish_silu)


def stage_down1(k):
    ffn_down(k, "w_down", lambda j: k.mod1[:, 5, bass.ds(j, 1)], None)


B_MIX = 0
B_FREE = KD * T
B_MOD = B_FREE + 4 * T
B_CTX = B_MOD + KD * T
LN_TINY = math.log(TINY)


def stage_context(k):
    nc, ins = k.nc, k.ins
    rows = k.ar(0, CCH, D)
    loaded, turned, ones_set, masked, v_ord, exped, subtracted = map(
        k.sem, ("loaded", "turned", "ones_set", "masked", "v_ord", "exped", "subtracted"))
    p_exp = k.ar(CCH * D, 2 * HG_HEADS)
    p_sum = k.ar(CCH * D + 8, 2 * HG_HEADS)
    ctx = k.ar(B_CTX, KD, CTX)
    with nc.Block() as block:
        @block.sync
        def _(sp):
            sp.dma_start(rows, ins["ctx_2"].rearrange("o (t p) d -> p (o t) d", p=P)).then_inc(loaded, 16)

        @block.tensor
        def _(pe):
            pe.wait_ge(loaded, 16)
            for f in range(KD):
                for t in range(CCH):
                    last = pe.transpose(k.ps[:, f // 2, (f % 2) * CTX + t * P:(f % 2) * CTX + (t + 1) * P],
                                        rows[:, t, f * P:(f + 1) * P], k.ident[:, :])
            last.then_inc(turned, 1)

        @block.scalar
        def _(act):
            act.wait_ge(subtracted, 1)
            act.activation(p_exp, p_exp, ACT.Exp).then_inc(exped, 1)

        @block.vector
        def _(dve):
            link = chained(dve, v_ord)
            lb = k.col("hg_lb_2", 0, 2 * HG_HEADS)
            dve.tensor_tensor(p_exp, lb, lb, ALU.subtract).then_inc(subtracted, 1)
            dve.wait_ge(exped, 1)
            link(dve.reciprocal(p_sum, p_exp))
            link(dve.tensor_tensor(p_exp, p_exp, p_sum, ALU.mult))
            link(dve.tensor_tensor(k.lower[:, :], p_exp, p_exp, ALU.subtract))
            link(dve.tensor_scalar(k.one_less[:, :], k.lower[:, :], -1.0, 1.0, ALU.mult, ALU.add))
            dve.wait_ge(turned, 1)
            for f in range(0, KD, 2):
                dve.tensor_copy(ctx[:, f:f + 2, :],
                                k.ps[:, f // 2, :].rearrange("p (a b) -> p a b", a=2))

        @block.gpsimd
        def _(pool):
            pool.memset(k.masks[:, :, :, :], 0.0).then_inc(ones_set, 1)
            pool.wait_ge(ones_set, 1)
            n = 0
            for l, m in enumerate(LEVELS):
                for d in range(2):
                    quarter = k.masks[:, d, l, :].rearrange("p (b h r) -> p b h r", h=2, r=m)[:, :, 1 - d, :]
                    pool.memset(quarter, 1.0).then_inc(masked, 1)
                    n += 1
                    pool.wait_ge(masked, n)
                    for base, sign in ((-m * d, 1), (m * d + m - 1, -1)):
                        pool.affine_select(out=quarter, in_=quarter, compare_op=ALU.is_ge, fill=0.0, base=base,
                                           pattern=[[-2 * m * sign, P // (2 * m)], [0, m]],
                                           channel_multiplier=sign).then_inc(masked, 1)
                        n += 1
                        pool.wait_ge(masked, n)


def stage_modulate2(k):
    for c, (a, b) in enumerate(((CTX, TT), (0, CTX))):
        stage_norm(k, 0, (lambda t: k.xT[:, t, :]) if c == 0 else (lambda t: k.ar(B_CTX, KD, CTX)[:, t, :]),
                   lambda t, a=a, b=b: k.ar(B_MOD, KD, T)[:, t, 0:b - a], KD, D,
                   shift=lambda t, c=c: k.mod2[:, 0, t, c:c + 1], weight=lambda t: k.gain[:, 0, t:t + 1],
                   scale=(k.mod2[:, 1, :, c], None), centre=True, tokens=b - a, tmp_at=B_FREE,
                   split=lambda t, s, a=a, b=b: k.hT[:, s, t, a:b])


def stage_short_conv(k):
    nc, ins = k.nc, k.ins
    n_t = SC_WIDTH // P
    gate_c, x, y = (k.ar(B_FREE + 4 * KD * P + i * n_t * T, n_t, T) for i in range(3))
    mix = k.ar(B_MIX, KD, T)
    made, copied, used, x_ready, centre, v_ord = map(
        k.sem, ("made", "copied", "used", "x_ready", "centre", "v_ord"))
    parts = [(part, t) for t in range(n_t) for part in (1, 2, 0)]
    src = ins["w_in_2"].rearrange("o (k p) n -> p (o k) n", p=P)
    columns = [O_SC + part * SC_WIDTH + t * P for part, t in parts]
    stream = WeightStream(k, [[src[:, :, c:c + P]] for c in columns], made, B_FREE, B_FREE + 2 * KD * P)
    with nc.Block() as block:
        @block.sync
        def _(sp):
            for n in range(len(parts)):
                stream.load(sp, n)

        @block.tensor
        def _(pe):
            for n in range(len(parts)):
                stream.ready(pe, n)
                if n >= 4:
                    pe.wait_ge(copied, 1)
                    pe.wait_ge(used, n - 4)
                split_matmuls(pe, [k.ps[:, 2 * (n % 4) + half, :] for half in range(2)],
                              lambda s, kt: stream.part(n, s, kt),
                              lambda s, kt, half: k.hT[:, s, kt, CTX + half * HALF:CTX + (half + 1) * HALF], KD)\
                    .then_inc(made, 1)

        @block.scalar
        def _(act):
            for n in range(3):
                stream.hi(act, n)
            for t in range(n_t):
                act.wait_ge(made, 3 * t + 1)
                act.activation(gate_c[:, t, :], pair(k, 3 * t), ACT.Copy).then_inc(copied, 1)
                act.wait_ge(x_ready, t + 1)
                act.activation(y[:, t, :], x[:, t, :], ACT.Copy, scale=k.col("sc_conv_w_2", n_t + t)).then_inc(centre, 1)
                if t == 0:
                    for n in range(3, len(parts)):
                        stream.hi(act, n)

        @block.vector
        def _(dve):
            link = chained(dve, v_ord)
            for n in range(3):
                stream.lo(dve, n)
            for t in range(n_t):
                dve.wait_ge(copied, t + 1)
                dve.wait_ge(made, 3 * t + 2)
                ins_ = dve.tensor_tensor(x[:, t, :], pair(k, 3 * t + 1), gate_c[:, t, :], ALU.mult)
                ins_.then_inc(x_ready, 1)
                dve.wait_ge(centre, t + 1)
                dve.sem_inc(used, 1)
                if t == 0:
                    for n in range(3, len(parts)):
                        stream.lo(dve, n)
                link(dve.scalar_tensor_tensor(y[:, t, 1:T], x[:, t, 0:T - 1], k.col("sc_conv_w_2", t),
                                              y[:, t, 1:T], ALU.mult, ALU.add))
                link(dve.scalar_tensor_tensor(y[:, t, 0:T - 1], x[:, t, 1:T], k.col("sc_conv_w_2", 2 * n_t + t),
                                              y[:, t, 0:T - 1], ALU.mult, ALU.add))
                dve.wait_ge(made, 3 * t + 3)
                dve.tensor_tensor(mix[:, HG_HEADS + t, :], pair(k, 3 * t + 2), y[:, t, :], ALU.mult).then_inc(used, 1)


def stage_spatial_gate(k):
    nc, ins = k.nc, k.ins
    n_t, nb = SG_WIDTH // P, T // P
    at = B_FREE
    w = k.ar(at, KD, 2 * SG_WIDTH); at += KD * 2 * SG_WIDTH
    parts = k.ar(at, KD * 2 * SG_WIDTH).bitcast(BF16).rearrange("p (s k n) -> p s k n", s=2, k=KD)
    at += KD * 2 * SG_WIDTH
    u = k.ar(at, n_t, T); at += n_t * T
    v = k.ar(at, nb, SG_WIDTH); at += nb * SG_WIDTH
    sq = k.ar(at, nb, SG_WIDTH); at += nb * SG_WIDTH
    ws = k.ar(at, SG_HEADS, P); at += SG_HEADS * P
    ws_t = k.ar(at, SG_HEADS, P); at += SG_HEADS * P
    gb = k.ar(at, 2, SG_WIDTH); at += 2 * SG_WIDTH
    rows = k.ar(at, 2 * SG_WIDTH + SG_HEADS * P); at += 2 * SG_WIDTH + SG_HEADS * P
    stats = k.ar(at, 2, nb * SG_HEADS); at += 2 * nb * SG_HEADS
    mix = k.ar(B_MIX, KD, T)
    loaded, made, v_made, prep, copied, normed, mixed, v_ord, rooted, to_root = map(
        k.sem, ("loaded", "made", "v_made", "prep", "copied", "normed", "mixed", "v_ord", "rooted", "to_root"))
    hi_done, lo_done = k.sem("hi_done"), k.sem("lo_done")
    w_loaded = k.sem("w_loaded")
    with nc.Block() as block:
        @block.sync
        def _(sp):
            sp.dma_start(w, ins["w_in_2"].rearrange("o (k p) n -> p (o k) n", p=P)[:, :, O_SG:IN2]).then_inc(w_loaded, 16)
            sp.dma_start(ws, ins["sg_w_2"].rearrange("o g t s -> t (o g) s")).then_inc(loaded, 16)
            sp.dma_start(rows[0:1, 0:SG_WIDTH], ins["sg_ln_g_2"]).then_inc(loaded, 16)
            sp.dma_start(rows[0:1, SG_WIDTH:2 * SG_WIDTH], ins["sg_ln_b_2"]).then_inc(loaded, 16)
            sp.dma_start(rows[0:1, 2 * SG_WIDTH:], ins["sg_b_2"].rearrange("o g t -> o (g t)")).then_inc(loaded, 16)

        @block.tensor
        def _(pe):
            pe.wait_ge(lo_done, 1)
            for b in range(nb):
                last = split_matmuls(pe, [k.ps[:, b // 2, (b % 2) * SG_WIDTH:(b % 2 + 1) * SG_WIDTH]],
                                     lambda s, kt: k.hT[:, s, kt, CTX + b * P:CTX + (b + 1) * P],
                                     lambda s, kt, i: parts[:, s, kt, SG_WIDTH:2 * SG_WIDTH], KD)
            last.then_inc(v_made, 1)
            pe.wait_ge(loaded, 4 * 16)
            for g in range(SG_HEADS):
                last = pe.transpose(k.ps[:, 4, g * P:(g + 1) * P], ws[:, g, :], k.ident[:, :])
            last.then_inc(prep, 1)
            pe.matmul(k.ps[:, 5, :], k.ones[0:1, :], rows[0:1, 0:2 * SG_WIDTH], start=True, stop=True).then_inc(prep, 1)
            pe.wait_ge(copied, 6)
            for t in range(n_t):
                split_matmuls(pe, [k.ps[:, 2 * t + half, :] for half in range(2)],
                              lambda s, kt: parts[:, s, kt, t * P:(t + 1) * P],
                              lambda s, kt, half: k.hT[:, s, kt, CTX + half * HALF:CTX + (half + 1) * HALF], KD)\
                    .then_inc(made, 1)
            pe.wait_ge(normed, 1)
            for g in range(SG_HEADS):
                t, r = divmod(g, 2)
                out_rows = slice(64 * r, 64 * r + 64)
                for half in range(2):
                    bank = 4 + 2 * t + half
                    b_row = rows[0:1, 2 * SG_WIDTH + g * P:2 * SG_WIDTH + (g + 1) * P]
                    for i in range(4):
                        cols = slice(i * P, (i + 1) * P)
                        pe.matmul(k.ps[out_rows, bank, cols], k.ones[0:1, 0:SG_HD], b_row, start=True, stop=False,
                                  skip_group_check=True)
                        last = pe.matmul(k.ps[out_rows, bank, cols],
                                         v[:, 4 * half + i, g * SG_HD:(g + 1) * SG_HD], ws_t[:, g, :],
                                         start=False, stop=True, skip_group_check=True)
            last.then_inc(mixed, 1)

        @block.scalar
        def _(act):
            act.wait_ge(w_loaded, 16)
            act.activation(parts[:, 0], w, ACT.Copy).then_inc(hi_done, 1)
            act.wait_ge(v_made, 1)
            for b in range(4):
                act.activation(v[:, 2 * b:2 * b + 2, :].rearrange("p a b -> p (a b)"), k.ps[:, b, :], ACT.Copy).then_inc(copied, 1)
            act.wait_ge(prep, 1)
            act.activation(ws_t.rearrange("p a b -> p (a b)"), k.ps[:, 4, :], ACT.Copy).then_inc(copied, 1)
            act.wait_ge(prep, 2)
            act.activation(gb.rearrange("p a b -> p (a b)"), k.ps[:, 5, :], ACT.Copy).then_inc(copied, 1)
            for t in range(n_t):
                act.wait_ge(made, t + 1)
                act.activation(u[:, t, :], pair(k, t), ACT.Copy).then_inc(copied, 1)
            act.wait_ge(to_root, 1)
            act.activation(stats[:, 1, :], stats[:, 1, :], ACT.Sqrt).then_inc(rooted, 1)

        @block.vector
        def _(dve):
            link = chained(dve, v_ord)
            dve.wait_ge(hi_done, 1)
            dve.tensor_tensor(parts[:, 1], w, parts[:, 0], ALU.subtract).then_inc(lo_done, 1)
            dve.wait_ge(copied, 6)
            vg = v.rearrange("p b (g c) -> p (b g) c", c=SG_HD)
            sg = sq.rearrange("p b (g c) -> p (b g) c", c=SG_HD)
            mean, var = (stats[:, i, :].unsqueeze(2).to_broadcast((P, nb * SG_HEADS, SG_HD)) for i in range(2))
            link(dve.tensor_reduce(stats[:, 0, :], vg, AX.X, ALU.add))
            link(dve.tensor_scalar(stats[:, 0, :], stats[:, 0, :], 1.0 / SG_HD, None, ALU.mult))
            link(dve.tensor_tensor(vg, vg, mean, ALU.subtract))
            link(dve.tensor_tensor(sg, vg, vg, ALU.mult))
            link(dve.tensor_reduce(stats[:, 1, :], sg, AX.X, ALU.add))
            dve.tensor_scalar(stats[:, 1, :], stats[:, 1, :], 1.0 / SG_HD, EPS, ALU.mult, ALU.add).then_inc(to_root, 1)
            dve.wait_ge(rooted, 1)
            link(dve.reciprocal(stats[:, 1, :], stats[:, 1, :]))
            link(dve.tensor_tensor(vg, vg, var, ALU.mult))
            for i, op in enumerate((ALU.mult, ALU.add)):
                link(dve.tensor_tensor(v, v, gb[:, i:i + 1, :].to_broadcast((P, nb, SG_WIDTH)), op))
            dve.sem_inc(normed, 1)
            dve.wait_ge(mixed, 1)
            for t in range(n_t):
                dve.wait_ge(copied, 7 + t)
                dve.tensor_tensor(mix[:, HG_HEADS + 2 + t, :],
                                  k.ps[:, 4 + 2 * t:6 + 2 * t, :].rearrange("p b n -> p (b n)"), u[:, t, :], ALU.mult)


def stage_hgrn(k):
    nc, ins = k.nc, k.ins
    at = [B_FREE]

    def take(*shape):
        v = k.ar(at[0], *shape)
        at[0] += int(np.prod(shape))
        return v

    raw_at = at[0]; take(KD, P)
    split_at = at[0]; take(2, KD, P)
    vals = take(2, NCH, P)
    q = take(2, T)
    keys, b = take(2, TT), take(2, TT)
    x = take(2, T)
    att, qh = take(T), take(T)
    kh = take(NCH, P)
    kh_t = take(NCH, P)
    z, l1 = (t.rearrange("p a b -> p (a b)") for t in (kh, kh_t))
    states = take(T // CHUNK, P)
    state0 = take(P)
    chunk_decay = take(NCH)
    root = take(T)
    assert at[0] <= ARENA - TT - 1
    starts = k.chunk_starts[:, :]
    mix = k.ar(B_MIX, KD, T)
    NL = len(LEVELS)
    units = [(h, d) for h in range(HG_HEADS) for d in range(2)]
    last_unit = len(units) - 1

    w_src = ins["w_in_2"].rearrange("o (k p) n -> p (o k) n", p=P)
    stream = WeightStream(k, [[w_src[:, :, s * HG_WIDTH + h * P:s * HG_WIDTH + (h + 1) * P]]
                              for h in range(HG_HEADS) for s in (0, 1, 3, 2, 4)], None, raw_at, split_at, n_raw=1)

    def tile_of(n, piece):
        h, d = units[n]
        return (5 * h + 3 + (0, 0, 1)[piece], piece > 0) if d else (5 * h + (0, 0, 1, 1, 2)[piece], piece in (1, 3, 4))

    def pieces(n):
        return 5 if units[n][1] == 0 else 3

    jobs = [(0, "front", i) for i in range(5)]
    for n, (h, d) in enumerate(units):
        front = [(n + 1, "front", i) for i in range(pieces(n + 1))] if n < last_unit else []
        jobs += [(n, "kt", 0), (n, "kt", 1)] + front[0:1] + ([(n, "ss", 0)] if d == 0 and h else []) + \
                [(n, "kv", 0), (n, "kv", 1), (n, "level", NL)] + front[1:2] + [(n, "level", 0)] + front[2:3] + \
                [(n, "level", 1)] + front[3:4] + [(n, "level", 2)] + front[4:5] + [(n, "level", l) for l in range(3, NL)]
    jobs.append((last_unit + 1, "ss", 0))

    def slot(job):
        i = jobs.index(job)
        return i % 3, i // 3

    def banks(job):
        s, _ = slot(job)
        return k.ps[:, 2 * s:2 * s + 2, :].rearrange("p b n -> p (b n)")

    made = [k.sem(f"made{i}") for i in range(3)]
    read = [k.sem(f"read{i}") for i in range(3)]

    def wait_free(pe, job):
        s, use = slot(job)
        if use >= 1:
            pe.wait_ge(read[s], use)

    def wait_made(eng, job):
        s, use = slot(job)
        eng.wait_ge(made[s], use + 1)

    def x_tokens(t):
        return t[:, CTX:TT]

    def halves_of(v, m):
        r = v.rearrange("p (b h r) -> p b h r", h=2, r=m)
        return r[:, :, 0, :], r[:, :, 1, :]

    def buffer(n, l):
        return (NL * n + l) % 2

    (silu_done, q_scaled, v_done, l_ready, sp_ready, k_raw, lt_ready, k_ready, b_ready, kh_sub, kh_exp, kh_ready,
     kt_done, g_exp, qh_exp, qh_ready, sub_done, exp_done, xk_ready, xq_ready, selected, inter_made, o_made, sq_done,
     root_ready, o_free, a_ord, v_ord, states_ready) = map(k.sem, (
         "silu_done", "q_scaled", "v_done", "l_ready", "sp_ready", "k_raw", "lt_ready", "k_ready", "b_ready", "kh_sub",
         "kh_exp", "kh_ready", "kt_done", "g_exp", "qh_exp", "qh_ready", "sub_done", "exp_done", "xk_ready", "xq_ready",
         "selected", "inter_made", "o_made", "sq_done", "root_ready", "o_free", "a_ord", "v_ord", "states_ready"))
    o_ps = k.ps[:, 6:8, :].rearrange("p b n -> p (b n)")
    mask_u = k.masks[:, :, :, :].bitcast(U32)

    with nc.Block() as block:
        @block.sync
        def _(sp):
            for n in range(5 * HG_HEADS):
                stream.load(sp, n)

        @block.tensor
        def _(pe):
            def front(n, piece):
                if n > last_unit or piece >= pieces(n):
                    return
                h, d = units[n]
                job = (n, "front", piece)
                tile, _ = tile_of(n, piece)
                stream.ready(pe, tile)
                wait_free(pe, job)
                if d == 0 and piece < 2:
                    for i, c in enumerate(range(8) if piece == 0 else range(8, NCH)):
                        last = split_matmuls(pe, [banks(job)[:, i * P:(i + 1) * P]],
                                             lambda s, kt: k.hT[:, s, kt, c * P:(c + 1) * P],
                                             lambda s, kt, i: stream.part(tile, s, kt), KD)
                else:
                    gate = piece == (2 if d == 0 else 0) or piece == (3 if d == 0 else 1)
                    first, end = (0, T) if piece == (2 if d == 0 else 0) else (T, TT) if gate else (CTX, TT)
                    spans = [(a, min(a + HALF, end)) for a in range(first, end, HALF)]
                    last = split_matmuls(pe, [banks(job)[:, a - first:e - first] for a, e in spans],
                                         lambda s, kt: stream.part(tile, s, kt),
                                         lambda s, kt, i: k.hT[:, s, kt, spans[i][0]:spans[i][1]], KD)
                last.then_inc(made[slot(job)[0]], 1)

            def chunk_job(job, chunks, fn):
                wait_free(pe, job)
                for i, c in enumerate(chunks):
                    last = fn(banks(job)[:, i * P:(i + 1) * P], c)
                last.then_inc(made[slot(job)[0]], 1)

            def level(n, l):
                pe.wait_ge(xk_ready, NL * n + l + 1)
                pe.wait_ge(xq_ready, NL * n + l + 1)
                v = x[:, buffer(n, l), :]
                chunk_job((n, "level", l), range(T // P), lambda out, c: pe.matmul(
                    out, v[:, c * P:(c + 1) * P], v[:, c * P:(c + 1) * P], start=True, stop=True))

            def sum_of_squares(n, h):
                pe.wait_ge(sq_done, h)
                job = (n, "ss", 0)
                wait_free(pe, job)
                for half in range(2):
                    last = pe.matmul(banks(job)[:, half * HALF:(half + 1) * HALF], k.ones[:, :],
                                     root[:, half * HALF:(half + 1) * HALF], start=True, stop=True)
                last.then_inc(made[slot(job)[0]], 1)

            for piece in range(5):
                front(0, piece)
            for n, (h, d) in enumerate(units):
                halves = (range(8), range(8, NCH))
                pe.wait_ge(kh_ready, n + 1)
                for i in range(2):
                    chunk_job((n, "kt", i), halves[i], lambda out, c: pe.transpose(out, kh[:, c, :], k.ident[:, :]))
                front(n + 1, 0)
                if d == 0 and h:
                    sum_of_squares(n, h)
                pe.wait_ge(kt_done, 2 * n + 2)
                pe.wait_ge(v_done, 2 * h + 2)
                for i in range(2):
                    chunk_job((n, "kv", i), halves[i], lambda out, c: pe.matmul(
                        out, kh_t[:, c, :], vals[:, h % 2, c, :], start=True, stop=True))
                pe.wait_ge(k_ready, n + 1)
                pe.wait_ge(q_scaled, h + 1)
                chunk_job((n, "level", NL), range(T // P), lambda out, c: pe.matmul(
                    out, keys[:, n % 2, CTX + c * P:CTX + (c + 1) * P], q[:, h % 2, c * P:(c + 1) * P],
                    start=True, stop=True))
                front(n + 1, 1)
                for l in range(3):
                    level(n, l)
                    if l < 2:
                        front(n + 1, l + 2)
                pe.wait_ge(states_ready, n + 1)
                pe.wait_ge(qh_ready, n + 1)
                if d == 0 and h:
                    pe.wait_ge(o_free, h)
                for c in range(T // P):
                    last = pe.matmul(o_ps[:, c * P:(c + 1) * P], states[:, c, :], qh[:, c * P:(c + 1) * P],
                                     start=d == 0 and c % 4 == 0, stop=False, skip_group_check=True)
                last.then_inc(inter_made, 1)
                front(n + 1, 4)
                for l in range(3, NL):
                    level(n, l)
                pe.wait_ge(selected, n + 1)
                for c in range(T // P):
                    last = pe.matmul(o_ps[:, c * P:(c + 1) * P], vals[:, h % 2, CCH + c, :], att[:, c * P:(c + 1) * P],
                                     start=False, stop=d == 1, skip_group_check=True)
                last.then_inc(o_made, 1)
            sum_of_squares(last_unit + 1, HG_HEADS)

        @block.scalar
        def _(act):
            link = chained(act, a_ord)

            def take_out(job, dst, func=ACT.Copy):
                wait_made(act, job)
                act.activation(dst, banks(job)[:, 0:int(np.prod(dst.shape[1:]))], func).then_inc(read[slot(job)[0]], 1)

            def signal(job, done):
                s, use = slot(job)
                act.wait_ge(read[s], use + 1)
                act.sem_inc(done, 1)

            def front(n, piece):
                if n > last_unit or piece >= pieces(n):
                    return
                h, d = units[n]
                job = (n, "front", piece)
                if d == 0 and piece < 2:
                    chunks = (slice(0, 8), slice(8, NCH))[piece]
                    take_out(job, vals[:, h % 2, chunks, :].rearrange("p a b -> p (a b)"))
                    act.wait_ge(read[slot(job)[0]], slot(job)[1] + 1)
                    act.sem_inc(v_done, 1)
                elif piece == (2 if d == 0 else 0):
                    take_out(job, z[:, 0:T])
                elif piece == (3 if d == 0 else 1):
                    take_out(job, z[:, T:TT])
                else:
                    take_out(job, q[:, h % 2, :] if d == 0 else mix[:, h, :], ACT.Silu)
                    signal(job, silu_done)
                tile, done = tile_of(n, piece)
                if done and tile + 2 < 5 * HG_HEADS:
                    stream.hi(act, tile + 2)

            def softplus_parts(n):
                if n > last_unit:
                    return
                job = (n, "front", 3 if units[n][1] == 0 else 1)
                act.wait_ge(read[slot(job)[0]], slot(job)[1] + 1)
                if n:
                    wait_made(act, (n - 1, "kv", 1))
                link(act.activation(l1, z, ACT.Abs))
                link(act.activation(l1, l1, ACT.Exp, scale=-1.0))
                act.activation(l1, l1, ACT.Ln, bias=1.0).then_inc(l_ready, 1)

            def forget_parts(n):
                if n > last_unit:
                    return
                h, d = units[n]
                kk = keys[:, n % 2, :]
                act.wait_ge(sp_ready, n + 1)
                act.activation(kk, kk, ACT.Exp, scale=-1.0).then_inc(k_raw, 1)
                link(act.activation(z, z, ACT.Exp, scale=-1.0))
                act.activation(z, z, ACT.Ln, bias=1.0, scale=k.lower[:, h + d * HG_HEADS:h + d * HG_HEADS + 1])\
                    .then_inc(lt_ready, 1)

            def level(n, l):
                act.wait_ge(sub_done, NL * n + l + 1)
                v = x[:, buffer(n, l), :]
                act.activation(v, v, ACT.Exp).then_inc(exp_done, 1)

            def decays(n):
                if n > last_unit:
                    return
                d = units[n][1]
                act.wait_ge(kh_sub, n + 1)
                act.activation(z, z, ACT.Exp).then_inc(kh_exp, 1)
                level(n, 0)
                bn = b[:, n % 2, :]
                edge = bn.rearrange("p (c r) -> p c r", r=CHUNK)[:, :, CHUNK - 1 if d == 0 else 0]
                if n:
                    act.wait_ge(states_ready, n)
                act.activation(chunk_decay, edge, ACT.Exp).then_inc(g_exp, 1)
                if n:
                    act.wait_ge(inter_made, n)
                act.activation(qh, x_tokens(bn), ACT.Exp).then_inc(qh_exp, 1)

            def squares(h):
                act.wait_ge(o_made, 2 * h + 2)
                act.activation(root, o_ps, ACT.Square).then_inc(sq_done, 1)

            def inverse_root(n):
                job = (n, "ss", 0)
                wait_made(act, job)
                act.activation(root, banks(job), ACT.Ln, bias=k.eps[:, 0:1], scale=1.0 / HG_DK).then_inc(read[slot(job)[0]], 1)
                act.wait_ge(read[slot(job)[0]], slot(job)[1] + 1)
                act.activation(root, root, ACT.Exp, scale=-0.5).then_inc(root_ready, 1)

            stream.hi(act, 0)
            stream.hi(act, 1)
            for piece in range(5):
                front(0, piece)
            softplus_parts(0)
            forget_parts(0)
            decays(0)
            for n, (h, d) in enumerate(units):
                take_out((n, "kt", 0), kh_t[:, 0:8, :].rearrange("p a b -> p (a b)"))
                signal((n, "kt", 0), kt_done)
                take_out((n, "kt", 1), kh_t[:, 8:NCH, :].rearrange("p a b -> p (a b)"))
                signal((n, "kt", 1), kt_done)
                if d == 0 and h:
                    squares(h - 1)
                level(n, 1)
                front(n + 1, 0)
                if d == 0 and h:
                    inverse_root(n)
                front(n + 1, 1)
                level(n, 2)
                front(n + 1, 2)
                level(n, 3)
                front(n + 1, 3)
                softplus_parts(n + 1)
                level(n, 4)
                front(n + 1, 4)
                level(n, 5)
                forget_parts(n + 1)
                level(n, 6)
                decays(n + 1)
            squares(HG_HEADS - 1)
            inverse_root(last_unit + 1)

        @block.gpsimd
        def _(pool):
            for n, (h, d) in enumerate(units):
                qn = q[:, h % 2, :]
                pool.wait_ge(q_scaled, h + 1)
                for l in range(NL):
                    pool.wait_ge(exp_done, NL * n + l + 1)
                    side = halves_of(x[:, buffer(n, l), :], LEVELS[l])[1 - d]
                    pool.tensor_tensor(side, side, halves_of(qn, LEVELS[l])[1 - d], ALU.mult).then_inc(xq_ready, 1)
                    if l == 0:
                        pool.wait_ge(qh_exp, n + 1)
                        pool.tensor_tensor(qh, qh, qn, ALU.mult).then_inc(qh_ready, 1)

        @block.vector
        def _(dve):
            link = chained(dve, v_ord)

            def weights_lo(n, piece):
                if n > last_unit or piece >= pieces(n):
                    return
                tile, done = tile_of(n, piece)
                if done and tile + 2 < 5 * HG_HEADS:
                    stream.lo(dve, tile + 2)

            def scale_q(n):
                if n <= last_unit and units[n][1] == 0:
                    h = units[n][0]
                    dve.wait_ge(silu_done, 2 * h + 1)
                    dve.tensor_scalar(q[:, h % 2, :], q[:, h % 2, :], HG_DK ** -0.5, None, ALU.mult).then_inc(q_scaled, 1)

            def softplus(n):
                if n > last_unit:
                    return
                dve.wait_ge(l_ready, n + 1)
                link(dve.scalar_tensor_tensor(b[:, n % 2, :], z, 0.0, l1, ALU.min, ALU.subtract))
                dve.scalar_tensor_tensor(keys[:, n % 2, :], z, 0.0, l1, ALU.max, ALU.add)
                dve.tensor_scalar(z, z, -44.0, None, ALU.max).then_inc(sp_ready, 1)

            def forget(n):
                if n > last_unit:
                    return
                h, d = units[n]
                bn, kn = b[:, n % 2, :], keys[:, n % 2, :]
                dve.wait_ge(k_raw, n + 1)
                dve.tensor_scalar(kn, kn, k.one_less[:, h + d * HG_HEADS:h + d * HG_HEADS + 1], None, ALU.mult)\
                   .then_inc(k_ready, 1)
                dve.wait_ge(lt_ready, n + 1)
                link(dve.tensor_tensor(bn, bn, z, ALU.add))
                link(dve.tensor_scalar(bn, bn, LN_TINY, 0.0, ALU.max, ALU.min))
                if d == 0:
                    scan = dve.tensor_tensor_scan(bn, starts[:, 0:TT], bn, 0.0, ALU.mult, ALU.add)
                else:
                    scan = dve.tensor_tensor_scan(bn[:, ::-1], starts[:, 1:TT + 1][:, ::-1], bn[:, ::-1], 0.0,
                                                  ALU.mult, ALU.add)
                scan.then_inc(b_ready, 1)

            def key_distance(n):
                if n > last_unit:
                    return
                dve.wait_ge(b_ready, n + 1)
                bc = b[:, n % 2, :].rearrange("p (c r) -> p c r", r=CHUNK)
                edge = bc[:, :, CHUNK - 1:CHUNK] if units[n][1] == 0 else bc[:, :, 0:1]
                dve.tensor_tensor(kh, edge.to_broadcast((P, NCH, CHUNK)), bc, ALU.subtract).then_inc(kh_sub, 1)

            def decayed_keys(n):
                if n > last_unit:
                    return
                dve.wait_ge(k_ready, n + 1)
                dve.wait_ge(kh_exp, n + 1)
                dve.tensor_tensor(kh, kh, keys[:, n % 2, :].rearrange("p (c r) -> p c r", r=CHUNK), ALU.mult)\
                   .then_inc(kh_ready, 1)

            def subtract(n, l):
                if n > last_unit:
                    return
                m = LEVELS[l]
                i = NL * n + l - 2
                if i >= 0:
                    wait_made(dve, (i // NL, "level", i % NL))
                left, right = halves_of(x_tokens(b[:, n % 2, :]), m)
                xl, xr = halves_of(x[:, buffer(n, l), :], m)
                if units[n][1] == 0:
                    mid = left[:, :, m - 1:m].to_broadcast((P, T // (2 * m), m))
                    dve.tensor_tensor(xl, mid, left, ALU.subtract)
                    last = dve.tensor_tensor(xr, right, mid, ALU.subtract)
                else:
                    mid = right[:, :, 0:1].to_broadcast((P, T // (2 * m), m))
                    dve.tensor_tensor(xl, left, mid, ALU.subtract)
                    last = dve.tensor_tensor(xr, mid, right, ALU.subtract)
                last.then_inc(sub_done, 1)

            def weigh(n, l):
                d = units[n][1]
                dve.wait_ge(exp_done, NL * n + l + 1)
                side = halves_of(x[:, buffer(n, l), :], LEVELS[l])[d]
                dve.tensor_tensor(side, side, halves_of(x_tokens(keys[:, n % 2, :]), LEVELS[l])[d], ALU.mult)\
                   .then_inc(xk_ready, 1)

            def select(n, l):
                job = (n, "level", l)
                mask = mask_u[:, units[n][1], l, :].unsqueeze(1).to_broadcast((P, T // P, P))
                wait_made(dve, job)
                s_, use = slot((n, "level", NL if l == 0 else l - 1))
                dve.wait_ge(read[s_], use + 1)
                dve.copy_predicated(att.rearrange("p (c r) -> p c r", r=P), mask,
                                    banks(job).rearrange("p (c r) -> p c r", r=P)).then_inc(read[slot(job)[0]], 1)

            def diagonal(n):
                job = (n, "level", NL)
                wait_made(dve, job)
                if n:
                    dve.wait_ge(o_made, n)
                dve.tensor_tensor(att.rearrange("p (c r) -> p c r", r=P), banks(job).rearrange("p (c r) -> p c r", r=P),
                                  k.ident[:, :].unsqueeze(1).to_broadcast((P, T // P, P)), ALU.mult)\
                   .then_inc(read[slot(job)[0]], 1)

            def chain_states(n):
                d = units[n][1]
                dve.wait_ge(g_exp, n + 1)
                for i in range(2):
                    wait_made(dve, (n, "kv", i))
                kv = lambda c: banks((n, "kv", c // 8))[:, (c % 8) * P:(c % 8 + 1) * P]
                order = list(range(NCH)) if d == 0 else list(range(CCH - 1, -1, -1)) + list(range(NCH - 1, CCH - 1, -1))
                if n:
                    dve.wait_ge(inter_made, n)
                prev = None
                for i, c in enumerate(order[:-1]):
                    to = order[i + 1]
                    dst = states[:, to - CCH, :] if to >= CCH else state0
                    if prev is None:
                        link(dve.tensor_copy(dst, kv(c)))
                    else:
                        link(dve.scalar_tensor_tensor(dst, prev, chunk_decay[:, c:c + 1], kv(c), ALU.mult, ALU.add))
                    prev = dst
                dve.sem_inc(states_ready, 1)
                for i in range(2):
                    dve.sem_inc(read[slot((n, "kv", i))[0]], 1)

            def finish(h):
                dve.wait_ge(root_ready, h + 1)
                link(dve.tensor_tensor(root, o_ps, root, ALU.mult))
                dve.sem_inc(o_free, 1)
                dve.wait_ge(silu_done, 2 * h + 2)
                dve.scalar_tensor_tensor(mix[:, h, :], root, k.col("hg_norm_g_2"), mix[:, h, :], ALU.mult, ALU.mult)

            stream.lo(dve, 0)
            stream.lo(dve, 1)
            for piece in range(5):
                weights_lo(0, piece)
            scale_q(0)
            softplus(0)
            forget(0)
            key_distance(0)
            subtract(0, 0)
            decayed_keys(0)
            for n, (h, d) in enumerate(units):
                subtract(n, 1)
                weigh(n, 0)
                chain_states(n)
                if d == 0 and h:
                    finish(h - 1)
                diagonal(n)
                for l in range(1, NL):
                    if l + 1 < NL:
                        subtract(n, l + 1)
                    weigh(n, l)
                    select(n, l - 1)
                    if l == 2:
                        weights_lo(n + 1, 1)
                    if l == 3:
                        weights_lo(n + 1, 2)
                        softplus(n + 1)
                    if l == 4:
                        weights_lo(n + 1, 3)
                    if l == 5:
                        weights_lo(n + 1, 4)
                        scale_q(n + 1)
                        forget(n + 1)
                key_distance(n + 1)
                subtract(n + 1, 0)
                select(n, NL - 1)
                s_, use = slot((n, "level", NL - 1))
                dve.wait_ge(read[s_], use + 1)
                dve.sem_inc(selected, 1)
                decayed_keys(n + 1)
            finish(HG_HEADS - 1)


def stage_starts(k):
    set_ = k.sem("starts_set")
    with k.nc.Block() as block:
        @block.gpsimd
        def _(pool):
            pool.memset(k.chunk_starts[:, :], 1.0).then_inc(set_, 1)
            pool.wait_ge(set_, 1)
            pool.memset(k.chunk_starts[:, 0:TT + 1:CHUNK], 0.0).then_inc(set_, 1)


def stage_mix_norm2(k):
    pass


def stage_out2(k):
    stage_out_projection(k, "w_out_2", lambda n: k.mod2[:, 2, n, 0:1], ALPHA, src_at=B_MIX)


def stage_ln(k, g, b):
    stage_norm(k, 0, lambda t: k.xT[:, t, :], lambda t: k.xT[:, t, :], KD, D,
               shift=lambda t: k.col(b, t), weight=lambda t: k.col(g, t), scale=None, centre=True, tmp_at=0)


def stage_ln1(k):
    stage_ln(k, "ln1_g_2", "ln1_b_2")


def stage_modulate_ffn2(k):
    stage_norm(k, 0, lambda t: k.xT[:, t, :], lambda t: k.ar(4 * T, KD, T)[:, t, :], KD, D,
               shift=lambda t: k.mod2[:, 3, t, 0:1], weight=lambda t: k.gain[:, 0, t:t + 1],
               scale=(k.mod2[:, 4, :, 0], None), centre=True, tmp_at=0, split=lambda t, s: k.hT[:, s, t, 0:T])


def stage_up2(k):
    ffn_up(k, "ffn_up_2", 8, conv_grid, finish_gelu)


def stage_down2(k):
    ffn_down(k, "ffn_down_2", lambda j: k.mod2[:, 5, bass.ds(j, 1), 0], ALPHA)


def stage_ln2(k):
    stage_ln(k, "ln2_g_2", "ln2_b_2")


def stage_store(k):
    nc = k.nc
    rows = k.ar(0, T // P, D)
    turned, copied, stored = map(k.sem, ("turned", "copied", "stored"))
    with nc.Block() as block:
        @block.tensor
        def _(pe):
            for n in range(2 * (T // P)):
                t, g = divmod(n, 2)
                if n >= 8:
                    pe.wait_ge(copied, n - 7)
                for i in range(4):
                    f = 4 * g + i
                    last = pe.transpose(k.ps[:, n % 8, i * P:(i + 1) * P], k.xT[:, f, t * P:(t + 1) * P], k.ident[:, :])
                last.then_inc(turned, 1)

        @block.vector
        def _(dve):
            for n in range(2 * (T // P)):
                t, g = divmod(n, 2)
                dve.wait_ge(turned, n + 1)
                dve.tensor_copy(rows[:, t, g * HALF:(g + 1) * HALF], k.ps[:, n % 8, :]).then_inc(copied, 1)

        @block.sync
        def _(sp):
            for t in range(T // P):
                sp.wait_ge(copied, 2 * t + 2)
                sp.dma_start(k.out[0, t * P:(t + 1) * P, :], rows[:, t, :]).then_inc(stored, 16)
            sp.wait_ge(stored, 16 * (T // P))


STAGES = [
    stage_load, stage_modulation,
    stage_norm1, stage_project, stage_qk_norm, stage_bias, stage_attention, stage_ssm_params, stage_ssm, stage_glu,
    stage_mixer_norms, stage_out1, stage_norm2, stage_up1, stage_down1,
    stage_starts, stage_context, stage_modulate2, stage_short_conv, stage_spatial_gate, stage_hgrn,
    stage_out2, stage_ln1, stage_modulate_ffn2, stage_up2, stage_down2, stage_ln2, stage_store,
]


MAX_STAGE_SEMS = 90


def build_program(nc, ins, out):
    with ExitStack() as ctx:
        k = Kernel(nc, ins, out, ctx)
        for stage in STAGES:
            stage(k)
            if len(k.stage_sems) > MAX_STAGE_SEMS:
                k.release_sems()
        k.stage_ctx.close()


def lay_out(inputs):
    arrays = {name: np.ascontiguousarray(a) for name, a in inputs.items()}
    arrays["bucket_sel"] = bucket_selection()
    return arrays


def kernel(**inputs):
    import concourse.bacc as bacc
    from concourse.bass_utils import run_bass_kernel_spmd

    nc = bacc.Bacc("TRN2", target_bir_lowering=False, num_devices=1)
    arrays = lay_out(inputs)
    ins = {name: nc.dram_tensor(f"{name}_dram", a.shape, mybir.dt.from_np(a.dtype), kind="ExternalInput").ap()
           for name, a in arrays.items()}
    out = nc.dram_tensor("out_dram", (1, T, D), F32, kind="ExternalOutput").ap()
    build_program(nc, ins, out)
    r = run_bass_kernel_spmd(nc, [{f"{name}_dram": a for name, a in arrays.items()}], core_ids=[0])
    return r.results[0]["out_dram"]
```

```python
import math
from contextlib import ExitStack

import numpy as np

import concourse.bass as bass
from concourse import mybir

F32 = mybir.dt.float32
BF16 = mybir.dt.bfloat16
I32 = mybir.dt.int32
U32 = mybir.dt.uint32
ALU = mybir.AluOpType
ACT = mybir.ActivationFunctionType
AX = mybir.AxisListType

P = 128
T = 1024
HALF = 512
D = 1024
KD = D // P
EPS = 1e-6

D_SSM, SSM_GROUP, N_GROUPS, SSM_STATE = 512, 16, 32, 64
U_TILES = D_SSM // P
S_TILES = N_GROUPS * SSM_STATE // P
SPU = S_TILES // U_TILES
HEAD_DIM, N_Q, N_KV = 64, 8, 2
D_ATTN = N_Q * HEAD_DIM
A_TILES = D_ATTN // P
KV_DIM = N_KV * HEAD_DIM
D_IN = D_SSM + D_ATTN + 2 * KV_DIM
WINDOW = 128
NB = T // WINDOW
N_BUCKETS, MAX_DISTANCE = 32, 128
NEG_INF = -1e30
D_FF = 2816
FT = D_FF // P
TAB = 32

GRID_W = 64
GRID_H = T // GRID_W
CTX = 256
TT = CTX + T
HG_DK, HG_HEADS, HG_WIDTH = 128, 4, 512
SC_WIDTH, SG_WIDTH, SG_HEADS, SG_HD = 256, 256, 4, 64
IN2 = 5 * HG_WIDTH + 3 * SC_WIDTH + 2 * SG_WIDTH
O_Q, O_G, O_SC = 3 * HG_WIDTH, 4 * HG_WIDTH, 5 * HG_WIDTH
O_SG = O_SC + 3 * SC_WIDTH
ALPHA = 2.0 ** 0.25
TINY = 1e-30
CHUNK = 128
LEVELS = [64, 32, 16, 8, 4, 2, 1]
NCH = TT // CHUNK
CCH = CTX // CHUNK


def bucket_of(n):
    n = np.maximum(n, 0)
    exact = N_BUCKETS // 2
    log_part = np.log(np.maximum(n, 1) / exact) / math.log(MAX_DISTANCE / exact)
    large = np.minimum(exact + (log_part * (N_BUCKETS - exact)).astype(np.int32), N_BUCKETS - 1)
    return np.where(n < exact, n, large).astype(np.int32)


RB = 384


def bucket_selection():
    sel = np.zeros((N_BUCKETS + 1, RB), np.float32)
    for i in range(RB):
        dist = 2 * WINDOW - 1 - i
        if 0 <= dist < WINDOW:
            sel[bucket_of(np.array([dist]))[0], i] = 1.0
        else:
            sel[N_BUCKETS, i] = NEG_INF
    return sel


VECTORS = [
    ("c", 8), ("c_2", 8), ("c_ctx_2", 8), ("b_mod", 48), ("norm1_w", 8), ("norm2_w", 8),
    ("lam_re", 16), ("lam_im", 16), ("ssm_d", 4), ("b_glu", 4),
    ("ada_b_2", 48), ("out_norm_ssm", 4), ("out_norm_attn", 4), ("conv_b", 44), ("conv_w", 132),
    ("q_norm_w", 1), ("k_norm_w", 1),
    ("hg_lb_2", 8), ("hg_norm_g_2", 1), ("sc_conv_w_2", 6), ("ln1_g_2", 8), ("ln1_b_2", 8),
    ("ln2_g_2", 8), ("ln2_b_2", 8), ("ffn_conv_b_2", 22), ("ffn_conv_w_2", 198),
]
ROW_OF, _r = {}, 0
for _name, _n in VECTORS:
    ROW_OF[_name] = _r
    _r += _n
N_ROWS = _r
N_VT = -(-N_ROWS // P)

ARENA = 31400


class Kernel:

    def __init__(self, nc, ins, out, ctx):
        self.nc, self.ins, self.out, self.ctx = nc, ins, out, ctx
        self.n_sems = 0
        self.stage_ctx, self.stage_sems = ctx, []
        self.vec = self.sb("vec", [P, N_VT * P])
        self.ident = self.sb("ident", [P, P])
        self.ones = self.sb("ones", [P, P])
        self.halves = self.sb("halves", [P, P])
        self.mod1 = self.sb("mod1", [P, 6, KD])
        self.mod2 = self.sb("mod2", [P, 6, KD, 2])
        self.gain = self.sb("gain", [P, 2, KD])
        self.cact = self.sb("cact", [P, 3, KD])
        self.xT = self.sb("xT", [P, KD, T])
        self.hT = self.sb("hT", [P, 2, KD, TT], BF16)
        self.eps = self.sb("eps", [P, 1])
        self.arena = self.sb("arena", [P, ARENA])
        self.sink = self.sb("sink", [P, N_Q])
        self.ssm_neg = self.sb("ssm_neg", [P, 5, S_TILES])
        self.masks = self.sb("masks", [P, 2, len(LEVELS), P])
        self.lower = self.sb("lower", [P, 2 * HG_HEADS])
        self.one_less = self.sb("one_less", [P, 2 * HG_HEADS])
        self.raw_up = views_hT(self)(0, 2, KD, TT // 2)[:, :, :, T // 2:TT // 2]
        self.ps = ctx.enter_context(nc.psum_tensor("ps", [P, 8, HALF], F32))
        self.x_back = self.sem("x_back")
        self.stage_ctx, self.stage_sems = ExitStack(), []

    def sb(self, name, shape, dt=F32):
        return self.ctx.enter_context(self.nc.sbuf_tensor(name, shape, dt))

    def sem(self, name):
        self.n_sems += 1
        s = self.stage_ctx.enter_context(self.nc.semaphore(f"{name}_{self.n_sems}"))
        self.stage_sems.append(s)
        return s

    def release_sems(self):
        with self.nc.Block() as block:
            @block.sync
            def _(sp):
                for s in self.stage_sems:
                    sp.sem_clear(s)
        self.stage_ctx.close()
        self.stage_ctx, self.stage_sems = ExitStack(), []

    def col(self, name, i=0, n=1):
        r = ROW_OF[name] + i
        return self.vec[:, r:r + n]

    def ar(self, at, *shape):
        n = int(np.prod(shape))
        assert at + n <= ARENA, (at, n)
        v = self.arena[:, at:at + n]
        names = "abcd"[:len(shape)]
        if len(shape) == 1:
            return v
        return v.rearrange(f"p ({' '.join(names)}) -> p {' '.join(names)}",
                           **{x: s for x, s in zip(names, shape)})


PASSES = ((0, 0), (0, 1), (1, 0))


def split_matmuls(pe, outs, lhs, rhs, n_k, start=True, stop=True, before=None):
    for kt in range(n_k):
        if before is not None:
            before(kt)
        for a, b in PASSES:
            for i, out in enumerate(outs):
                last = pe.matmul(out, lhs(a, kt), rhs(b, kt, i), start=start and kt == 0 and (a, b) == (0, 0),
                                 stop=stop and kt == n_k - 1 and (a, b) == PASSES[-1], skip_group_check=True)
    return last


class WeightStream:

    def __init__(self, k, sources, used, raw_at, split_at, n_k=KD, width=P, whole=(), n_raw=2):
        self.sources, self.used, self.n_k, self.width, self.whole = sources, used, n_k, width, whole
        self.n_raw = n_raw
        self.exact = k.ar(split_at, 2, n_k, width)
        self.arrived = [16 * sum(len(x) for x in sources[n % n_raw:n + 1:n_raw]) for n in range(len(sources))]
        self.raw = k.ar(raw_at, n_raw, n_k, width)
        self.parts = k.ar(split_at, 2, n_k, width).rearrange("p a k n -> p (a k n)").bitcast(BF16)\
            .rearrange("p (r s k n) -> p r s k n", r=2, s=2, k=n_k)
        self.loaded = [k.sem(f"weights_in{i}") for i in range(n_raw)]
        self.hi_done, self.lo_done = map(k.sem, ("hi_done", "lo_done"))

    def load(self, sp, n):
        r = n % self.n_raw
        if n >= self.n_raw:
            sp.wait_ge(self.lo_done, n - self.n_raw + 1)
        w = self.width // len(self.sources[n])
        for i, piece in enumerate(self.sources[n]):
            sp.dma_start(self.raw[:, r, :, i * w:(i + 1) * w], piece).then_inc(self.loaded[r], 16)

    def hi(self, act, n):
        if n >= 2 and self.used is not None:
            act.wait_ge(self.used, n - 1)
        act.wait_ge(self.loaded[n % self.n_raw], self.arrived[n])
        act.activation(self.exact[:, n % 2] if n in self.whole else self.parts[:, n % 2, 0], self.raw[:, n % self.n_raw], ACT.Copy)\
           .then_inc(self.hi_done, 1)

    def lo(self, dve, n):
        dve.wait_ge(self.hi_done, n + 1)
        if n in self.whole:
            if n >= 1:
                dve.wait_ge(self.lo_done, n)
            dve.sem_inc(self.lo_done, 1)
            return
        dve.tensor_tensor(self.parts[:, n % 2, 1], self.raw[:, n % self.n_raw], self.parts[:, n % 2, 0], ALU.subtract)\
           .then_inc(self.lo_done, 1)

    def ready(self, pe, n):
        pe.wait_ge(self.lo_done, n + 1)

    def part(self, n, part, kt):
        return self.parts[:, n % 2, part, kt, :]


def chained(eng, sem, start=0):
    count = [start]

    def link(instruction):
        count[0] += 1
        instruction.then_inc(sem, 1)
        eng.wait_ge(sem, count[0])

    return link


M_W = N_VT * P + T // P * D
M_ROW = M_W + 2 * KD * D


def stage_load(k):
    nc, ins = k.nc, k.ins
    raw = k.ar(0, N_VT, P)
    x_rows = k.ar(N_VT * P, T // P, D)
    w = k.ar(M_W, 2, KD, D)
    w_src = ins["w_mod"].rearrange("o (k p) (m n) -> m p (o k) n", p=P, m=6)
    mod_row = k.ar(M_ROW, 2 * D)[0:1, :]
    rows_in, made, turned, copied, silu_c, mod_made, row_copied, mod_turned = map(k.sem, (
        "rows_in", "made", "turned", "copied", "silu_c", "mod_made", "row_copied", "mod_turned"))
    x_in = [k.sem(f"x_in{g}") for g in range(2)]
    w_in = [k.sem(f"w_in{i}") for i in range(8)]
    n_units = 2 * KD

    def row_view(name, n):
        a = ins[name]
        flat = a.rearrange(" ".join("abcd"[:len(a.shape)]) + " -> (" + " ".join("abcd"[:len(a.shape)]) + ")")
        return flat

    loads = []
    for name, n in VECTORS:
        flat, at, done = row_view(name, n), ROW_OF[name], 0
        while done < n:
            m = min(n - done, P - (at + done) % P)
            tile, row = divmod(at + done, P)
            if name in ("q_norm_w", "k_norm_w"):
                for half in range(2):
                    loads.append((raw[row:row + 1, tile, half * HEAD_DIM:(half + 1) * HEAD_DIM],
                                  flat.rearrange("(a b) -> a b", a=1)))
            else:
                loads.append((raw[row:row + m, tile, :],
                              flat[done * P:(done + m) * P].rearrange("(a b) -> a b", b=P)))
            done += m
    groups = [list(range(4 * g, 4 * g + 4)) for g in range(2)]

    with nc.Block() as block:
        @block.sync
        def _(sp):
            for t in range(T // P):
                sp.dma_start(x_rows[:, t, :], ins["x"][0, t * P:(t + 1) * P, :]).then_inc(x_in[t // 4], 16)
            sp.wait_ge(rows_in, 16 * len(loads))
            for i in range(8):
                m, kt = i // 4, 2 * (i % 4)
                sp.dma_start(w[:, m, kt:kt + 2, :], w_src[m][:, kt:kt + 2, :]).then_inc(w_in[i], 16)

        @block.gpsimd
        def _(pool):
            pool.memset(k.ident[:, :], 0.0).then_inc(made, 1)
            pool.memset(k.ones[:, :], 1.0).then_inc(made, 1)
            pool.memset(k.eps[:, :], EPS).then_inc(made, 1)
            pool.memset(k.halves[:, :], 0.0).then_inc(made, 1)
            pool.wait_ge(made, 4)
            pool.affine_select(out=k.ident[:, :], in_=k.ident[:, :], compare_op=ALU.not_equal, fill=1.0,
                               base=0, pattern=[[-1, P]], channel_multiplier=1).then_inc(made, 1)
            pool.wait_ge(made, 5)
            pool.memset(k.halves[0:64, 0:64], 1.0).then_inc(made, 1)
            pool.memset(k.halves[64:128, 64:128], 1.0).then_inc(made, 1)

        @block.scalar
        def _(act):
            for dst, src in loads:
                act.dma_start(dst, src).then_inc(rows_in, 16)
            act.wait_ge(copied, n_units + 2)
            act.activation(k.cact[:, :, :], k.vec[:, 0:3 * KD].rearrange("p (c f) -> p c f", c=3),
                           ACT.Silu).then_inc(silu_c, 1)
            for m in range(2):
                act.wait_ge(mod_made, m + 1)
                act.activation(mod_row[:, m * D:(m + 1) * D], k.ps[0:1, 2 + 2 * m:4 + 2 * m, :].rearrange("p b n -> p (b n)"),
                               ACT.Copy).then_inc(row_copied, 1)

        @block.tensor
        def _(pe):
            pe.wait_ge(made, 7)
            for unit in range(n_units):
                g, f = divmod(unit, KD)
                pe.wait_ge(x_in[g], 16 * 4)
                if unit >= 6:
                    pe.wait_ge(copied, unit - 5)
                for n, t in enumerate(groups[g]):
                    last = pe.transpose(k.ps[:, 2 + unit % 6, n * P:(n + 1) * P],
                                        x_rows[:, t, f * P:(f + 1) * P], k.ident[:, :])
                last.then_inc(turned, 1)
            pe.wait_ge(rows_in, 16 * len(loads))
            for v in range(N_VT):
                n = min(P, N_ROWS - v * P)
                last = pe.transpose(k.ps[:, v // 4, (v % 4) * P:(v % 4) * P + n],
                                    raw[0:n, v, :], k.ident[0:n, 0:n])
            last.then_inc(turned, 1)
            pe.wait_ge(silu_c, 1)
            for i in range(8):
                m = i // 4
                pe.wait_ge(w_in[i], 16)
                for kt in range(2 * (i % 4), 2 * (i % 4) + 2):
                    for half in range(2):
                        last = pe.matmul(k.ps[0:1, 2 + 2 * m + half, :], k.cact[:, 0, kt:kt + 1],
                                         w[:, m, kt, half * HALF:(half + 1) * HALF], start=kt == 0, stop=kt == KD - 1)
                if i % 4 == 3:
                    last.then_inc(mod_made, 1)
            for m in range(2):
                pe.wait_ge(row_copied, m + 1)
                for f in range(m * KD, (m + 1) * KD):
                    last = pe.transpose(k.ps[:, 6, f:f + 1], mod_row[:, f * P:(f + 1) * P], k.ident[0:1, 0:1])
            last.then_inc(mod_turned, 1)

        @block.vector
        def _(dve):
            for unit in range(n_units):
                g, f = divmod(unit, KD)
                dve.wait_ge(turned, unit + 1)
                dve.tensor_copy(k.xT[:, f, g * HALF:(g + 1) * HALF], k.ps[:, 2 + unit % 6, :]).then_inc(copied, 1)
            dve.wait_ge(turned, n_units + 1)
            dve.tensor_copy(k.vec[:, 0:min(N_ROWS, 4 * P)], k.ps[:, 0, 0:min(N_ROWS, 4 * P)]).then_inc(copied, 1)
            dve.tensor_copy(k.vec[:, 4 * P:N_ROWS], k.ps[:, 1, 0:N_ROWS - 4 * P]).then_inc(copied, 1)
            dve.wait_ge(copied, n_units + 2)
            dve.wait_ge(mod_turned, 1)
            dve.tensor_tensor(k.mod1[:, 0:2, :].rearrange("p m f -> p (m f)"), k.ps[:, 6, 0:2 * KD],
                              k.col("b_mod", 0, 2 * KD), ALU.add)


class LateModulation:

    def __init__(self, k, row_at):
        self.k = k
        w1, w2 = (k.ins[name].rearrange("o (k p) n -> p (o k) n", p=P) for name in ("w_mod", "ada_w_2"))
        self.chunks = [(w1[:, :, c:c + HALF], 1, c // P) for c in range(2 * D, 6 * D, HALF)] + \
                      [(w2[:, :, c:c + HALF], 2, c // P) for c in range(0, 6 * D, HALF)]
        self.w = [k.xT[:, 4 * i:4 * i + 4, :].rearrange("p a b -> p (a b)").rearrange("p (k n) -> p k n", k=KD)
                  for i in range(2)]
        self.row = k.ar(row_at, HALF)
        self.rows, self.columns = k.ps[:, 6, :], k.ps[:, 7, :]
        self.kept, self.made, self.copied, self.turned = map(k.sem, ("kept", "made", "copied", "turned"))
        self.loaded = [k.sem(f"loaded{i}") for i in range(2)]

    def sync(self, sp):
        k = self.k
        sp.dma_start(k.x_kept, k.xT[:, :, :]).then_inc(self.kept, 16)
        sp.wait_ge(self.kept, 16)
        for c, (src, _, _) in enumerate(self.chunks):
            if c >= 2:
                sp.wait_ge(self.made, c - 1)
            sp.dma_start(self.w[c % 2], src).then_inc(self.loaded[c % 2], 16)
        sp.wait_ge(self.made, len(self.chunks))
        sp.dma_start(k.xT[:, :, :], k.x_kept).then_inc(k.x_back, 16)

    def turn(self, pe, c):
        _, m, f0 = self.chunks[c]
        first = f0 if m == 1 else 6 * KD + 2 * f0
        pe.wait_ge(self.copied, c + 1)
        for f in range(HALF // P):
            last = pe.transpose(self.columns[:, first + m * f:first + m * (f + 1)], self.row[0:m, f * P:(f + 1) * P],
                                self.k.ident[0:m, 0:m])
        last.then_inc(self.turned, 1)

    def pe(self, pe, c):
        _, m, _ = self.chunks[c]
        vectors = (lambda kt: self.k.cact[:, 0, kt:kt + 1]) if m == 1 else (lambda kt: self.k.cact[:, 1:3, kt])
        pe.wait_ge(self.loaded[c % 2], 16 * (c // 2 + 1))
        if c >= 1:
            pe.wait_ge(self.copied, c)
        for kt in range(KD):
            last = pe.matmul(self.rows[0:m, :], vectors(kt), self.w[c % 2][:, kt, :], start=kt == 0, stop=kt == KD - 1)
        last.then_inc(self.made, 1)
        if c >= 1:
            self.turn(pe, c - 1)

    def act(self, act, c):
        m = self.chunks[c][1]
        act.wait_ge(self.made, c + 1)
        if c >= 1:
            act.wait_ge(self.turned, c)
        act.activation(self.row[0:m, :], self.rows[0:m, :], ACT.Copy).then_inc(self.copied, 1)

    def dve(self, dve):
        k = self.k
        dve.wait_ge(self.turned, len(self.chunks))
        dve.tensor_tensor(k.mod1[:, 2:6, :].rearrange("p m f -> p (m f)"), self.columns[:, 2 * KD:6 * KD],
                          k.col("b_mod", 2 * KD, 4 * KD), ALU.add)
        for c in range(2):
            dve.tensor_tensor(k.mod2[:, :, :, c].rearrange("p m f -> p (m f)"),
                              self.columns[:, 6 * KD:18 * KD].rearrange("p (f c) -> p f c", c=2)[:, :, c],
                              k.col("ada_b_2", 0, 6 * KD), ALU.add)


class Norm:

    def __init__(self, k, gain_index, src, dst, tiles, width, shift, weight, scale, centre=False, tokens=T, tmp_at=0,
                 split=None, bank=0):
        self.bank = bank
        self.k, self.gain_index, self.src, self.dst, self.tiles, self.width = k, gain_index, src, dst, tiles, width
        self.shift, self.weight, self.scale, self.centre, self.split = shift, weight, scale, centre, split
        self.halves = [(a, min(a + HALF, tokens)) for a in range(0, tokens, HALF)]
        self.sq = k.ar(tmp_at, 4, HALF)
        self.rstd = k.ar(tmp_at + 2 * T, T)
        self.mean = k.ar(tmp_at + 3 * T, T)
        (self.sqd, self.used, self.normed, self.meaned, self.centred, self.v_ord, self.logged, self.rooted, self.hi_done,
         self.final, self.ready) = map(k.sem, ("sqd", "used", "normed", "meaned", "centred", "v_ord", "logged", "rooted",
                                               "hi_done", "final", "norm_ready"))

    def steps(self):
        return [(n, a, b, t) for n, (a, b) in enumerate(self.halves) for t in range(self.tiles)]

    def sum_bank(self, n):
        a, b = self.halves[n % 2]
        return self.k.ps[:, self.bank + n, 0:b - a]

    def pe(self, pe):
        k = self.k
        if self.centre:
            for n, a, b, t in self.steps():
                last = pe.matmul(self.sum_bank(2 + n), k.ones[:, :], self.src(t)[:, a:b], start=t == 0,
                                 stop=t == self.tiles - 1)
                if t == self.tiles - 1:
                    last.then_inc(self.meaned, 1)
        for i, (n, a, b, t) in enumerate(self.steps()):
            pe.wait_ge(self.sqd, i + 1)
            pe.matmul(self.sum_bank(n), k.ones[:, :], self.sq[:, i % 4, 0:b - a], start=t == 0,
                      stop=t == self.tiles - 1).then_inc(self.used, 1)

    def act_squares(self, act):
        for i, (n, a, b, t) in enumerate(self.steps()):
            if i >= 4:
                act.wait_ge(self.used, i - 3)
            if self.centre:
                act.wait_ge(self.centred, i + 1)
            act.activation(self.sq[:, i % 4, 0:b - a], (self.dst if self.centre else self.src)(t)[:, a:b], ACT.Square)\
               .then_inc(self.sqd, 1)

    def act_root(self, act, n):
        a, b = self.halves[n]
        act.wait_ge(self.used, (n + 1) * self.tiles)
        act.activation(self.rstd[:, a:b], self.sum_bank(n), ACT.Ln, bias=self.k.eps[:, 0:1], scale=1.0 / self.width)\
           .then_inc(self.logged, 1)
        act.wait_ge(self.logged, n + 1)
        act.activation(self.rstd[:, a:b], self.rstd[:, a:b], ACT.Exp, scale=-0.5).then_inc(self.rooted, 1)

    def act_finish(self, act):
        for n in range(len(self.halves)):
            self.act_root(act, n)
        for i, (n, a, b, t) in enumerate(self.steps()):
            act.wait_ge(self.normed, i + 1)
            dst = self.dst(t)[:, a:b]
            affine = dict(scale=self.weight(t)) if self.shift is None else dict(scale=self.weight(t), bias=self.shift(t))
            if self.split is not None:
                act.activation(self.split(t, 0)[:, a:b], dst, ACT.Identity, **affine).then_inc(self.hi_done, 1)
            act.activation(dst, dst, ACT.Identity, **affine).then_inc(self.final, 1)

    def dve_centre(self, dve):
        self.link = link = chained(dve, self.v_ord)
        if self.scale is not None:
            g = self.k.gain[:, self.gain_index, :]
            link(dve.tensor_scalar(g, self.scale[0], 1.0, None, ALU.add))
            if self.scale[1] is not None:
                link(dve.tensor_tensor(g, g, self.scale[1], ALU.mult))
        if self.centre:
            for n, a, b, t in self.steps():
                if t == 0:
                    dve.wait_ge(self.meaned, n + 1)
                    link(dve.tensor_scalar(self.mean[:, a:b], self.sum_bank(2 + n), 1.0 / self.width, None, ALU.mult))
                dve.tensor_tensor(self.dst(t)[:, a:b], self.src(t)[:, a:b], self.mean[:, a:b], ALU.subtract)\
                   .then_inc(self.centred, 1)

    def dve_finish(self, dve):
        steps = self.steps()
        if self.centre:
            dve.wait_ge(self.centred, len(steps))
        for i in range(len(steps) + 2):
            if i < len(steps):
                n, a, b, t = steps[i]
                if t == 0:
                    dve.wait_ge(self.rooted, n + 1)
                dve.tensor_tensor(self.dst(t)[:, a:b], (self.dst if self.centre else self.src)(t)[:, a:b],
                                  self.rstd[:, a:b], ALU.mult).then_inc(self.normed, 1)
            if self.split is not None and i >= 2:
                n, a, b, t = steps[i - 2]
                dve.wait_ge(self.final, i - 1)
                dve.tensor_tensor(self.split(t, 1)[:, a:b], self.dst(t)[:, a:b], self.split(t, 0)[:, a:b], ALU.subtract)\
                   .then_inc(self.ready, 1)

    def wait_parts(self, pe, half, t):
        pe.wait_ge(self.ready, half * self.tiles + t + 1)


def stage_norm(*args, **kwargs):
    norm = Norm(*args, **kwargs)
    with norm.k.nc.Block() as block:
        @block.tensor
        def _(pe):
            norm.pe(pe)

        @block.scalar
        def _(act):
            norm.act_squares(act)
            norm.act_finish(act)

        @block.vector
        def _(dve):
            norm.dve_centre(dve)
            norm.dve_finish(dve)


def norm1(k):
    return Norm(k, 0, lambda t: k.xT[:, t, :], lambda t: k.ar(A_H, KD, T)[:, t, :], KD, D,
               shift=lambda t: k.mod1[:, 0, t:t + 1], weight=lambda t: k.gain[:, 0, t:t + 1],
               scale=(k.mod1[:, 1, :], k.col("norm1_w", 0, KD)), split=lambda t, s: k.hT[:, s, t, CTX:TT])


A_U = 0
A_Q = A_U + U_TILES * T
A_K = A_Q + A_TILES * T
A_V = A_K + N_KV * T
A_FREE = A_V + NB * KV_DIM
A_H = ARENA - KD * T
A_STREAM = A_FREE


def stream_units(k, pe, stream, units, rhs, made, read, wait_parts=None):
    for n in range(units):
        stream.ready(pe, n)
        if n >= 4:
            pe.wait_ge(read, n - 3)
        if n in stream.whole:
            for half in range(2):
                for kt in range(stream.n_k):
                    last = pe.matmul(k.ps[:, 2 * (n % 4) + half, :], stream.exact[:, n % 2, kt, :], rhs(None, kt, half),
                                     start=kt == 0, stop=kt == stream.n_k - 1)
            last.then_inc(made, 1)
            continue
        if n == 0 and wait_parts is not None:
            for half in range(2):
                last = split_matmuls(pe, [k.ps[:, half, :]], lambda s, kt: stream.part(n, s, kt),
                                     lambda s, kt, i: rhs(s, kt, half), stream.n_k,
                                     before=lambda kt: wait_parts(pe, half, kt))
        else:
            last = split_matmuls(pe, [k.ps[:, 2 * (n % 4) + half, :] for half in range(2)],
                                 lambda s, kt: stream.part(n, s, kt), rhs, stream.n_k)
        last.then_inc(made, 1)


def pair(k, n, pairs=4):
    b = 2 * (n % pairs)
    return k.ps[:, b:b + 2, :].rearrange("p b n -> p (b n)")


def stage_project(k):
    norm = norm1(k)
    nc, ins = k.nc, k.ins
    u, q, kk = k.ar(A_U, U_TILES, T), k.ar(A_Q, A_TILES, T), k.ar(A_K, N_KV, T)
    v = k.ar(A_V, NB, KV_DIM)
    w_src = ins["w_in"].rearrange("o (k p) n -> p (o k) n", p=P)
    made, read, v_made = map(k.sem, ("made", "read", "v_made"))
    k_at = D_SSM + D_ATTN
    outs = [u[:, t, :] for t in range(U_TILES)] + [q[:, t, :] for t in range(A_TILES)] + \
           [kk[:, t, :] for t in range(N_KV)]
    units = len(outs)
    sources = [[w_src[:, :, n * P:(n + 1) * P]] for n in range(U_TILES + A_TILES)]
    sources += [[w_src[:, :, k_at + g * HEAD_DIM:k_at + (g + 1) * HEAD_DIM]] * 2 for g in range(N_KV)]
    sources += [[w_src[:, :, k_at + KV_DIM:D_IN]]]
    stream = WeightStream(k, sources, made, A_STREAM, A_STREAM + 2 * KD * P, whole=range(U_TILES, units))
    h = k.ar(A_H, KD, T)

    def activations(part, kt, half):
        if part is None:
            return h[:, kt, half * HALF:(half + 1) * HALF]
        return k.hT[:, part, kt, CTX + half * HALF:CTX + (half + 1) * HALF]

    with nc.Block() as block:
        @block.sync
        def _(sp):
            for n in range(units + 1):
                stream.load(sp, n)

        @block.tensor
        def _(pe):
            norm.pe(pe)
            stream_units(k, pe, stream, units, activations, made, read, norm.wait_parts)
            stream.ready(pe, units)
            for n in range(2):
                pe.wait_ge(read, units - 4 + (n + 2) % 4 + 1)
                for t in range(4):
                    b = 4 * n + t
                    last = split_matmuls(pe, [k.ps[:, 2 * ((units + n) % 4), t * P:(t + 1) * P]],
                                         lambda s, kt: k.hT[:, s, kt, CTX + b * P:CTX + (b + 1) * P],
                                         lambda s, kt, i: stream.part(units, s, kt), KD)
                last.then_inc(v_made, 1)

        @block.scalar
        def _(act):
            norm.act_squares(act)
            stream.hi(act, 0)
            stream.hi(act, 1)
            norm.act_finish(act)
            for n in range(2, units + 1):
                stream.hi(act, n)

        @block.vector
        def _(dve):
            norm.dve_centre(dve)
            stream.lo(dve, 0)
            stream.lo(dve, 1)
            norm.dve_finish(dve)
            for n in range(units):
                if n >= 1:
                    stream.lo(dve, n + 1)
                dve.wait_ge(made, n + 1)
                dve.tensor_copy(outs[n], pair(k, n)).then_inc(read, 1)
            for n in range(2):
                dve.wait_ge(v_made, n + 1)
                dve.tensor_copy(v[:, 4 * n:4 * n + 4, :].rearrange("p a b -> p (a b)"),
                                k.ps[:, 2 * ((units + n) % 4), :])


A_Y = 0
A_BIAS = A_FREE
A_ATT = A_BIAS + N_Q * 2 * WINDOW


def stage_bias_and_qk_norm(k):
    nc, ins = k.nc, k.ins
    q, kk = k.ar(A_Q, A_TILES, T), k.ar(A_K, N_KV, T)
    tiles = [(q[:, t, :], "q_norm_w") for t in range(A_TILES)] + [(kk[:, t, :], "k_norm_w") for t in range(N_KV)]
    sq, rstd = (k.ar(ARENA - i * len(tiles) * T, len(tiles), T) for i in (2, 1))
    bias = k.ar(A_BIAS, N_Q, 2 * WINDOW)
    table, sel, rows = k.ar(A_ATT, N_Q), k.ar(A_ATT + 8, RB), k.ar(A_ATT + 8 + RB, RB)
    sink_row = k.ar(A_ATT + 8 + 2 * RB, N_Q)
    mirrored, flip = k.ar(A_ATT + 16 + 2 * RB, N_Q, 2 * WINDOW), k.ar(A_ATT + 16 + 2 * RB + N_Q * 2 * WINDOW, P)
    k.rows_dram = nc.dram_tensor("bias_rows", (N_Q, RB), F32)
    rows_dram = k.rows_dram.ap()
    loaded, ones_set, made, copied, stored, flip_set, fetched = map(
        k.sem, ("loaded", "ones_set", "made", "copied", "stored", "flip_set", "fetched"))

    sqd, summed, taken, logged, root, vr, v_ord = map(k.sem, ("sqd", "summed", "taken", "logged", "root", "vr", "v_ord"))

    def sums(n):
        return k.ps[:, 2 + 2 * (n % 3):4 + 2 * (n % 3), :].rearrange("p b n -> p (b n)")

    with nc.Block() as block:
        @block.scalar
        def _(act):
            for n, (x, _) in enumerate(tiles):
                act.activation(sq[:, n, :], x, ACT.Square).then_inc(sqd, 1)
            for n in range(len(tiles)):
                act.wait_ge(summed, n + 1)
                act.activation(sq[:, n, :], sums(n), ACT.Identity, bias=k.eps[:, 0:1], scale=1.0 / HEAD_DIM)\
                   .then_inc(taken, 1)
            for g in range(0, len(tiles), 2):
                for n in range(g, g + 2):
                    act.wait_ge(taken, n + 1)
                    act.activation(rstd[:, n, :], sq[:, n, :], ACT.Ln).then_inc(logged, 1)
                for n in range(g, g + 2):
                    act.wait_ge(logged, n + 1)
                    act.activation(rstd[:, n, :], rstd[:, n, :], ACT.Exp, scale=-0.5).then_inc(root, 1)

        @block.gpsimd
        def _(pool):
            pool.memset(flip, 0.0).then_inc(flip_set, 1)
            pool.wait_ge(flip_set, 1)
            pool.affine_select(out=flip, in_=flip, compare_op=ALU.not_equal, fill=1.0, base=1 - P,
                               pattern=[[1, P]], channel_multiplier=1).then_inc(flip_set, 1)
            for n in range(len(tiles)):
                pool.wait_ge(root, n + 1)
                pool.tensor_tensor(sq[:, n, :], sq[:, n, :], rstd[:, n, :], ALU.mult).then_inc(vr, 1)

        @block.vector
        def _(dve):
            dve.memset(table[N_BUCKETS:N_BUCKETS + 1, :], 1.0).then_inc(ones_set, 1)
            dve.wait_ge(made, 1)
            dve.tensor_copy(rows[0:N_Q, :], k.ps[0:N_Q, 0, 0:RB]).then_inc(copied, 1)
            dve.wait_ge(made, 2)
            dve.tensor_copy(k.sink[:, :], k.ps[:, 1, 0:N_Q])
            link = chained(dve, v_ord)
            for n, (x, w) in enumerate(tiles):
                v, r = sq[:, n, :], rstd[:, n, :]
                dve.wait_ge(root, n + 1)
                dve.scalar_tensor_tensor(x, x, k.col(w), r, ALU.mult, ALU.mult)
                dve.wait_ge(vr, n + 1)
                link(dve.tensor_tensor(v, v, r, ALU.mult))
                link(dve.tensor_scalar(v, v, -0.5, 1.5, ALU.mult, ALU.add))
                link(dve.tensor_tensor(x, x, v, ALU.mult))
            dve.wait_ge(made, 3)
            dve.tensor_copy(bias.rearrange("p a b -> p (a b)"), k.ps[:, 2:6, :].rearrange("p b n -> p (b n)"))

        @block.tensor
        def _(pe):
            pe.wait_ge(loaded, 48)
            pe.wait_ge(ones_set, 1)
            pe.matmul(k.ps[0:N_Q, 0, 0:RB], table[0:N_BUCKETS + 1, :], sel[0:N_BUCKETS + 1, :],
                      start=True, stop=True).then_inc(made, 1)
            pe.matmul(k.ps[:, 1, 0:N_Q], k.ones[0:1, :], sink_row[0:1, :], start=True, stop=True).then_inc(made, 1)
            for n in range(len(tiles)):
                pe.wait_ge(sqd, n + 1)
                if n >= 3:
                    pe.wait_ge(taken, n - 2)
                for half in range(2):
                    last = pe.matmul(sums(n)[:, half * HALF:(half + 1) * HALF], k.halves[:, :],
                                     sq[:, n, half * HALF:(half + 1) * HALF], start=True, stop=True)
                last.then_inc(summed, 1)
            pe.wait_ge(taken, len(tiles))
            pe.wait_ge(flip_set, 2)
            pe.wait_ge(fetched, 16 * N_Q)
            for n in range(4):
                last = pe.matmul(k.ps[:, 2 + n, :], flip, mirrored[:, 2 * n:2 * n + 2, :].rearrange("p a b -> p (a b)"),
                                 start=True, stop=True)
            last.then_inc(made, 1)

        @block.sync
        def _(sp):
            sp.dma_start(table[0:N_BUCKETS, :], ins["rel_bias"]).then_inc(loaded, 16)
            sp.dma_start(sel[0:N_BUCKETS + 1, :], ins["bucket_sel"]).then_inc(loaded, 16)
            sp.dma_start(sink_row[0:1, :], ins["sinks"]).then_inc(loaded, 16)
            sp.wait_ge(copied, 1)
            sp.dma_start(rows_dram, rows[0:N_Q, :]).then_inc(stored, 16)
            sp.wait_ge(stored, 16)
            for h in range(N_Q):
                window = bass.AP(k.rows_dram, h * RB, [[1, P], [1, 2 * WINDOW]])
                sp.dma_start(mirrored[:, h, :], window).then_inc(fetched, 16)


def stage_attention(k):
    nc = k.nc
    q, kk, v = k.ar(A_Q, A_TILES, T), k.ar(A_K, N_KV, T), k.ar(A_V, NB, KV_DIM)
    bias = k.ar(A_BIAS, N_Q, 2 * WINDOW)
    logits = k.ar(A_ATT, 2, 2, 2 * WINDOW)
    probs = k.ar(A_ATT + 1024, 2, 2, 2 * WINDOW)
    probs_t = k.ar(A_ATT + 2048, 2, 4, P)
    small_of = k.ar(A_ATT + 3072, 2, 6, 2)
    yT = k.ar(A_Q, A_TILES, T)
    scale = HEAD_DIM ** -0.5
    units = [(n, t) for n in range(NB) for t in range(A_TILES)]
    scored, softmaxed, turned, turned_read, mixed, mixed_read, maxed, exped, v_ord, sink_exp = map(
        k.sem, ("scored", "softmaxed", "turned", "turned_read", "mixed", "mixed_read", "maxed", "exped",
                "v_ord", "sink_exp"))

    def keys(n):
        return (0, WINDOW) if n == 0 else ((n - 1) * WINDOW, 2 * WINDOW)

    with nc.Block() as block:
        @block.tensor
        def _(pe):
            def scores(i):
                n, t = units[i]
                k0, nk = keys(n)
                if i >= 2:
                    pe.wait_ge(maxed, i - 1)
                for j in range(2):
                    h = 2 * t + j
                    rows = slice(64 * j, 64 * j + 64)
                    last = pe.matmul(k.ps[:, 2 * (i % 2) + j, 0:nk], q[rows, t, n * WINDOW:(n + 1) * WINDOW],
                                     kk[rows, h // (N_Q // N_KV), k0:k0 + nk], start=True, stop=True)
                last.then_inc(scored, 1)

            def turn(i):
                nk = keys(units[i][0])[1]
                pe.wait_ge(softmaxed, i + 1)
                if i >= 2:
                    pe.wait_ge(turned_read, i - 1)
                for j in range(2):
                    for b in range(nk // P):
                        last = pe.transpose(k.ps[:, 4 + i % 2, (2 * j + b) * P:(2 * j + b + 1) * P],
                                            probs[:, i % 2, j, b * P:(b + 1) * P], k.ident[:, :])
                last.then_inc(turned, 1)

            def mix(i):
                n, t = units[i]
                k0, nk = keys(n)
                pe.wait_ge(turned_read, i + 1)
                if i >= 2:
                    pe.wait_ge(mixed_read, i - 1)
                for j in range(2):
                    h = 2 * t + j
                    g = h // (N_Q // N_KV)
                    for b in range(nk // P):
                        last = pe.matmul(k.ps[64 * j:64 * j + 64, 6 + i % 2, 0:P],
                                         v[:, k0 // P + b, g * 64:(g + 1) * 64], probs_t[:, i % 2, 2 * j + b, :],
                                         start=b == 0, stop=b == nk // P - 1)
                last.then_inc(mixed, 1)

            scores(0)
            scores(1)
            for i in range(len(units)):
                if i + 2 < len(units):
                    scores(i + 2)
                turn(i)
                if i >= 1:
                    mix(i - 1)
            mix(len(units) - 1)

        @block.scalar
        def _(act):
            def exponentials(i):
                t, (_, nk), small = units[i][1], keys(units[i][0]), small_of[:, i % 2]
                act.wait_ge(maxed, i + 1)
                for j in range(2):
                    act.activation(probs[:, i % 2, j, 0:nk], logits[:, i % 2, j, 0:nk], ACT.Exp,
                                   bias=small[:, 1, j:j + 1], accum_out=small[:, 2, j:j + 1])
                    last = act.activation(small[:, 3, j:j + 1], k.sink[:, 2 * t + j:2 * t + j + 1], ACT.Exp,
                                          bias=small[:, 1, j:j + 1])
                last.then_inc(exped, 1)

            exponentials(0)
            for i, (n, t) in enumerate(units):
                nk = keys(n)[1]
                if i + 1 < len(units):
                    exponentials(i + 1)
                act.wait_ge(turned, i + 1)
                act.activation(probs_t[:, i % 2, :, :] if nk > P else probs_t[:, i % 2, 0:4:2, :],
                               k.ps[:, 4 + i % 2, :].rearrange("p (a b) -> p a b", b=P) if nk > P else
                               k.ps[:, 4 + i % 2, :].rearrange("p (a b) -> p a b", b=P)[:, 0:4:2, :],
                               ACT.Copy).then_inc(turned_read, 1)

        @block.vector
        def _(dve):
            link = chained(dve, v_ord)

            def output(i):
                n, t = units[i]
                dve.wait_ge(mixed, i + 1)
                for j in range(2):
                    last = dve.tensor_copy(yT[64 * j:64 * j + 64, t, n * WINDOW:(n + 1) * WINDOW],
                                           k.ps[64 * j:64 * j + 64, 6 + i % 2, 0:P])
                last.then_inc(mixed_read, 1)

            def logits_of(i):
                (n, t), small = units[i], small_of[:, i % 2]
                nk = keys(n)[1]
                x = logits[:, i % 2, :, 0:nk]
                b = bias[:, 2 * t:2 * t + 2, 2 * WINDOW - nk:2 * WINDOW]
                dve.wait_ge(scored, i + 1)
                link(dve.scalar_tensor_tensor(x, k.ps[:, 2 * (i % 2):2 * (i % 2) + 2, 0:nk],
                                              scale, b, ALU.mult, ALU.add))
                link(dve.tensor_reduce(small[:, 0, :], x, AX.X, ALU.max))
                link(dve.tensor_tensor(small[:, 0, :], small[:, 0, :], k.sink[:, 2 * t:2 * t + 2], ALU.max))
                dve.tensor_scalar(small[:, 1, :], small[:, 0, :], -1.0, None, ALU.mult).then_inc(maxed, 1)

            logits_of(0)
            for i, (n, t) in enumerate(units):
                nk, small = keys(n)[1], small_of[:, i % 2]
                if i + 1 < len(units):
                    logits_of(i + 1)
                dve.wait_ge(exped, i + 1)
                link(dve.tensor_tensor(small[:, 4, :], small[:, 2, :], small[:, 3, :], ALU.add))
                link(dve.reciprocal(small[:, 5, :], small[:, 4, :]))
                for j in range(2):
                    last = dve.tensor_scalar(probs[:, i % 2, j, 0:nk], probs[:, i % 2, j, 0:nk],
                                             small[:, 5, j:j + 1], None, ALU.mult)
                last.then_inc(softmaxed, 1)
                if i >= 2:
                    output(i - 2)
            output(len(units) - 2)
            output(len(units) - 1)


H_BT, H_CT = 0, 2 * S_TILES * P
H_TAB = 2 * H_CT
H_SMALL = H_TAB + 2 * S_TILES * TAB
A_W = A_K
A_IN = A_W + 6 * T
A_Z = A_IN + 4 * T
A_OUT = A_Z + 4 * T
A_S = A_OUT + 4 * T
LN2_HI, LN2_LO = 0.693359375, -2.12194440e-4
ROUND = 12582912.0
TWO_PI = (6.28125, 1.93500518798828125e-3, 3.01991598195e-7)
POWERS = [TAB << i for i in range(5)]


def views_hT(k):
    flat = k.hT[:, :, :, :].rearrange("p s a b -> p (s a b)").bitcast(F32)

    def at(start, *shape):
        v = flat[:, start:start + int(np.prod(shape))]
        if len(shape) == 1:
            return v
        names = "abcd"[:len(shape)]
        return v.rearrange(f"p ({' '.join(names)}) -> p {' '.join(names)}", **dict(zip(names, shape)))
    return at


def exp_steps(dve, link, out, x, n, r):
    link(dve.tensor_scalar(x, x, -104.0, 89.0, ALU.max, ALU.min))
    link(dve.tensor_scalar(n, x, 1.4426950408889634, ROUND, ALU.mult, ALU.add))
    link(dve.tensor_scalar(n, n, -ROUND, None, ALU.add))
    link(dve.scalar_tensor_tensor(r, n, -LN2_HI, x, ALU.mult, ALU.add))
    link(dve.scalar_tensor_tensor(r, n, -LN2_LO, r, ALU.mult, ALU.add))
    link(dve.tensor_scalar(out, r, 1.0 / math.factorial(8), None, ALU.mult))
    for i in range(7, 0, -1):
        link(dve.scalar_tensor_tensor(out, out, 1.0 / math.factorial(i), r, ALU.add, ALU.mult))
    link(dve.tensor_scalar(n, n, -127.0, 128.0, ALU.max, ALU.min))
    link(dve.tensor_scalar(r.bitcast(I32), n, 127.0, float(1 << 23), ALU.add, ALU.mult))
    link(dve.scalar_tensor_tensor(out, out, 1.0, r, ALU.add, ALU.mult))


def stage_ssm_params(k):
    nc, ins = k.nc, k.ins
    h = views_hT(k)
    bt, ct = h(H_BT, 2, S_TILES, P), h(H_CT, 2, S_TILES, P)
    tab = h(H_TAB, 2, S_TILES, TAB)
    small = h(H_SMALL, 32, S_TILES)
    b_raw, c_raw = k.ar(A_W, 2, S_TILES, SSM_GROUP), k.ar(A_W + 512, 2, U_TILES, SSM_STATE)
    b_wide, c_wide = k.ar(A_IN, 2, S_TILES, P), k.ar(A_Z, 2, S_TILES, P)
    row_mask = k.ar(A_W + 1024, 8)
    b_scaled, tmp = k.ar(A_OUT, 2, S_TILES, SSM_GROUP), k.ar(A_OUT + 512, 4, S_TILES * TAB)
    ldt, sel = k.ar(A_S, S_TILES), k.ar(A_S + 16, P)
    loaded, made, spread, wide, turned, copied, v_ord, b_ord = map(
        k.sem, ("loaded", "made", "spread", "wide", "turned", "copied", "v_ord", "b_ord"))
    s = lambda i: small[:, i, :]
    (LR, DT, TH, N, R, X2, SN, CS, SIN, CM1, COS, MAG, AIM, AM1, DEN, FR, FI, T1, T2) = range(19)
    k.mag = s(MAG)
    k.powers = small[:, 19:19 + 10, :]
    k.tab, k.bt, k.ct = tab, bt, ct
    k.neg_powers = k.ssm_neg[:, :, :]
    lam_re, lam_im = k.col("lam_re", 0, S_TILES), k.col("lam_im", 0, S_TILES)

    with nc.Block() as block:
        @block.sync
        def _(sp):
            sp.dma_start(ldt[0:2, :], ins["log_dt"].rearrange("o (t k) -> (o k) t", k=2),
                         allow_slow_non_contiguous=True).then_inc(loaded, 16)
            for c, name in enumerate(("ssm_b_re", "ssm_b_im")):
                for half in range(2):
                    sp.dma_start(b_raw[64 * half:64 * half + 64, c],
                                 ins[name].rearrange("o (t k) p h -> (o k) p t h", k=2)[half]).then_inc(loaded, 16)
            for c, name in enumerate(("ssm_c_re", "ssm_c_im")):
                sp.dma_start(c_raw[:, c], ins[name].rearrange("o (j g) h p -> (o g h) j p", g=8)).then_inc(loaded, 16)

        @block.gpsimd
        def _(pool):
            pool.memset(sel[:, :], 1.0).then_inc(made, 1)
            pool.memset(row_mask, 1.0).then_inc(made, 1)
            pool.memset(b_wide, 0.0).then_inc(made, 1)
            pool.wait_ge(made, 3)
            pool.affine_select(out=sel[0:2, :], in_=sel[0:2, :], compare_op=ALU.is_ge, fill=0.0, base=0,
                               pattern=[[1, P]], channel_multiplier=-64).then_inc(made, 1)
            pool.wait_ge(made, 4)
            pool.affine_select(out=sel[0:2, :], in_=sel[0:2, :], compare_op=ALU.is_ge, fill=0.0, base=63,
                               pattern=[[-1, P]], channel_multiplier=64).then_inc(made, 1)
            pool.affine_select(out=row_mask, in_=row_mask, compare_op=ALU.is_ge, fill=0.0, base=0,
                               pattern=[[-16, 8]], channel_multiplier=1).then_inc(made, 1)
            pool.wait_ge(made, 6)
            pool.affine_select(out=row_mask, in_=row_mask, compare_op=ALU.is_ge, fill=0.0, base=15,
                               pattern=[[16, 8]], channel_multiplier=-1).then_inc(made, 1)

        @block.tensor
        def _(pe):
            pe.wait_ge(made, 7)
            pe.wait_ge(loaded, 7 * 16)
            pe.matmul(k.ps[:, 0, 0:S_TILES], sel[0:2, :], ldt[0:2, :], start=True, stop=True).then_inc(spread, 1)
            pe.wait_ge(wide, 1)
            for n in range(16):
                c, g = divmod(n % 8, 4)
                if n >= 7:
                    pe.wait_ge(copied, n - 6)
                for i in range(4):
                    last = pe.transpose(k.ps[:, 1 + n % 7, i * P:(i + 1) * P],
                                        (b_wide if n < 8 else c_wide)[:, c, 4 * g + i, :], k.ident[:, :])
                last.then_inc(turned, 1)

        @block.scalar
        def _(act):
            for n in range(16):
                c, g = divmod(n % 8, 4)
                act.wait_ge(turned, n + 1)
                act.activation((bt if n < 8 else ct)[:, c, 4 * g:4 * g + 4, :].rearrange("p a b -> p (a b)"),
                               k.ps[:, 1 + n % 7, :], ACT.Copy).then_inc(copied, 1)

        @block.vector
        def _(dve):
            link = chained(dve, v_ord)
            tt, ts, stt = dve.tensor_tensor, dve.tensor_scalar, dve.scalar_tensor_tensor
            dve.wait_ge(spread, 1)
            link(dve.tensor_copy(s(T1), k.ps[:, 0, 0:S_TILES]))
            exp_steps(dve, link, s(DT), s(T1), s(N), s(R))
            link(ts(s(LR), lam_re, -1e-4, None, ALU.min))
            link(tt(s(T1), s(DT), s(LR), ALU.mult))
            exp_steps(dve, link, s(MAG), s(T1), s(N), s(R))
            link(tt(s(TH), s(DT), lam_im, ALU.mult))
            link(ts(s(N), s(TH), 1.0 / (2 * math.pi), ROUND, ALU.mult, ALU.add))
            link(ts(s(N), s(N), -ROUND, None, ALU.add))
            for part in TWO_PI:
                link(stt(s(TH), s(N), -part, s(TH), ALU.mult, ALU.add))
            link(ts(s(TH), s(TH), 0.5, None, ALU.mult))
            link(tt(s(X2), s(TH), s(TH), ALU.mult))
            for dst, first in ((SN, 13), (CS, 14)):
                sign = lambda i: -1.0 if (i // 2) % 2 else 1.0
                link(ts(s(dst), s(X2), sign(first) / math.factorial(first), None, ALU.mult))
                for i in range(first - 2, 1, -2):
                    link(stt(s(dst), s(dst), sign(i) / math.factorial(i), s(X2), ALU.add, ALU.mult))
            link(stt(s(SN), s(SN), 1.0, s(TH), ALU.add, ALU.mult))
            link(ts(s(CS), s(CS), 1.0, None, ALU.add))
            link(stt(s(SIN), s(SN), 2.0, s(CS), ALU.mult, ALU.mult))
            link(stt(s(CM1), s(SN), -2.0, s(SN), ALU.mult, ALU.mult))
            link(ts(s(COS), s(CM1), 1.0, None, ALU.add))
            link(tt(s(AIM), s(MAG), s(SIN), ALU.mult))
            link(tt(s(AM1), s(MAG), s(COS), ALU.mult))
            link(ts(s(AM1), s(AM1), -1.0, None, ALU.add))
            link(tt(s(DEN), s(LR), s(LR), ALU.mult))
            link(tt(s(T1), lam_im, lam_im, ALU.mult))
            link(tt(s(DEN), s(DEN), s(T1), ALU.add))
            link(dve.reciprocal(s(DEN), s(DEN)))
            link(tt(s(T1), s(AM1), s(LR), ALU.mult))
            link(tt(s(T2), s(AIM), lam_im, ALU.mult))
            link(tt(s(FR), s(T1), s(T2), ALU.add))
            link(tt(s(FR), s(FR), s(DEN), ALU.mult))
            link(tt(s(T1), s(AIM), s(LR), ALU.mult))
            link(tt(s(T2), s(AM1), lam_im, ALU.mult))
            link(tt(s(FI), s(T1), s(T2), ALU.subtract))
            link(tt(s(FI), s(FI), s(DEN), ALU.mult))
            shape = (P, S_TILES, SSM_GROUP)
            fr, fi = (s(i).unsqueeze(2).to_broadcast(shape) for i in (FR, FI))
            t1 = tmp[:, 0, 0:256].rearrange("p (a b) -> p a b", b=SSM_GROUP)
            t2 = tmp[:, 1, 0:256].rearrange("p (a b) -> p a b", b=SSM_GROUP)
            dve.wait_ge(loaded, 7 * 16)
            link(tt(t1, b_raw[:, 0], fr, ALU.mult))
            link(tt(t2, b_raw[:, 1], fi, ALU.mult))
            link(tt(b_scaled[:, 0], t1, t2, ALU.subtract))
            link(tt(t1, b_raw[:, 1], fr, ALU.mult))
            link(tt(t2, b_raw[:, 0], fi, ALU.mult))
            link(tt(b_scaled[:, 1], t1, t2, ALU.add))
            dve.wait_ge(made, 7)
            for c in range(2):
                for g in range(2):
                    rows = slice(64 * g, 64 * g + 64)
                    for i in range(SPU):
                        at = 32 * i + 16 * g
                        link(dve.tensor_copy(b_wide[rows, c, i:S_TILES:SPU, at:at + SSM_GROUP],
                                             b_scaled[rows, c, i:S_TILES:SPU, :]))
            for c in range(2):
                for i in range(SPU):
                    for g in range(2):
                        m = row_mask[:, 2 * i + g:2 * i + g + 1]
                        link(ts(c_wide[:, c, i:S_TILES:SPU, 64 * g:64 * g + 64], c_raw[:, c],
                                m, 1.0 if c == 0 else -1.0, ALU.mult, ALU.mult))
            dve.sem_inc(wide, 1)
            link(dve.memset(tab[:, 0, :, 0:1], 1.0))
            link(dve.memset(tab[:, 1, :, 0:1], 0.0))
            wr, wi = s(COS), s(SIN)
            n = 1
            while n < T:
                if n < TAB:
                    shape = (P, S_TILES, n)
                    br, bi = (w.unsqueeze(2).to_broadcast(shape) for w in (wr, wi))
                    t = [tmp[:, j, 0:S_TILES * n].rearrange("p (a b) -> p a b", b=n) for j in range(4)]
                    link(tt(t[0], tab[:, 0, :, 0:n], br, ALU.mult))
                    link(tt(t[1], tab[:, 1, :, 0:n], bi, ALU.mult))
                    link(tt(t[2], tab[:, 0, :, 0:n], bi, ALU.mult))
                    link(tt(t[3], tab[:, 1, :, 0:n], br, ALU.mult))
                    link(tt(tab[:, 0, :, n:2 * n], t[0], t[1], ALU.subtract))
                    link(tt(tab[:, 1, :, n:2 * n], t[2], t[3], ALU.add))
                else:
                    link(ts(k.neg_powers[:, POWERS.index(n), :], wi, -1.0, None, ALU.mult))
                n *= 2
                if n < T:
                    if n >= TAB:
                        i = POWERS.index(n)
                        nr, ni = k.powers[:, 2 * i, :], k.powers[:, 2 * i + 1, :]
                    else:
                        nr, ni = (s(SN), s(CS)) if (wr is not None and n in (2, 8)) else (s(X2), s(TH))
                    link(tt(s(T1), wr, wr, ALU.mult))
                    link(tt(s(T2), wi, wi, ALU.mult))
                    link(stt(ni, wr, 2.0, wi, ALU.mult, ALU.mult))
                    link(tt(nr, s(T1), s(T2), ALU.subtract))
                    wr, wi = nr, ni


def stage_ssm(k):
    nc = k.nc
    u = k.ar(A_U, U_TILES, T)
    tables, m_in, z, m_out, st = (k.ar(A_W, 3, 2, T), k.ar(A_IN, 4, T), k.ar(A_Z, 2, 2, T), k.ar(A_OUT, 4, T),
                                  k.ar(A_S, 2, 2, T))
    bu_made, in_done, in_added, scanned, out_done, out_added, y_made, y_sum, scaled, level, seeded, half_out = map(
        k.sem, ("bu_made", "in_done", "in_added", "scanned", "out_done", "out_added", "y_made",
                "y_sum", "scaled", "level", "seeded", "half_out"))
    N = S_TILES
    L = len(POWERS)
    bu = [k.ps[:, 2 * c:2 * c + 2, :].rearrange("p b n -> p (b n)") for c in range(2)]

    y_ps = k.ps[:, 4:6, :]
    late = LateModulation(k, A_S + 4 * T)

    def late_chunks(i):
        n = len(late.chunks)
        return range(i * n // N, (i + 1) * n // N)

    with nc.Block() as block:
        @block.sync
        def _(sp):
            late.sync(sp)

        @block.tensor
        def _(pe):
            def inputs(i):
                if i >= 1:
                    pe.wait_ge(in_done, 2 * i)
                for c in range(2):
                    for half in range(2):
                        last = pe.matmul(k.ps[:, 2 * c + half, :], k.bt[:, c, i, :],
                                         u[:, i // SPU, half * HALF:(half + 1) * HALF], start=True, stop=True)
                last.then_inc(bu_made, 1)

            def outputs(i):
                j = i // SPU
                pe.wait_ge(out_added, 2 * i + 2)
                if i % SPU == 0 and j >= 1:
                    pe.wait_ge(y_sum, j)
                for c in range(2):
                    for half in range(2):
                        last = pe.matmul(y_ps[:, half, :], k.ct[:, c, i, :],
                                         st[:, i % 2, c, half * HALF:(half + 1) * HALF],
                                         start=i % SPU == 0 and c == 0, stop=i % SPU == SPU - 1 and c == 1,
                                         skip_group_check=True)
                last.then_inc(y_made, 1)

            inputs(0)
            inputs(1)
            for i in range(N):
                if i + 2 < N:
                    inputs(i + 2)
                outputs(i)
                for c in late_chunks(i):
                    late.pe(pe, c)
            late.turn(pe, len(late.chunks) - 1)

        @block.scalar
        def _(act):
            def gelu(j):
                act.wait_ge(y_sum, j + 1)
                act.activation(u[:, j, :], u[:, j, :], ACT.Gelu_apprx_tanh)

            def table_level(i, l):
                w, n = tables[:, i % 3], POWERS[l]
                if l == 0:
                    if i >= 3:
                        act.wait_ge(out_done, i - 2)
                    act.activation(w[:, :, 0:TAB], k.tab[:, :, i, :], ACT.Copy).then_inc(seeded, 1)
                    act.wait_ge(seeded, i + 1)
                else:
                    act.wait_ge(level, L * i + l)
                act.activation(w[:, :, n:2 * n], w[:, :, 0:n], ACT.Copy,
                               scale=k.powers[:, 2 * l, i:i + 1]).then_inc(scaled, 1)

            for i in range(N):
                for l in range(L):
                    table_level(i, l)
                if i >= 2 * SPU - 1 and i % SPU == SPU - 1:
                    gelu(i // SPU - 1)
                if i >= 3:
                    for c in late_chunks(i - 3):
                        late.act(act, c)
            for i in range(N - 3, N):
                for c in late_chunks(i):
                    late.act(act, c)
            gelu(U_TILES - 1)

        @block.vector
        def _(dve):
            def table_level(i, l):
                if i >= N:
                    return
                w, n = tables[:, i % 3], POWERS[l]
                dve.wait_ge(scaled, L * i + l + 1)
                dve.scalar_tensor_tensor(w[:, 0, n:2 * n], w[:, 1, 0:n], k.neg_powers[:, l, i:i + 1],
                                         w[:, 0, n:2 * n], ALU.mult, ALU.add)
                dve.scalar_tensor_tensor(w[:, 1, n:2 * n], w[:, 0, 0:n], k.powers[:, 2 * l + 1, i:i + 1],
                                         w[:, 1, n:2 * n], ALU.mult, ALU.add).then_inc(level, 1)

            def rotate_in(i):
                if i >= N:
                    return
                w = tables[:, i % 3]
                dve.wait_ge(level, L * i + L)
                dve.wait_ge(bu_made, i + 1)
                if i >= 1:
                    dve.wait_ge(in_added, 2 * i)
                dve.tensor_tensor(m_in[:, 0, :], bu[0], w[:, 0, :], ALU.mult)
                dve.tensor_tensor(m_in[:, 1, :], bu[1], w[:, 1, :], ALU.mult).then_inc(in_done, 1)
                dve.tensor_tensor(m_in[:, 2, :], bu[1], w[:, 0, :], ALU.mult)
                dve.tensor_tensor(m_in[:, 3, :], bu[0], w[:, 1, :], ALU.mult).then_inc(in_done, 1)

            def scan(i, c):
                dve.wait_ge(in_added, 2 * i + c + 1)
                dve.tensor_tensor_scan(z[:, i % 2, c, :], k.mag[:, i:i + 1].to_broadcast((P, T)),
                                       z[:, i % 2, c, :], 0.0, ALU.mult, ALU.add).then_inc(scanned, 1)

            def rotate_out(i):
                w = tables[:, i % 3]
                dve.wait_ge(scanned, 2 * i + 2)
                if i >= 1:
                    dve.wait_ge(out_added, 2 * i)
                zz = z[:, i % 2]
                dve.tensor_tensor(m_out[:, 0, :], zz[:, 0, :], w[:, 0, :], ALU.mult)
                dve.tensor_tensor(m_out[:, 1, :], zz[:, 1, :], w[:, 1, :], ALU.mult).then_inc(half_out, 1)
                table_level(i + 2, 3)
                dve.tensor_tensor(m_out[:, 2, :], zz[:, 1, :], w[:, 0, :], ALU.mult)
                dve.tensor_tensor(m_out[:, 3, :], zz[:, 0, :], w[:, 1, :], ALU.mult).then_inc(out_done, 1)

            def skip(j):
                dve.wait_ge(y_made, SPU * (j + 1))
                dve.scalar_tensor_tensor(u[:, j, :], u[:, j, :], k.col("ssm_d", j),
                                         y_ps.rearrange("p b n -> p (b n)"),
                                         ALU.mult, ALU.add).then_inc(y_sum, 1)

            for i in range(2):
                for l in range(L):
                    table_level(i, l)
                if i == 0:
                    rotate_in(0)
            for i in range(N):
                scan(i, 0)
                table_level(i + 2, 0)
                scan(i, 1)
                table_level(i + 2, 1)
                rotate_in(i + 1)
                table_level(i + 2, 2)
                rotate_out(i)
                table_level(i + 2, 4)
                if i >= SPU and i % SPU == 0:
                    skip(i // SPU - 1)
            skip(U_TILES - 1)
            late.dve(dve)

        @block.gpsimd
        def _(pool):
            def add_in(i):
                if i >= 2:
                    pool.wait_ge(out_done, i - 1)
                pool.wait_ge(in_done, 2 * i + 1)
                pool.tensor_tensor(z[:, i % 2, 0, :], m_in[:, 0, :], m_in[:, 1, :], ALU.add).then_inc(in_added, 1)
                pool.wait_ge(in_done, 2 * i + 2)
                pool.tensor_tensor(z[:, i % 2, 1, :], m_in[:, 2, :], m_in[:, 3, :], ALU.subtract).then_inc(in_added, 1)

            add_in(0)
            for i in range(N):
                if i + 1 < N:
                    add_in(i + 1)
                pool.wait_ge(half_out, i + 1)
                if i >= 2:
                    pool.wait_ge(y_made, i - 1)
                pool.tensor_tensor(st[:, i % 2, 0, :], m_out[:, 0, :], m_out[:, 1, :], ALU.subtract).then_inc(out_added, 1)
                pool.wait_ge(out_done, i + 1)
                pool.tensor_tensor(st[:, i % 2, 1, :], m_out[:, 2, :], m_out[:, 3, :], ALU.add).then_inc(out_added, 1)


A_WG = A_K


def split_tiles(k, act, dve, n, src, part, hi_done, lo_done):
    for t in range(n):
        if act is not None:
            act.activation(part(0, t), src(t), ACT.Copy).then_inc(hi_done, 1)
        else:
            dve.wait_ge(hi_done, t + 1)
            dve.tensor_tensor(part(1, t), src(t), part(0, t), ALU.subtract).then_inc(lo_done, 1)


def stage_glu(k):
    nc, ins = k.nc, k.ins
    z = k.ar(A_U, U_TILES, T)
    zs = lambda s, t: k.hT[:, s, t, 0:T]
    gate = k.ar(A_WG + U_TILES * D_SSM, U_TILES, T)
    made, gated, z_hi, z_lo = map(k.sem, ("made", "gated", "z_hi", "z_lo"))
    src = ins["w_glu"].rearrange("o (k p) n -> p (o k) n", p=P)
    stream = WeightStream(k, [[src[:, :, n * P:(n + 1) * P]] for n in range(U_TILES)], made,
                          A_WG + 2 * U_TILES * D_SSM + U_TILES * T, A_WG, n_k=U_TILES)
    with nc.Block() as block:
        @block.sync
        def _(sp):
            for n in range(U_TILES):
                stream.load(sp, n)

        @block.tensor
        def _(pe):
            pe.wait_ge(z_lo, U_TILES)
            stream_units(k, pe, stream, U_TILES, lambda s, kt, half: zs(s, kt)[:, half * HALF:(half + 1) * HALF],
                         made, None)

        @block.scalar
        def _(act):
            split_tiles(k, act, None, U_TILES, lambda t: z[:, t, :], zs, z_hi, z_lo)
            for n in range(U_TILES):
                stream.hi(act, n)
                if n >= 1:
                    act.wait_ge(made, n)
                    act.activation(gate[:, n - 1, :], pair(k, n - 1), ACT.Sigmoid, bias=k.col("b_glu", n - 1)).then_inc(gated, 1)
            act.wait_ge(made, U_TILES)
            act.activation(gate[:, U_TILES - 1, :], pair(k, U_TILES - 1), ACT.Sigmoid,
                           bias=k.col("b_glu", U_TILES - 1)).then_inc(gated, 1)

        @block.vector
        def _(dve):
            split_tiles(k, None, dve, U_TILES, lambda t: z[:, t, :], zs, z_hi, z_lo)
            for n in range(U_TILES):
                stream.lo(dve, n)
            for n in range(U_TILES):
                dve.wait_ge(gated, n + 1)
                dve.tensor_tensor(z[:, n, :], z[:, n, :], gate[:, n, :], ALU.mult)


def stage_out_projection(k, name, gate, residual_scale=None, src_at=None, norms=(), stream_at=A_K):
    nc, ins = k.nc, k.ins
    parts = lambda s, t: k.hT[:, s, t, 0:T]
    src = ins[name].rearrange("o (k p) n -> p (o k) n", p=P)
    made, read, v_ord, mix_hi, mix_lo = map(k.sem, ("made", "read", "v_ord", "mix_hi", "mix_lo"))
    stream = WeightStream(k, [[src[:, :, n * P:(n + 1) * P]] for n in range(KD)], made, stream_at, stream_at + 2 * KD * P)

    def wait_parts(pe, half, kt):
        if src_at is not None:
            pe.wait_ge(mix_lo, kt + 1)
        else:
            norms[kt // (KD // 2)].wait_parts(pe, half, kt % (KD // 2))

    with nc.Block() as block:
        @block.sync
        def _(sp):
            for n in range(KD):
                stream.load(sp, n)

        @block.tensor
        def _(pe):
            for norm in norms:
                norm.pe(pe)
            stream_units(k, pe, stream, KD, lambda s, kt, half: parts(s, kt)[:, half * HALF:(half + 1) * HALF], made, read,
                         wait_parts)

        @block.scalar
        def _(act):
            if src_at is not None:
                split_tiles(k, act, None, KD, lambda t: k.ar(src_at, KD, T)[:, t, :], parts, mix_hi, mix_lo)
            for norm in norms:
                norm.act_squares(act)
            stream.hi(act, 0)
            stream.hi(act, 1)
            for norm in norms:
                norm.act_finish(act)
            for n in range(2, KD):
                stream.hi(act, n)

        @block.vector
        def _(dve):
            link = chained(dve, v_ord)
            if src_at is not None:
                split_tiles(k, None, dve, KD, lambda t: k.ar(src_at, KD, T)[:, t, :], parts, mix_hi, mix_lo)
            for norm in norms:
                norm.dve_centre(dve)
            stream.lo(dve, 0)
            stream.lo(dve, 1)
            for norm in norms:
                norm.dve_finish(dve)
            if norms:
                dve.wait_ge(k.x_back, 16)
            for n in range(KD):
                x = k.xT[:, n, :]
                if 1 <= n < KD - 1:
                    stream.lo(dve, n + 1)
                if residual_scale is not None:
                    link(dve.tensor_scalar(x, x, residual_scale, None, ALU.mult))
                dve.wait_ge(made, n + 1)
                dve.scalar_tensor_tensor(x, pair(k, n), gate(n), x, ALU.mult, ALU.add).then_inc(read, 1)


def stage_out1(k):
    norms = [Norm(k, None, lambda t, at=at: k.ar(at, U_TILES, T)[:, t, :],
                  lambda t, i=i: k.ar(A_K + (8 + 4 * i) * T, U_TILES, T)[:, t, :], U_TILES, D_SSM, shift=None,
                  weight=lambda t, name=name: k.col(name, t), scale=None, tmp_at=A_K + 4 * i * T,
                  split=lambda t, s, i=i: k.hT[:, s, i * U_TILES + t, 0:T], bank=2 * i)
             for i, (at, name) in enumerate(((A_U, "out_norm_ssm"), (A_Q, "out_norm_attn")))]
    stage_out_projection(k, "w_out", lambda n: k.mod1[:, 2, n:n + 1], norms=norms, stream_at=A_K + 16 * T)


F_G = 0
F_S = F_G + FT * T
F_C = F_S + 4 * KD * P


def gated_parts(k):
    return k.ar(F_G, FT, T).rearrange("p a t -> p (a t)").bitcast(BF16).rearrange("p (s a t) -> p s a t", s=2, t=T)


class DownProjection:

    def __init__(self, k, w_name, gate, residual_scale):
        self.k, self.gate, self.residual_scale = k, gate, residual_scale
        self.g = gated_parts(k)
        h = views_hT(k)
        self.raw = h(0, FT, P)
        self.w = h(FT * P, 2 * FT * P).bitcast(BF16).rearrange("p (b h k n) -> p b h k n", b=2, h=2, n=P)
        self.src = k.ins[w_name].rearrange("o (k p) (m n) -> m p (o k) n", p=P, n=P)
        self.loaded, self.hi, self.lo, self.made, self.read, self.scaled = (
            [k.sem(f"down_{name}{b}") for b in range(2)] for name in ("loaded", "hi", "lo", "made", "read", "scaled"))

    def sync(self, sp):
        with sp.Fori(0, KD // 2) as i:
            for b in range(2):
                sp.wait_ge(self.lo[1 - b], i + 1)
                sp.dma_start(self.raw, self.src[2 * i + b]).then_inc(self.loaded[b], 16)

    def unit(self, pe, i, b, before=None):
        pe.wait_ge(self.lo[b], i + 1 + b)
        pe.wait_ge(self.read[b], i + 1)
        split_matmuls(pe, [self.k.ps[:, 2 * b + half, :] for half in range(2)],
                      lambda part, kt: self.w[:, b, part, kt, :],
                      lambda part, kt, half: self.g[:, part, kt, half * HALF:(half + 1) * HALF], FT, before=before)\
            .then_inc(self.made[b], 1)

    def pe(self, pe, g_ready):
        pe.sem_inc(self.made[0], 1)
        pe.sem_inc(self.made[1], 1)
        self.unit(pe, 0, 0, g_ready)
        self.unit(pe, 0, 1)
        with pe.Fori(1, KD // 2) as i:
            for b in range(2):
                self.unit(pe, i, b)

    def split_hi(self, act, i, b):
        act.wait_ge(self.loaded[b], i * 16 + 16)
        act.wait_ge(self.made[b], i + 1)
        act.activation(self.w[:, b, 0], self.raw, ACT.Copy).then_inc(self.hi[b], 1)

    def act(self, act):
        self.split_hi(act, 0, 1)
        with act.Fori(1, KD // 2) as i:
            for b in range(2):
                self.split_hi(act, i, b)

    def split_lo(self, dve, i, b):
        dve.wait_ge(self.hi[b], i + 1)
        dve.tensor_tensor(self.w[:, b, 1], self.raw, self.w[:, b, 0], ALU.subtract).then_inc(self.lo[b], 1)

    def output(self, dve, i, b):
        x = self.k.xT[:, 2 * i + b, :]
        if self.residual_scale is not None:
            dve.tensor_scalar(x, x, self.residual_scale, None, ALU.mult).then_inc(self.scaled[b], 1)
            dve.wait_ge(self.scaled[b], i + 1)
        dve.wait_ge(self.made[b], i + 2)
        dve.scalar_tensor_tensor(x, pair(self.k, b), self.gate(2 * i + b), x, ALU.mult, ALU.add).then_inc(self.read[b], 1)

    def dve(self, dve):
        self.split_lo(dve, 0, 1)
        with dve.Fori(0, KD // 2 - 1) as i:
            self.output(dve, i, 0)
            self.split_lo(dve, i + 1, 0)
            self.output(dve, i, 1)
            self.split_lo(dve, i + 1, 1)
        self.output(dve, KD // 2 - 1, 0)
        self.output(dve, KD // 2 - 1, 1)


def ffn(k, w_name, n_taps, convolve, finish, norm, down):
    nc, ins = k.nc, k.ins
    g = gated_parts(k)
    raw = k.raw_up
    w = k.ar(F_S, 4 * KD * P).bitcast(BF16).rearrange("p (b s h k n) -> p b s h k n", b=2, s=2, h=2, n=P)
    conv = k.ar(F_C, 4, T)
    src = ins[w_name].rearrange("o (k p) (s j n) -> j s p (o k) n", p=P, s=2, n=P)
    loaded, hi, lo, made, centre, conved, acted, g_hi, done = (
        [k.sem(f"{name}{b}") for b in range(2)] for name in
        ("loaded", "hi", "lo", "made", "centre", "conved", "acted", "g_hi", "done"))
    v_ord = k.sem("v_ord")

    def ps(b, s):
        bank = 4 * b + 2 * s
        return k.ps[:, bank:bank + 2, :].rearrange("p b n -> p (b n)")

    with nc.Block() as block:
        @block.sync
        def _(sp):
            with sp.Fori(0, FT // 2) as i:
                for b in range(2):
                    sp.wait_ge(lo[1 - b], i + 1)
                    for s in range(2):
                        sp.dma_start(raw[:, s], src[2 * i + b, s]).then_inc(loaded[b], 16)
            for b in range(2):
                sp.wait_ge(made[b], FT // 2 + 1)
            down.sync(sp)

        @block.tensor
        def _(pe):
            pe.sem_inc(made[0], 1)
            pe.sem_inc(made[1], 1)
            norm.pe(pe)

            def unit(i, b, waits):
                pe.wait_ge(lo[b], i + 1 + b)
                pe.wait_ge(done[b], i + 1)
                for half in range(2):
                    for s in range(2):
                        last = split_matmuls(pe, [k.ps[:, 4 * b + 2 * s + half, :]],
                                             lambda part, kt: w[:, b, s, part, kt, :],
                                             lambda part, kt, i: k.hT[:, part, kt, half * HALF:(half + 1) * HALF], KD,
                                             before=(lambda kt: norm.wait_parts(pe, half, kt)) if waits and s == 0 else None)
                last.then_inc(made[b], 1)

            unit(0, 0, True)
            unit(0, 1, False)
            with pe.Fori(1, FT // 2) as i:
                for b in range(2):
                    unit(i, b, False)
            pe.wait_ge(done[0], FT // 2 + 1)
            down.pe(pe, lambda kt: pe.wait_ge(done[1], FT // 2 + 1) if kt == FT - 1 else None)

        @block.scalar
        def _(act):
            def split_hi(i, b):
                act.wait_ge(loaded[b], i * 32 + 32)
                act.wait_ge(made[b], i + 1)
                act.activation(w[:, b, :, 0], raw, ACT.Copy).then_inc(hi[b], 1)

            def unit(i, b, between=None):
                c = [conv[:, 2 * b + s, :] for s in range(2)]
                act.wait_ge(made[b], i + 2)
                act.wait_ge(done[b], i + 1)
                convolve(k, "scalar", act, 2 * i + b, c, [ps(b, s) for s in range(2)], centre[b])
                if between is not None:
                    between()
                act.wait_ge(conved[b], i + 1)
                finish(k, "scalar", act, c, None, None, acted[b])
                act.wait_ge(g_hi[b], 2 * i + 1)
                act.activation(g[:, 0, 2 * i + b, :], c[0], ACT.Copy).then_inc(g_hi[b], 1)

            norm.act_squares(act)
            split_hi(0, 0)
            norm.act_finish(act)
            with act.Fori(0, FT // 2 - 1) as i:
                split_hi(i, 1)
                unit(i, 0)
                split_hi(i + 1, 0)
                unit(i, 1)
            split_hi(FT // 2 - 1, 1)
            unit(FT // 2 - 1, 0)
            unit(FT // 2 - 1, 1, lambda: down.split_hi(act, 0, 0))
            down.act(act)

        @block.vector
        def _(dve):
            def split_lo(i, b):
                dve.wait_ge(hi[b], i + 1)
                dve.tensor_tensor(w[:, b, :, 1], raw, w[:, b, :, 0], ALU.subtract).then_inc(lo[b], 1)

            def unit(i, b, between=None):
                dve.wait_ge(centre[b], i + 1)
                c = [conv[:, 2 * b + s, :] for s in range(2)]
                p = [ps(b, s) for s in range(2)]
                convolve(k, "vector", dve, 2 * i + b, c, p, (v_ord, i * (2 * n_taps) + b * n_taps, conved[b]))
                if between is not None:
                    between()
                dve.wait_ge(acted[b], i + 1)
                finish(k, "vector", dve, c, p, c[0], g_hi[b])
                dve.wait_ge(g_hi[b], 2 * i + 2)
                dve.tensor_tensor(g[:, 1, 2 * i + b, :], c[0], g[:, 0, 2 * i + b, :], ALU.subtract).then_inc(done[b], 1)

            dve.sem_inc(done[0], 1)
            dve.sem_inc(done[1], 1)
            dve.sem_inc(lo[1], 1)
            dve.sem_inc(down.lo[1], 1)
            dve.sem_inc(down.read[0], 1)
            dve.sem_inc(down.read[1], 1)
            norm.dve_centre(dve)
            split_lo(0, 0)
            norm.dve_finish(dve)
            with dve.Fori(0, FT // 2 - 1) as i:
                split_lo(i, 1)
                unit(i, 0)
                split_lo(i + 1, 0)
                unit(i, 1)
            split_lo(FT // 2 - 1, 1)
            unit(FT // 2 - 1, 0)
            unit(FT // 2 - 1, 1, lambda: down.split_lo(dve, 0, 0))
            down.dve(dve)


def conv_causal(k, engine, eng, j, c, p, sems):
    w = k.col("conv_w", 0, 6 * FT).rearrange("p (t s j) -> p t s j", t=3, s=2)
    bias = k.col("conv_b", 0, 2 * FT).rearrange("p (s j) -> p s j", s=2)
    if engine == "scalar":
        for s in range(2):
            last = eng.activation(c[s], p[s], ACT.Identity, bias=bias[:, s, bass.ds(j, 1)], scale=w[:, 2, s, bass.ds(j, 1)])
        last.then_inc(sems, 1)
        return
    v_ord, base, conved = sems
    n = 0
    for tap in (1, 0):
        lag = 2 - tap
        for s in range(2):
            if tap == 0:
                eng.wait_ge(v_ord, base + s + 1)
            last = eng.scalar_tensor_tensor(c[s][:, lag:T], p[s][:, 0:T - lag], w[:, tap, s, bass.ds(j, 1)],
                                            c[s][:, lag:T], ALU.mult, ALU.add)
            n += 1
            last.then_inc(v_ord, 1)
    eng.wait_ge(v_ord, base + n)
    eng.sem_inc(conved, 1)


def finish_silu(k, engine, eng, c, p, g, sem):
    if engine == "scalar":
        eng.activation(c[1], c[1], ACT.Silu).then_inc(sem, 1)
    else:
        eng.tensor_tensor(g, c[0], c[1], ALU.mult).then_inc(sem, 1)


def conv_grid(k, engine, eng, j, c, p, sems):
    w = k.col("ffn_conv_w_2", 0, 9 * FT).rearrange("p (t j) -> p t j", t=9)
    if engine == "scalar":
        eng.activation(c[0], p[0], ACT.Identity, bias=k.col("ffn_conv_b_2", 0, FT)[:, bass.ds(j, 1)],
                       scale=w[:, 4, bass.ds(j, 1)]).then_inc(sems, 1)
        return
    v_ord, base, conved = sems
    out = c[0].rearrange("p (r c) -> p r c", c=GRID_W)
    src = p[0].rearrange("p (r c) -> p r c", c=GRID_W)
    n = 0
    for di in (-1, 0, 1):
        for dj in (-1, 0, 1):
            if di == dj == 0:
                continue
            r0, r1 = max(0, -di), GRID_H - max(0, di)
            c0, c1 = max(0, -dj), GRID_W - max(0, dj)
            to = out[:, r0:r1, c0:c1]
            eng.scalar_tensor_tensor(to, src[:, r0 + di:r1 + di, c0 + dj:c1 + dj],
                                     w[:, 3 * (di + 1) + dj + 1, bass.ds(j, 1)], to, ALU.mult, ALU.add).then_inc(v_ord, 1)
            n += 1
            eng.wait_ge(v_ord, base + n)
    eng.sem_inc(conved, 1)


def finish_gelu(k, engine, eng, c, p, g, sem):
    if engine == "scalar":
        eng.activation(c[0], c[0], ACT.Gelu).then_inc(sem, 1)
    else:
        eng.tensor_tensor(g, c[0], p[1], ALU.mult).then_inc(sem, 1)


def stage_ffn1(k):
    norm = Norm(k, 0, lambda t: k.xT[:, t, :], lambda t: k.ar(4 * T, KD, T)[:, t, :], KD, D,
               shift=lambda t: k.mod1[:, 3, t:t + 1], weight=lambda t: k.gain[:, 0, t:t + 1],
               scale=(k.mod1[:, 4, :], k.col("norm2_w", 0, KD)), split=lambda t, s: k.hT[:, s, t, 0:T])
    ffn(k, "w_up", 4, conv_causal, finish_silu, norm,
        DownProjection(k, "w_down", lambda j: k.mod1[:, 5, bass.ds(j, 1)], None))


B_MIX = 0
B_FREE = KD * T
B_MOD = B_FREE + 4 * T
B_SHORT = B_MOD + KD * T + KD * CTX
B_CTX = B_MOD + KD * T
LN_TINY = math.log(TINY)


def stage_context(k):
    nc, ins = k.nc, k.ins
    rows = k.ar(0, CCH, D)
    loaded, turned, ones_set, masked, v_ord, exped, subtracted = map(
        k.sem, ("loaded", "turned", "ones_set", "masked", "v_ord", "exped", "subtracted"))
    p_exp = k.ar(CCH * D, 2 * HG_HEADS)
    p_sum = k.ar(CCH * D + 8, 2 * HG_HEADS)
    ctx = k.ar(B_CTX, KD, CTX)
    with nc.Block() as block:
        @block.sync
        def _(sp):
            sp.dma_start(rows, ins["ctx_2"].rearrange("o (t p) d -> p (o t) d", p=P)).then_inc(loaded, 16)

        @block.tensor
        def _(pe):
            pe.wait_ge(loaded, 16)
            for f in range(KD):
                for t in range(CCH):
                    last = pe.transpose(k.ps[:, f // 2, (f % 2) * CTX + t * P:(f % 2) * CTX + (t + 1) * P],
                                        rows[:, t, f * P:(f + 1) * P], k.ident[:, :])
            last.then_inc(turned, 1)

        @block.scalar
        def _(act):
            act.wait_ge(subtracted, 1)
            act.activation(p_exp, p_exp, ACT.Exp).then_inc(exped, 1)

        @block.vector
        def _(dve):
            link = chained(dve, v_ord)
            lb = k.col("hg_lb_2", 0, 2 * HG_HEADS)
            dve.tensor_tensor(p_exp, lb, lb, ALU.subtract).then_inc(subtracted, 1)
            dve.wait_ge(exped, 1)
            link(dve.reciprocal(p_sum, p_exp))
            link(dve.tensor_tensor(p_exp, p_exp, p_sum, ALU.mult))
            link(dve.tensor_tensor(k.lower[:, :], p_exp, p_exp, ALU.subtract))
            link(dve.tensor_scalar(k.one_less[:, :], k.lower[:, :], -1.0, 1.0, ALU.mult, ALU.add))
            dve.wait_ge(turned, 1)
            for f in range(0, KD, 2):
                dve.tensor_copy(ctx[:, f:f + 2, :],
                                k.ps[:, f // 2, :].rearrange("p (a b) -> p a b", a=2))

        @block.gpsimd
        def _(pool):
            pool.memset(k.masks[:, :, :, :], 0.0).then_inc(ones_set, 1)
            pool.wait_ge(ones_set, 1)
            n = 0
            for l, m in enumerate(LEVELS):
                for d in range(2):
                    quarter = k.masks[:, d, l, :].rearrange("p (b h r) -> p b h r", h=2, r=m)[:, :, 1 - d, :]
                    pool.memset(quarter, 1.0).then_inc(masked, 1)
                    n += 1
                    pool.wait_ge(masked, n)
                    for base, sign in ((-m * d, 1), (m * d + m - 1, -1)):
                        pool.affine_select(out=quarter, in_=quarter, compare_op=ALU.is_ge, fill=0.0, base=base,
                                           pattern=[[-2 * m * sign, P // (2 * m)], [0, m]],
                                           channel_multiplier=sign).then_inc(masked, 1)
                        n += 1
                        pool.wait_ge(masked, n)


def modulate2(k):
    return [Norm(k, c, (lambda t: k.xT[:, t, :]) if c == 0 else (lambda t: k.ar(B_CTX, KD, CTX)[:, t, :]),
                 (lambda t: k.ar(B_MOD, KD, T)[:, t, :]) if c == 0 else (lambda t: k.ar(B_CTX, KD, CTX)[:, t, :]), KD, D,
                 shift=lambda t, c=c: k.mod2[:, 0, t, c:c + 1], weight=lambda t, c=c: k.gain[:, c, t:t + 1],
                 scale=(k.mod2[:, 1, :, c], None), centre=True, tokens=b - a, tmp_at=(B_FREE, B_MIX)[c],
                 split=lambda t, s, a=a, b=b: k.hT[:, s, t, a:b], bank=4 * c)
            for c, (a, b) in enumerate(((CTX, TT), (0, CTX)))]


def gate_weights(k):
    return (k.ar(B_FREE, KD, 2 * SG_WIDTH),
            k.ar(B_MOD + 6 * T, KD * 2 * SG_WIDTH).bitcast(BF16).rearrange("p (s k n) -> p s k n", s=2, k=KD))


def stage_short_conv(k):
    nc, ins = k.nc, k.ins
    norms = modulate2(k)
    gate_raw, gate_parts = gate_weights(k)
    gate_loaded, gate_hi = map(k.sem, ("gate_loaded", "gate_hi"))
    n_t = SC_WIDTH // P
    gate_c, x, y = (k.ar(B_MOD + i * n_t * T, n_t, T) for i in range(3))
    mix = k.ar(B_MIX, KD, T)
    made, copied, used, x_ready, centre, v_ord = map(
        k.sem, ("made", "copied", "used", "x_ready", "centre", "v_ord"))
    parts = [(part, t) for t in range(n_t) for part in (1, 2, 0)]
    src = ins["w_in_2"].rearrange("o (k p) n -> p (o k) n", p=P)
    columns = [O_SC + part * SC_WIDTH + t * P for part, t in parts]
    stream = WeightStream(k, [[src[:, :, c:c + P]] for c in columns], made, B_SHORT, B_SHORT + 2 * KD * P)
    with nc.Block() as block:
        @block.sync
        def _(sp):
            for n in range(len(parts)):
                stream.load(sp, n)
                if n == 2:
                    for norm in norms:
                        sp.wait_ge(norm.ready, len(norm.steps()))
                    sp.dma_start(gate_raw, src[:, :, O_SG:IN2]).then_inc(gate_loaded, 16)

        @block.tensor
        def _(pe):
            for norm in norms:
                norm.pe(pe)
            for norm in norms:
                norm.wait_parts(pe, len(norm.halves) - 1, KD - 1)
            for n in range(len(parts)):
                stream.ready(pe, n)
                if n >= 4:
                    pe.wait_ge(copied, 1)
                    pe.wait_ge(used, n - 4)
                split_matmuls(pe, [k.ps[:, 2 * (n % 4) + half, :] for half in range(2)],
                              lambda s, kt: stream.part(n, s, kt),
                              lambda s, kt, half: k.hT[:, s, kt, CTX + half * HALF:CTX + (half + 1) * HALF], KD)\
                    .then_inc(made, 1)

        @block.scalar
        def _(act):
            for norm in norms:
                norm.act_squares(act)
            stream.hi(act, 0)
            stream.hi(act, 1)
            for norm in norms:
                norm.act_finish(act)
            stream.hi(act, 2)
            for t in range(n_t):
                act.wait_ge(made, 3 * t + 1)
                act.activation(gate_c[:, t, :], pair(k, 3 * t), ACT.Copy).then_inc(copied, 1)
                act.wait_ge(x_ready, t + 1)
                act.activation(y[:, t, :], x[:, t, :], ACT.Copy, scale=k.col("sc_conv_w_2", n_t + t)).then_inc(centre, 1)
                if t == 0:
                    for n in range(3, len(parts)):
                        stream.hi(act, n)
            act.wait_ge(gate_loaded, 16)
            act.activation(gate_parts[:, 0], gate_raw, ACT.Copy).then_inc(gate_hi, 1)

        @block.vector
        def _(dve):
            link = chained(dve, v_ord)
            for norm in norms:
                norm.dve_centre(dve)
            stream.lo(dve, 0)
            stream.lo(dve, 1)
            for norm in norms:
                norm.dve_finish(dve)
            stream.lo(dve, 2)
            for t in range(n_t):
                dve.wait_ge(copied, t + 1)
                dve.wait_ge(made, 3 * t + 2)
                ins_ = dve.tensor_tensor(x[:, t, :], pair(k, 3 * t + 1), gate_c[:, t, :], ALU.mult)
                ins_.then_inc(x_ready, 1)
                dve.wait_ge(centre, t + 1)
                dve.sem_inc(used, 1)
                if t == 0:
                    for n in range(3, len(parts)):
                        stream.lo(dve, n)
                link(dve.scalar_tensor_tensor(y[:, t, 1:T], x[:, t, 0:T - 1], k.col("sc_conv_w_2", t),
                                              y[:, t, 1:T], ALU.mult, ALU.add))
                link(dve.scalar_tensor_tensor(y[:, t, 0:T - 1], x[:, t, 1:T], k.col("sc_conv_w_2", 2 * n_t + t),
                                              y[:, t, 0:T - 1], ALU.mult, ALU.add))
                dve.wait_ge(made, 3 * t + 3)
                dve.tensor_tensor(mix[:, HG_HEADS + t, :], pair(k, 3 * t + 2), y[:, t, :], ALU.mult).then_inc(used, 1)
            dve.wait_ge(gate_hi, 1)
            dve.tensor_tensor(gate_parts[:, 1], gate_raw, gate_parts[:, 0], ALU.subtract)


def stage_spatial_gate(k):
    nc, ins = k.nc, k.ins
    n_t, nb = SG_WIDTH // P, T // P
    at = B_FREE
    _, parts = gate_weights(k)
    at = B_MOD
    u = k.ar(at, n_t, T); at += n_t * T
    v = k.ar(at, nb, SG_WIDTH); at += nb * SG_WIDTH
    sq = k.ar(at, nb, SG_WIDTH); at += nb * SG_WIDTH
    at = B_SHORT
    ws = k.ar(at, SG_HEADS, P); at += SG_HEADS * P
    ws_t = k.ar(at, SG_HEADS, P); at += SG_HEADS * P
    gb = k.ar(at, 2, SG_WIDTH); at += 2 * SG_WIDTH
    rows = k.ar(at, 2 * SG_WIDTH + SG_HEADS * P); at += 2 * SG_WIDTH + SG_HEADS * P
    stats = k.ar(at, 2, nb * SG_HEADS); at += 2 * nb * SG_HEADS
    mix = k.ar(B_MIX, KD, T)
    loaded, made, v_made, prep, copied, normed, mixed, v_ord, rooted, to_root = map(
        k.sem, ("loaded", "made", "v_made", "prep", "copied", "normed", "mixed", "v_ord", "rooted", "to_root"))
    with nc.Block() as block:
        @block.sync
        def _(sp):
            sp.dma_start(ws, ins["sg_w_2"].rearrange("o g t s -> t (o g) s")).then_inc(loaded, 16)
            sp.dma_start(rows[0:1, 0:SG_WIDTH], ins["sg_ln_g_2"]).then_inc(loaded, 16)
            sp.dma_start(rows[0:1, SG_WIDTH:2 * SG_WIDTH], ins["sg_ln_b_2"]).then_inc(loaded, 16)
            sp.dma_start(rows[0:1, 2 * SG_WIDTH:], ins["sg_b_2"].rearrange("o g t -> o (g t)")).then_inc(loaded, 16)

        @block.tensor
        def _(pe):
            for b in range(nb):
                last = split_matmuls(pe, [k.ps[:, b // 2, (b % 2) * SG_WIDTH:(b % 2 + 1) * SG_WIDTH]],
                                     lambda s, kt: k.hT[:, s, kt, CTX + b * P:CTX + (b + 1) * P],
                                     lambda s, kt, i: parts[:, s, kt, SG_WIDTH:2 * SG_WIDTH], KD)
            last.then_inc(v_made, 1)
            pe.wait_ge(loaded, 4 * 16)
            for g in range(SG_HEADS):
                last = pe.transpose(k.ps[:, 4, g * P:(g + 1) * P], ws[:, g, :], k.ident[:, :])
            last.then_inc(prep, 1)
            pe.matmul(k.ps[:, 5, :], k.ones[0:1, :], rows[0:1, 0:2 * SG_WIDTH], start=True, stop=True).then_inc(prep, 1)
            pe.wait_ge(copied, 6)
            for t in range(n_t):
                split_matmuls(pe, [k.ps[:, 2 * t + half, :] for half in range(2)],
                              lambda s, kt: parts[:, s, kt, t * P:(t + 1) * P],
                              lambda s, kt, half: k.hT[:, s, kt, CTX + half * HALF:CTX + (half + 1) * HALF], KD)\
                    .then_inc(made, 1)
            pe.wait_ge(normed, 1)
            for g in range(SG_HEADS):
                t, r = divmod(g, 2)
                out_rows = slice(64 * r, 64 * r + 64)
                for half in range(2):
                    bank = 4 + 2 * t + half
                    b_row = rows[0:1, 2 * SG_WIDTH + g * P:2 * SG_WIDTH + (g + 1) * P]
                    for i in range(4):
                        cols = slice(i * P, (i + 1) * P)
                        pe.matmul(k.ps[out_rows, bank, cols], k.ones[0:1, 0:SG_HD], b_row, start=True, stop=False,
                                  skip_group_check=True)
                        last = pe.matmul(k.ps[out_rows, bank, cols],
                                         v[:, 4 * half + i, g * SG_HD:(g + 1) * SG_HD], ws_t[:, g, :],
                                         start=False, stop=True, skip_group_check=True)
            last.then_inc(mixed, 1)

        @block.scalar
        def _(act):
            act.wait_ge(v_made, 1)
            for b in range(4):
                act.activation(v[:, 2 * b:2 * b + 2, :].rearrange("p a b -> p (a b)"), k.ps[:, b, :], ACT.Copy).then_inc(copied, 1)
            act.wait_ge(prep, 1)
            act.activation(ws_t.rearrange("p a b -> p (a b)"), k.ps[:, 4, :], ACT.Copy).then_inc(copied, 1)
            act.wait_ge(prep, 2)
            act.activation(gb.rearrange("p a b -> p (a b)"), k.ps[:, 5, :], ACT.Copy).then_inc(copied, 1)
            for t in range(n_t):
                act.wait_ge(made, t + 1)
                act.activation(u[:, t, :], pair(k, t), ACT.Copy).then_inc(copied, 1)
            act.wait_ge(to_root, 1)
            act.activation(stats[:, 1, :], stats[:, 1, :], ACT.Sqrt).then_inc(rooted, 1)

        @block.vector
        def _(dve):
            link = chained(dve, v_ord)
            dve.wait_ge(copied, 6)
            vg = v.rearrange("p b (g c) -> p (b g) c", c=SG_HD)
            sg = sq.rearrange("p b (g c) -> p (b g) c", c=SG_HD)
            mean, var = (stats[:, i, :].unsqueeze(2).to_broadcast((P, nb * SG_HEADS, SG_HD)) for i in range(2))
            link(dve.tensor_reduce(stats[:, 0, :], vg, AX.X, ALU.add))
            link(dve.tensor_scalar(stats[:, 0, :], stats[:, 0, :], 1.0 / SG_HD, None, ALU.mult))
            link(dve.tensor_tensor(vg, vg, mean, ALU.subtract))
            link(dve.tensor_tensor(sg, vg, vg, ALU.mult))
            link(dve.tensor_reduce(stats[:, 1, :], sg, AX.X, ALU.add))
            dve.tensor_scalar(stats[:, 1, :], stats[:, 1, :], 1.0 / SG_HD, EPS, ALU.mult, ALU.add).then_inc(to_root, 1)
            dve.wait_ge(rooted, 1)
            link(dve.reciprocal(stats[:, 1, :], stats[:, 1, :]))
            link(dve.tensor_tensor(vg, vg, var, ALU.mult))
            for i, op in enumerate((ALU.mult, ALU.add)):
                link(dve.tensor_tensor(v, v, gb[:, i:i + 1, :].to_broadcast((P, nb, SG_WIDTH)), op))
            dve.sem_inc(normed, 1)
            dve.wait_ge(mixed, 1)
            for t in range(n_t):
                dve.wait_ge(copied, 7 + t)
                dve.tensor_tensor(mix[:, HG_HEADS + 2 + t, :],
                                  k.ps[:, 4 + 2 * t:6 + 2 * t, :].rearrange("p b n -> p (b n)"), u[:, t, :], ALU.mult)


def stage_hgrn(k):
    nc, ins = k.nc, k.ins
    at = [B_FREE]

    def take(*shape):
        v = k.ar(at[0], *shape)
        at[0] += int(np.prod(shape))
        return v

    raw_at = at[0]; take(KD, P)
    split_at = at[0]; take(2, KD, P)
    vals = take(2, NCH, P)
    q = take(2, T)
    keys, b = take(2, TT), take(2, TT)
    x = take(3, T)
    att, qh = take(T), take(T)
    kh = take(NCH, P)
    kh_t = take(NCH, P)
    z, l1 = (t.rearrange("p a b -> p (a b)") for t in (kh, kh_t))
    states = take(T // CHUNK, P)
    state0 = take(P)
    chunk_decay = take(NCH)
    root = take(T)
    mix = k.ar(B_MIX, KD, T)
    NL = len(LEVELS)
    units = [(h, d) for h in range(HG_HEADS) for d in range(2)]
    last_unit = len(units) - 1

    w_src = ins["w_in_2"].rearrange("o (k p) n -> p (o k) n", p=P)
    stream = WeightStream(k, [[w_src[:, :, s * HG_WIDTH + h * P:s * HG_WIDTH + (h + 1) * P]]
                              for h in range(HG_HEADS) for s in (1, 0, 3, 2, 4)], None, raw_at, split_at, n_raw=1)
    Z0, Z1, V0, V1, QUERY, GATE = "z0", "z1", "v0", "v1", "q", "g"
    PIECES = ({Z0: 0, Z1: 0, V0: 1, V1: 1, QUERY: 2}, {Z0: 3, Z1: 3, GATE: 4})
    LAST = (Z1, V1, QUERY, GATE)

    def has(n, piece):
        return n <= last_unit and piece in PIECES[units[n][1]]

    def tile_of(n, piece):
        return 5 * units[n][0] + PIECES[units[n][1]][piece]

    jobs = [(0, "front", piece) for piece in PIECES[0]]
    for n, (h, d) in enumerate(units):
        def front_of_next(*pieces):
            return [(n + 1, "front", piece) for piece in pieces if has(n + 1, piece)]
        jobs += [(n, "kt", 0), (n, "kt", 1)] + front_of_next(Z0) + [(n, "level", NL), (n, "level", 0)] + \
                ([(n, "ss", 0)] if d == 0 and h else []) + [(n, "kv", 0), (n, "kv", 1)] + front_of_next(Z1) + \
                [(n, "level", 1)] + front_of_next(V0, GATE) + [(n, "level", 2), (n, "level", 3)] + front_of_next(V1) + \
                front_of_next(QUERY) + [(n, "level", l) for l in range(4, NL)]
    jobs.append((last_unit + 1, "ss", 0))

    def slot(job):
        i = jobs.index(job)
        return i % 3, i // 3

    def banks(job):
        s, _ = slot(job)
        return k.ps[:, 2 * s:2 * s + 2, :].rearrange("p b n -> p (b n)")

    made = [k.sem(f"made{i}") for i in range(3)]
    read = [k.sem(f"read{i}") for i in range(3)]

    def wait_free(pe, job):
        s, use = slot(job)
        if use >= 1:
            pe.wait_ge(read[s], use)

    def wait_made(eng, job):
        s, use = slot(job)
        eng.wait_ge(made[s], use + 1)

    def x_tokens(t):
        return t[:, CTX:TT]

    def halves_of(v, m):
        r = v.rearrange("p (b h r) -> p b h r", h=2, r=m)
        return r[:, :, 0, :], r[:, :, 1, :]

    def buffer(n, l):
        return (NL * n + l) % 3

    (silu_done, q_scaled, v_done, l_ready, sp_ready, k_raw, lt_ready, k_ready, b_ready, kh_sub, kh_exp, kh_ready,
     kt_done, g_exp, qh_exp, qh_ready, sub_done, exp_done, xk_ready, xq_ready, selected, inter_made, o_made, sq_done,
     root_ready, o_free, a_ord, v_ord, states_ready) = map(k.sem, (
         "silu_done", "q_scaled", "v_done", "l_ready", "sp_ready", "k_raw", "lt_ready", "k_ready", "b_ready", "kh_sub",
         "kh_exp", "kh_ready", "kt_done", "g_exp", "qh_exp", "qh_ready", "sub_done", "exp_done", "xk_ready", "xq_ready",
         "selected", "inter_made", "o_made", "sq_done", "root_ready", "o_free", "a_ord", "v_ord", "states_ready"))
    o_ps = k.ps[:, 6:8, :].rearrange("p b n -> p (b n)")
    mask_u = k.masks[:, :, :, :].bitcast(U32)

    with nc.Block() as block:
        @block.sync
        def _(sp):
            for n in range(5 * HG_HEADS):
                stream.load(sp, n)

        @block.tensor
        def _(pe):
            def front(n, piece, steps=(0, 1)):
                if not has(n, piece):
                    return
                job, tile = (n, "front", piece), tile_of(n, piece)
                if 0 in steps:
                    stream.ready(pe, tile)
                    wait_free(pe, job)
                if piece in (V0, V1):
                    chunks = range(8) if piece == V0 else range(8, NCH)
                    for i, c in enumerate(chunks):
                        if (2 * i) // len(chunks) in steps:
                            last = split_matmuls(pe, [banks(job)[:, i * P:(i + 1) * P]],
                                                 lambda s, kt: k.hT[:, s, kt, c * P:(c + 1) * P],
                                                 lambda s, kt, i: stream.part(tile, s, kt), KD)
                else:
                    first, end = {Z0: (0, T), Z1: (T, TT)}.get(piece, (CTX, TT))
                    spans = [(a, min(a + HALF, end)) for i, a in enumerate(range(first, end, HALF)) if i in steps]
                    last = split_matmuls(pe, [banks(job)[:, a - first:e - first] for a, e in spans],
                                         lambda s, kt: stream.part(tile, s, kt),
                                         lambda s, kt, i: k.hT[:, s, kt, spans[i][0]:spans[i][1]], KD)
                if 1 in steps:
                    last.then_inc(made[slot(job)[0]], 1)

            def chunk_job(job, chunks, fn):
                wait_free(pe, job)
                for i, c in enumerate(chunks):
                    last = fn(banks(job)[:, i * P:(i + 1) * P], c)
                last.then_inc(made[slot(job)[0]], 1)

            def level(n, l):
                pe.wait_ge(xk_ready, NL * n + l + 1)
                pe.wait_ge(xq_ready, NL * n + l + 1)
                v = x[:, buffer(n, l), :]
                chunk_job((n, "level", l), range(T // P), lambda out, c: pe.matmul(
                    out, v[:, c * P:(c + 1) * P], v[:, c * P:(c + 1) * P], start=True, stop=True))

            def sum_of_squares(n, h):
                pe.wait_ge(sq_done, h)
                job = (n, "ss", 0)
                wait_free(pe, job)
                for half in range(2):
                    last = pe.matmul(banks(job)[:, half * HALF:(half + 1) * HALF], k.ones[:, :],
                                     root[:, half * HALF:(half + 1) * HALF], start=True, stop=True)
                last.then_inc(made[slot(job)[0]], 1)

            for piece in PIECES[0]:
                front(0, piece)
            for n, (h, d) in enumerate(units):
                halves = (range(8), range(8, NCH))
                pe.wait_ge(kh_ready, n + 1)
                for i in range(2):
                    chunk_job((n, "kt", i), halves[i], lambda out, c: pe.transpose(out, kh[:, c, :], k.ident[:, :]))
                front(n + 1, Z0, (0,))
                pe.wait_ge(k_ready, n + 1)
                pe.wait_ge(q_scaled, h + 1)
                chunk_job((n, "level", NL), range(T // P), lambda out, c: pe.matmul(
                    out, keys[:, n % 2, CTX + c * P:CTX + (c + 1) * P], q[:, h % 2, c * P:(c + 1) * P],
                    start=True, stop=True))
                level(n, 0)
                front(n + 1, Z0, (1,))
                if d == 0 and h:
                    sum_of_squares(n, h)
                pe.wait_ge(kt_done, 2 * n + 2)
                pe.wait_ge(v_done, 2 * h + 2)
                for i in range(2):
                    chunk_job((n, "kv", i), halves[i], lambda out, c: pe.matmul(
                        out, kh_t[:, c, :], vals[:, h % 2, c, :], start=True, stop=True))
                front(n + 1, Z1)
                level(n, 1)
                front(n + 1, V0, (0,))
                front(n + 1, GATE, (0,))
                level(n, 2)
                front(n + 1, V0, (1,))
                front(n + 1, GATE, (1,))
                level(n, 3)
                pe.wait_ge(states_ready, n + 1)
                pe.wait_ge(qh_ready, n + 1)
                if d == 0 and h:
                    pe.wait_ge(o_free, h)
                for c in range(T // P):
                    last = pe.matmul(o_ps[:, c * P:(c + 1) * P], states[:, c, :], qh[:, c * P:(c + 1) * P],
                                     start=d == 0 and c % 4 == 0, stop=False, skip_group_check=True)
                last.then_inc(inter_made, 1)
                front(n + 1, V1)
                front(n + 1, QUERY, (0,))
                level(n, 4)
                front(n + 1, QUERY, (1,))
                for l in range(5, NL):
                    level(n, l)
                pe.wait_ge(selected, n + 1)
                for c in range(T // P):
                    last = pe.matmul(o_ps[:, c * P:(c + 1) * P], vals[:, h % 2, CCH + c, :], att[:, c * P:(c + 1) * P],
                                     start=False, stop=d == 1, skip_group_check=True)
                last.then_inc(o_made, 1)
            sum_of_squares(last_unit + 1, HG_HEADS)

        @block.scalar
        def _(act):
            link = chained(act, a_ord)

            def take_out(job, dst, func=ACT.Copy):
                wait_made(act, job)
                act.activation(dst, banks(job)[:, 0:int(np.prod(dst.shape[1:]))], func).then_inc(read[slot(job)[0]], 1)

            def signal(job, done):
                s, use = slot(job)
                act.wait_ge(read[s], use + 1)
                act.sem_inc(done, 1)

            def front(n, piece):
                if not has(n, piece):
                    return
                h = units[n][0]
                job, tile = (n, "front", piece), tile_of(n, piece)
                if piece in (V0, V1):
                    chunks = slice(0, 8) if piece == V0 else slice(8, NCH)
                    take_out(job, vals[:, h % 2, chunks, :].rearrange("p a b -> p (a b)"))
                    signal(job, v_done)
                elif piece in (Z0, Z1):
                    take_out(job, z[:, 0:T] if piece == Z0 else z[:, T:TT])
                else:
                    take_out(job, q[:, h % 2, :] if piece == QUERY else mix[:, h, :], ACT.Silu)
                    signal(job, silu_done)
                if piece in LAST and tile + 2 < 5 * HG_HEADS:
                    stream.hi(act, tile + 2)

            def softplus_parts(n):
                if n > last_unit:
                    return
                job = (n, "front", Z1)
                act.wait_ge(read[slot(job)[0]], slot(job)[1] + 1)
                if n:
                    wait_made(act, (n - 1, "kv", 1))
                link(act.activation(l1, z, ACT.Abs))
                link(act.activation(l1, l1, ACT.Exp, scale=-1.0))
                act.activation(l1, l1, ACT.Ln, bias=1.0).then_inc(l_ready, 1)

            def forget_parts(n):
                if n > last_unit:
                    return
                h, d = units[n]
                kk = keys[:, n % 2, :]
                act.wait_ge(sp_ready, n + 1)
                act.activation(kk, kk, ACT.Exp, scale=-1.0).then_inc(k_raw, 1)
                link(act.activation(z, z, ACT.Exp, scale=-1.0))
                act.activation(z, z, ACT.Ln, bias=1.0, scale=k.lower[:, h + d * HG_HEADS:h + d * HG_HEADS + 1])\
                    .then_inc(lt_ready, 1)

            def level(n, l):
                act.wait_ge(sub_done, NL * n + l + 1)
                v = x[:, buffer(n, l), :]
                act.activation(v, v, ACT.Exp).then_inc(exp_done, 1)

            def decays(n):
                if n > last_unit:
                    return
                d = units[n][1]
                act.wait_ge(kh_sub, n + 1)
                act.activation(z, z, ACT.Exp).then_inc(kh_exp, 1)
                level(n, 0)
                bn = b[:, n % 2, :]
                edge = bn.rearrange("p (c r) -> p c r", r=CHUNK)[:, :, CHUNK - 1 if d == 0 else 0]
                if n:
                    act.wait_ge(states_ready, n)
                act.activation(chunk_decay, edge, ACT.Exp).then_inc(g_exp, 1)
                if n:
                    act.wait_ge(inter_made, n)
                act.activation(qh, x_tokens(bn), ACT.Exp).then_inc(qh_exp, 1)
                level(n, 1)

            def squares(h):
                act.wait_ge(o_made, 2 * h + 2)
                act.activation(root, o_ps, ACT.Square).then_inc(sq_done, 1)

            def inverse_root(n):
                job = (n, "ss", 0)
                wait_made(act, job)
                act.activation(root, banks(job), ACT.Ln, bias=k.eps[:, 0:1], scale=1.0 / HG_DK).then_inc(read[slot(job)[0]], 1)
                act.wait_ge(read[slot(job)[0]], slot(job)[1] + 1)
                act.activation(root, root, ACT.Exp, scale=-0.5).then_inc(root_ready, 1)

            stream.hi(act, 0)
            stream.hi(act, 1)
            for piece in PIECES[0]:
                front(0, piece)
            softplus_parts(0)
            forget_parts(0)
            decays(0)
            for n, (h, d) in enumerate(units):
                take_out((n, "kt", 0), kh_t[:, 0:8, :].rearrange("p a b -> p (a b)"))
                signal((n, "kt", 0), kt_done)
                take_out((n, "kt", 1), kh_t[:, 8:NCH, :].rearrange("p a b -> p (a b)"))
                signal((n, "kt", 1), kt_done)
                if d == 0 and h:
                    squares(h - 1)
                level(n, 2)
                front(n + 1, Z0)
                if d == 0 and h:
                    inverse_root(n)
                level(n, 3)
                front(n + 1, Z1)
                softplus_parts(n + 1)
                level(n, 4)
                front(n + 1, V0)
                front(n + 1, GATE)
                forget_parts(n + 1)
                level(n, 5)
                front(n + 1, V1)
                level(n, 6)
                front(n + 1, QUERY)
                decays(n + 1)
            squares(HG_HEADS - 1)
            inverse_root(last_unit + 1)

        @block.gpsimd
        def _(pool):
            for n, (h, d) in enumerate(units):
                qn = q[:, h % 2, :]
                pool.wait_ge(q_scaled, h + 1)
                for l in range(NL):
                    pool.wait_ge(exp_done, NL * n + l + 1)
                    side = halves_of(x[:, buffer(n, l), :], LEVELS[l])[1 - d]
                    pool.tensor_tensor(side, side, halves_of(qn, LEVELS[l])[1 - d], ALU.mult).then_inc(xq_ready, 1)
                    if l == 0:
                        pool.wait_ge(qh_exp, n + 1)
                        pool.tensor_tensor(qh, qh, qn, ALU.mult).then_inc(qh_ready, 1)

        @block.vector
        def _(dve):
            link = chained(dve, v_ord)

            def weights_lo(n, piece):
                if has(n, piece) and tile_of(n, piece) + 2 < 5 * HG_HEADS:
                    stream.lo(dve, tile_of(n, piece) + 2)

            def scale_q(n):
                if n <= last_unit and units[n][1] == 0:
                    h = units[n][0]
                    dve.wait_ge(silu_done, 2 * h + 1)
                    dve.tensor_scalar(q[:, h % 2, :], q[:, h % 2, :], HG_DK ** -0.5, None, ALU.mult).then_inc(q_scaled, 1)

            def softplus(n):
                if n > last_unit:
                    return
                dve.wait_ge(l_ready, n + 1)
                link(dve.scalar_tensor_tensor(b[:, n % 2, :], z, 0.0, l1, ALU.min, ALU.subtract))
                dve.scalar_tensor_tensor(keys[:, n % 2, :], z, 0.0, l1, ALU.max, ALU.add)
                dve.tensor_scalar(z, z, -44.0, None, ALU.max).then_inc(sp_ready, 1)

            def forget(n):
                if n > last_unit:
                    return
                h, d = units[n]
                bn, kn = b[:, n % 2, :], keys[:, n % 2, :]
                dve.wait_ge(k_raw, n + 1)
                dve.tensor_scalar(kn, kn, k.one_less[:, h + d * HG_HEADS:h + d * HG_HEADS + 1], None, ALU.mult)\
                   .then_inc(k_ready, 1)
                dve.wait_ge(lt_ready, n + 1)
                link(dve.tensor_tensor(bn, bn, z, ALU.add))
                link(dve.tensor_scalar(bn, bn, LN_TINY, 0.0, ALU.max, ALU.min))
                for c in range(NCH):
                    bc = bn[:, c * CHUNK:(c + 1) * CHUNK]
                    bc = bc[:, ::-1] if d == 1 else bc
                    last = dve.tensor_tensor_scan(bc, k.ones[:, 0:CHUNK], bc, 0.0, ALU.mult, ALU.add)
                last.then_inc(b_ready, 1)

            def key_distance(n):
                if n > last_unit:
                    return
                dve.wait_ge(b_ready, n + 1)
                bc = b[:, n % 2, :].rearrange("p (c r) -> p c r", r=CHUNK)
                edge = bc[:, :, CHUNK - 1:CHUNK] if units[n][1] == 0 else bc[:, :, 0:1]
                dve.tensor_tensor(kh, edge.to_broadcast((P, NCH, CHUNK)), bc, ALU.subtract).then_inc(kh_sub, 1)

            def decayed_keys(n):
                if n > last_unit:
                    return
                dve.wait_ge(k_ready, n + 1)
                dve.wait_ge(kh_exp, n + 1)
                dve.tensor_tensor(kh, kh, keys[:, n % 2, :].rearrange("p (c r) -> p c r", r=CHUNK), ALU.mult)\
                   .then_inc(kh_ready, 1)

            def subtract(n, l):
                if n > last_unit:
                    return
                m = LEVELS[l]
                i = NL * n + l - 3
                if i >= 0:
                    wait_made(dve, (i // NL, "level", i % NL))
                left, right = halves_of(x_tokens(b[:, n % 2, :]), m)
                xl, xr = halves_of(x[:, buffer(n, l), :], m)
                if units[n][1] == 0:
                    mid = left[:, :, m - 1:m].to_broadcast((P, T // (2 * m), m))
                    dve.tensor_tensor(xl, mid, left, ALU.subtract)
                    last = dve.tensor_tensor(xr, right, mid, ALU.subtract)
                else:
                    mid = right[:, :, 0:1].to_broadcast((P, T // (2 * m), m))
                    dve.tensor_tensor(xl, left, mid, ALU.subtract)
                    last = dve.tensor_tensor(xr, mid, right, ALU.subtract)
                last.then_inc(sub_done, 1)

            def weigh(n, l):
                d = units[n][1]
                dve.wait_ge(exp_done, NL * n + l + 1)
                side = halves_of(x[:, buffer(n, l), :], LEVELS[l])[d]
                dve.tensor_tensor(side, side, halves_of(x_tokens(keys[:, n % 2, :]), LEVELS[l])[d], ALU.mult)\
                   .then_inc(xk_ready, 1)

            def select(n, l):
                job = (n, "level", l)
                mask = mask_u[:, units[n][1], l, :].unsqueeze(1).to_broadcast((P, T // P, P))
                wait_made(dve, job)
                s_, use = slot((n, "level", NL if l == 0 else l - 1))
                dve.wait_ge(read[s_], use + 1)
                dve.copy_predicated(att.rearrange("p (c r) -> p c r", r=P), mask,
                                    banks(job).rearrange("p (c r) -> p c r", r=P)).then_inc(read[slot(job)[0]], 1)

            def diagonal(n):
                job = (n, "level", NL)
                wait_made(dve, job)
                if n:
                    dve.wait_ge(o_made, n)
                dve.tensor_tensor(att.rearrange("p (c r) -> p c r", r=P), banks(job).rearrange("p (c r) -> p c r", r=P),
                                  k.ident[:, :].unsqueeze(1).to_broadcast((P, T // P, P)), ALU.mult)\
                   .then_inc(read[slot(job)[0]], 1)

            def chain_states(n):
                d = units[n][1]
                dve.wait_ge(g_exp, n + 1)
                for i in range(2):
                    wait_made(dve, (n, "kv", i))
                kv = lambda c: banks((n, "kv", c // 8))[:, (c % 8) * P:(c % 8 + 1) * P]
                order = list(range(NCH)) if d == 0 else list(range(CCH - 1, -1, -1)) + list(range(NCH - 1, CCH - 1, -1))
                if n:
                    dve.wait_ge(inter_made, n)
                prev = None
                for i, c in enumerate(order[:-1]):
                    to = order[i + 1]
                    dst = states[:, to - CCH, :] if to >= CCH else state0
                    if prev is None:
                        link(dve.tensor_copy(dst, kv(c)))
                    else:
                        link(dve.scalar_tensor_tensor(dst, prev, chunk_decay[:, c:c + 1], kv(c), ALU.mult, ALU.add))
                    prev = dst
                dve.sem_inc(states_ready, 1)
                for i in range(2):
                    dve.sem_inc(read[slot((n, "kv", i))[0]], 1)

            def finish(h):
                dve.wait_ge(root_ready, h + 1)
                link(dve.tensor_tensor(root, o_ps, root, ALU.mult))
                dve.sem_inc(o_free, 1)
                dve.wait_ge(silu_done, 2 * h + 2)
                dve.scalar_tensor_tensor(mix[:, h, :], root, k.col("hg_norm_g_2"), mix[:, h, :], ALU.mult, ALU.mult)

            stream.lo(dve, 0)
            stream.lo(dve, 1)
            for piece in (Z1, V1, QUERY):
                weights_lo(0, piece)
            scale_q(0)
            softplus(0)
            forget(0)
            key_distance(0)
            subtract(0, 0)
            subtract(0, 1)
            decayed_keys(0)
            for n, (h, d) in enumerate(units):
                weigh(n, 0)
                subtract(n, 2)
                diagonal(n)
                for l in range(1, NL):
                    weigh(n, l)
                    if l + 2 < NL:
                        subtract(n, l + 2)
                    select(n, l - 1)
                    if l == 1:
                        chain_states(n)
                        if d == 0 and h:
                            finish(h - 1)
                        weights_lo(n + 1, Z1)
                    if l == 2:
                        softplus(n + 1)
                    if l == 3:
                        weights_lo(n + 1, GATE)
                    if l == 4:
                        forget(n + 1)
                    if l == 5:
                        weights_lo(n + 1, V1)
                        key_distance(n + 1)
                        subtract(n + 1, 0)
                subtract(n + 1, 1)
                scale_q(n + 1)
                weights_lo(n + 1, QUERY)
                select(n, NL - 1)
                s_, use = slot((n, "level", NL - 1))
                dve.wait_ge(read[s_], use + 1)
                dve.sem_inc(selected, 1)
                decayed_keys(n + 1)
            finish(HG_HEADS - 1)


def stage_out2(k):
    stage_out_projection(k, "w_out_2", lambda n: k.mod2[:, 2, n, 0:1], ALPHA, src_at=B_MIX)


def stage_ln(k, g, b):
    stage_norm(k, 0, lambda t: k.xT[:, t, :], lambda t: k.xT[:, t, :], KD, D,
               shift=lambda t: k.col(b, t), weight=lambda t: k.col(g, t), scale=None, centre=True, tmp_at=0)


def stage_ln1(k):
    stage_ln(k, "ln1_g_2", "ln1_b_2")


def stage_ffn2(k):
    norm = Norm(k, 0, lambda t: k.xT[:, t, :], lambda t: k.ar(4 * T, KD, T)[:, t, :], KD, D,
               shift=lambda t: k.mod2[:, 3, t, 0:1], weight=lambda t: k.gain[:, 0, t:t + 1],
               scale=(k.mod2[:, 4, :, 0], None), centre=True, tmp_at=0, split=lambda t, s: k.hT[:, s, t, 0:T])
    ffn(k, "ffn_up_2", 8, conv_grid, finish_gelu, norm,
        DownProjection(k, "ffn_down_2", lambda j: k.mod2[:, 5, bass.ds(j, 1), 0], ALPHA))


def stage_ln2(k):
    stage_ln(k, "ln2_g_2", "ln2_b_2")


def stage_store(k):
    nc = k.nc
    rows = k.ar(0, T // P, D)
    turned, copied, stored = map(k.sem, ("turned", "copied", "stored"))
    with nc.Block() as block:
        @block.tensor
        def _(pe):
            for n in range(2 * (T // P)):
                t, g = divmod(n, 2)
                if n >= 8:
                    pe.wait_ge(copied, n - 7)
                for i in range(4):
                    f = 4 * g + i
                    last = pe.transpose(k.ps[:, n % 8, i * P:(i + 1) * P], k.xT[:, f, t * P:(t + 1) * P], k.ident[:, :])
                last.then_inc(turned, 1)

        @block.vector
        def _(dve):
            for n in range(2 * (T // P)):
                t, g = divmod(n, 2)
                dve.wait_ge(turned, n + 1)
                dve.tensor_copy(rows[:, t, g * HALF:(g + 1) * HALF], k.ps[:, n % 8, :]).then_inc(copied, 1)

        @block.sync
        def _(sp):
            for t in range(T // P):
                sp.wait_ge(copied, 2 * t + 2)
                sp.dma_start(k.out[0, t * P:(t + 1) * P, :], rows[:, t, :]).then_inc(stored, 16)
            sp.wait_ge(stored, 16 * (T // P))


STAGES = [
    stage_load,
    stage_project, stage_bias_and_qk_norm, stage_attention, stage_ssm_params, stage_ssm, stage_glu,
    stage_out1, stage_ffn1,
    stage_context, stage_short_conv, stage_spatial_gate, stage_hgrn,
    stage_out2, stage_ln1, stage_ffn2, stage_ln2, stage_store,
]


MAX_STAGE_SEMS = 90


def build_program(nc, ins, out):
    with ExitStack() as ctx:
        k = Kernel(nc, ins, out, ctx)
        k.x_kept = nc.dram_tensor("x_kept", (P, KD, T), F32, kind="Internal").ap()
        for stage in STAGES:
            stage(k)
            if len(k.stage_sems) > MAX_STAGE_SEMS:
                k.release_sems()
        k.stage_ctx.close()


def lay_out(inputs):
    arrays = {name: np.ascontiguousarray(a) for name, a in inputs.items()}
    arrays["bucket_sel"] = bucket_selection()
    return arrays


def kernel(**inputs):
    import concourse.bacc as bacc
    from concourse.bass_utils import run_bass_kernel_spmd

    nc = bacc.Bacc("TRN2", target_bir_lowering=False, num_devices=1)
    arrays = lay_out(inputs)
    ins = {name: nc.dram_tensor(f"{name}_dram", a.shape, mybir.dt.from_np(a.dtype), kind="ExternalInput").ap()
           for name, a in arrays.items()}
    out = nc.dram_tensor("out_dram", (1, T, D), F32, kind="ExternalOutput").ap()
    build_program(nc, ins, out)
    r = run_bass_kernel_spmd(nc, [{f"{name}_dram": a for name, a in arrays.items()}], core_ids=[0])
    return r.results[0]["out_dram"]
```
